# Optimizing a Trainium2 kernel written in Bass

```python
import math
import jax
import jax.numpy as jnp
from jax import lax
import numpy as np
import jax, jax.numpy as jnp

D_MODEL = 1024
BATCH = 1
SEQ = 256
DEPTH = 2

N_EVEN = (DEPTH + 1) // 2
N_ODD = DEPTH // 2
EPS = 1e-6
ROPE_THETA = 10000.0
Q_BLOCK = 128

GDN_HEADS = 4
GDN_DK = 128
GDN_DV = 128
GDN_CONV = 4
GDN_CHUNK = 64
GDN_QK = GDN_HEADS * GDN_DK
GDN_V = GDN_HEADS * GDN_DV
GDN_CONV_CH = 2 * GDN_QK + GDN_V
MOBA_HEADS = 4
MOBA_DH = 128
MOBA_BLOCK = 256
MOBA_TOPK = 3
MOBA_W = MOBA_HEADS * MOBA_DH
HY_SIZES = (GDN_CONV_CH, GDN_V, GDN_HEADS, GDN_HEADS, MOBA_W, MOBA_W, MOBA_W)
HY_IN = sum(HY_SIZES)
HY_SPLITS = tuple(int(i) for i in np.cumsum(HY_SIZES)[:-1])
HY_OUT = GDN_V + MOBA_W
MLA_HEADS = 8
MLA_Q_RANK = 512
MLA_KV_RANK = 256
MLA_NOPE = 128
MLA_ROPE = 64
MLA_V = 128
MLA_IN = MLA_Q_RANK + MLA_KV_RANK + MLA_ROPE
PEER_HEADS = 8
PEER_NKEYS = 128
PEER_EXPERTS = PEER_NKEYS * PEER_NKEYS
PEER_DKEY = 256
PEER_TOPK = 16
PEER_TOK_CHUNK = 128


def rmsnorm(x, w):
    xf = x.astype(jnp.float32)
    y = xf * lax.rsqrt(jnp.mean(xf * xf, axis=-1, keepdims=True) + EPS)
    return (y * w.astype(jnp.float32)).astype(x.dtype)

def l2norm(x):
    xf = x.astype(jnp.float32)
    return xf * lax.rsqrt(jnp.sum(xf * xf, axis=-1, keepdims=True) + EPS)

def rope_tables(positions, dim):
    inv_freq = ROPE_THETA ** (-jnp.arange(0, dim, 2, dtype=jnp.float32) / dim)
    ang = positions.astype(jnp.float32)[..., None] * inv_freq
    return jnp.cos(ang), jnp.sin(ang)

def apply_rope(x, cos, sin):
    x1, x2 = jnp.split(x.astype(jnp.float32), 2, axis=-1)
    c = cos[:, :, None, :]
    s = sin[:, :, None, :]
    return jnp.concatenate([x1 * c - x2 * s, x2 * c + x1 * s], axis=-1)

def causal_conv_silu(x, w):
    k_w = w.shape[0]
    s = x.shape[1]
    xp = jnp.pad(x, ((0, 0), (k_w - 1, 0), (0, 0)))
    y = xp[:, 0:s] * w[0]
    for j in range(1, k_w):
        y = y + xp[:, j:j + s] * w[j]
    return jax.nn.silu(y)

def unit_lower_inverse(l_strict):
    n = l_strict.shape[-1]
    eye = jnp.eye(n, dtype=l_strict.dtype)
    neg = -l_strict
    inv = eye + neg
    power = neg
    p = 2
    while p < n:
        power = power @ power
        inv = inv @ (eye + power)
        p *= 2
    return inv

def gated_delta_rule(q, k, v, g, beta):
    bsz, s, nh, dk = q.shape
    dv = v.shape[-1]
    cs = GDN_CHUNK
    nc = s // cs

    def to_chunks(t):
        t = t.reshape((bsz, nc, cs, nh) + t.shape[3:])
        return jnp.moveaxis(t, 3, 1)

    q = to_chunks(q * dk ** -0.5)
    k = to_chunks(k)
    v = to_chunks(v)
    beta = to_chunks(beta)
    g = jnp.cumsum(to_chunks(g), axis=-1)
    causal = jnp.tril(jnp.ones((cs, cs), dtype=bool))
    strict = jnp.tril(jnp.ones((cs, cs), dtype=bool), -1)
    decay = jnp.exp(jnp.where(causal, g[..., :, None] - g[..., None, :], -jnp.inf))
    k_beta = k * beta[..., None]
    l_strict = jnp.where(strict, jnp.einsum('bhncd,bhnmd->bhncm', k_beta, k) * decay, 0.0)
    t_inv = unit_lower_inverse(l_strict)
    u = t_inv @ (v * beta[..., None])
    w = t_inv @ (k_beta * jnp.exp(g)[..., None])
    qk = jnp.einsum('bhncd,bhnmd->bhncm', q, k) * decay
    q_dec = q * jnp.exp(g)[..., None]
    g_last = g[..., -1]
    k_dec = k * jnp.exp(g_last[..., None] - g)[..., None]

    def step(state, inp):
        qd, kd, uc, wc, qkc, gl = inp
        v_new = uc - jnp.einsum('bhck,bhkv->bhcv', wc, state)
        out = jnp.einsum('bhck,bhkv->bhcv', qd, state) + jnp.einsum('bhcm,bhmv->bhcv', qkc, v_new)
        state = state * jnp.exp(gl)[..., None, None] + jnp.einsum('bhck,bhcv->bhkv', kd, v_new)
        return state, out

    xs = tuple(jnp.moveaxis(t, 2, 0) for t in (q_dec, k_dec, u, w, qk, g_last))
    state0 = jnp.zeros((bsz, nh, dk, dv), jnp.float32)
    _, o = lax.scan(step, state0, xs)
    return jnp.transpose(o, (1, 0, 3, 2, 4)).reshape(bsz, s, nh, dv)

def moba_attention(q, k, v):
    bsz, s, nh, d = q.shape
    nb = -(-s // MOBA_BLOCK)
    pad = nb * MOBA_BLOCK - s
    topk = min(MOBA_TOPK, nb)
    qh = jnp.moveaxis(q, 2, 1) * d ** -0.5

    def to_blocks(t):
        t = jnp.pad(jnp.moveaxis(t, 2, 1), ((0, 0), (0, 0), (0, pad), (0, 0)))
        return t.reshape(bsz, nh, nb, MOBA_BLOCK, d)

    k_blk = to_blocks(k)
    v_blk = to_blocks(v)
    k_mean = jnp.mean(k_blk, axis=3)
    b_idx = jnp.arange(bsz)[:, None, None, None]
    h_idx = jnp.arange(nh)[None, :, None, None]
    blk_ids = jnp.arange(nb)

    def one_block(ci):
        start = ci * Q_BLOCK
        own = start // MOBA_BLOCK
        qc = lax.dynamic_slice_in_dim(qh, start, Q_BLOCK, axis=2)
        qpos = start + jnp.arange(Q_BLOCK)
        gate = jnp.einsum('bhqd,bhnd->bhqn', qc, k_mean)
        gate = jnp.where(blk_ids < own, gate, -jnp.inf)
        _, sel = lax.top_k(gate, topk)
        valid = sel < own
        k_sel = k_blk[b_idx, h_idx, sel]
        v_sel = v_blk[b_idx, h_idx, sel]
        s_sel = jnp.einsum('bhqd,bhqtkd->bhqtk', qc, k_sel)
        s_sel = jnp.where(valid[..., None], s_sel, -jnp.inf).reshape(bsz, nh, Q_BLOCK, topk * MOBA_BLOCK)
        k_own = lax.dynamic_index_in_dim(k_blk, own, axis=2, keepdims=False)
        v_own = lax.dynamic_index_in_dim(v_blk, own, axis=2, keepdims=False)
        kpos = own * MOBA_BLOCK + jnp.arange(MOBA_BLOCK)
        s_own = jnp.einsum('bhqd,bhkd->bhqk', qc, k_own)
        s_own = jnp.where(kpos[None, :] <= qpos[:, None], s_own, -jnp.inf)
        p = jax.nn.softmax(jnp.concatenate([s_sel, s_own], axis=-1), axis=-1)
        p_sel = p[..., :topk * MOBA_BLOCK].reshape(bsz, nh, Q_BLOCK, topk, MOBA_BLOCK)
        p_own = p[..., topk * MOBA_BLOCK:]
        return (jnp.einsum('bhqtk,bhqtkd->bhqd', p_sel, v_sel)
                + jnp.einsum('bhqk,bhkd->bhqd', p_own, v_own))

    o = lax.map(one_block, jnp.arange(s // Q_BLOCK))
    return jnp.transpose(o, (1, 0, 3, 2, 4)).reshape(bsz, s, nh, d)

def hybrid_mixer(h, cos, sin, w_in, conv_w, a_log, dt_bias, o_norm, w_out):
    bsz, s, _ = h.shape
    f32 = jnp.float32
    qkv_a, z_a, b_a, a_a, q_b, k_b, v_b = jnp.split(h @ w_in, HY_SPLITS, axis=-1)
    qkv_a = causal_conv_silu(qkv_a, conv_w)
    q_a, k_a, v_a = jnp.split(qkv_a, [GDN_QK, 2 * GDN_QK], axis=-1)
    q_a = l2norm(q_a.reshape(bsz, s, GDN_HEADS, GDN_DK))
    k_a = l2norm(k_a.reshape(bsz, s, GDN_HEADS, GDN_DK))
    v_a = v_a.reshape(bsz, s, GDN_HEADS, GDN_DV).astype(f32)
    beta = jax.nn.sigmoid(b_a.astype(f32))
    g = -jnp.exp(a_log.astype(f32)) * jax.nn.softplus(a_a.astype(f32) + dt_bias.astype(f32))
    o_a = gated_delta_rule(q_a, k_a, v_a, g, beta)
    o_a = rmsnorm(o_a, o_norm) * jax.nn.silu(z_a.reshape(bsz, s, GDN_HEADS, GDN_DV).astype(f32))
    q_b = apply_rope(q_b.reshape(bsz, s, MOBA_HEADS, MOBA_DH), cos, sin)
    k_b = apply_rope(k_b.reshape(bsz, s, MOBA_HEADS, MOBA_DH), cos, sin)
    v_b = v_b.reshape(bsz, s, MOBA_HEADS, MOBA_DH).astype(f32)
    o_b = moba_attention(q_b, k_b, v_b)
    o = jnp.concatenate([o_a.reshape(bsz, s, GDN_V), o_b.reshape(bsz, s, MOBA_W)], axis=-1)
    return o.astype(h.dtype) @ w_out

def mla_mixer(h, cos, sin, w_in, q_norm, kv_norm, w_uq, w_ukv, w_out):
    bsz, s, _ = h.shape
    f32 = jnp.float32
    cq, ckv, k_rope = jnp.split(h @ w_in, [MLA_Q_RANK, MLA_Q_RANK + MLA_KV_RANK], axis=-1)
    q = (rmsnorm(cq, q_norm) @ w_uq).reshape(bsz, s, MLA_HEADS, MLA_NOPE + MLA_ROPE)
    kv = (rmsnorm(ckv, kv_norm) @ w_ukv).reshape(bsz, s, MLA_HEADS, MLA_NOPE + MLA_V)
    q_nope, q_rope = jnp.split(q.astype(f32), [MLA_NOPE], axis=-1)
    k_nope, val = jnp.split(kv.astype(f32), [MLA_NOPE], axis=-1)
    q_rope = apply_rope(q_rope, cos, sin)
    k_rope = apply_rope(k_rope[:, :, None, :], cos, sin)[:, :, 0, :]
    scale = (MLA_NOPE + MLA_ROPE) ** -0.5
    qn = jnp.moveaxis(q_nope, 2, 1) * scale
    qr = jnp.moveaxis(q_rope, 2, 1) * scale
    kn = jnp.moveaxis(k_nope, 2, 1)
    vh = jnp.moveaxis(val, 2, 1)
    kpos = jnp.arange(s)

    def one_block(bi):
        start = bi * Q_BLOCK
        qn_b = lax.dynamic_slice_in_dim(qn, start, Q_BLOCK, axis=2)
        qr_b = lax.dynamic_slice_in_dim(qr, start, Q_BLOCK, axis=2)
        scores = (jnp.einsum('bhqd,bhkd->bhqk', qn_b, kn)
                  + jnp.einsum('bhqr,bkr->bhqk', qr_b, k_rope))
        qpos = start + jnp.arange(Q_BLOCK)
        scores = jnp.where(kpos[None, :] <= qpos[:, None], scores, -jnp.inf)
        return jnp.einsum('bhqk,bhkd->bhqd', jax.nn.softmax(scores, axis=-1), vh)

    o = lax.map(one_block, jnp.arange(s // Q_BLOCK))
    o = jnp.transpose(o, (1, 0, 3, 2, 4)).reshape(bsz, s, MLA_HEADS * MLA_V)
    return o.astype(h.dtype) @ w_out

def peer_ffn(h, w_q, sub_keys, u, v):
    bsz, s, d = h.shape
    f32 = jnp.float32
    q = (h @ w_q).astype(f32).reshape(bsz, s, PEER_HEADS, 2, PEER_DKEY // 2)
    scores = jnp.einsum('bshpd,hpnd->bshpn', q, sub_keys.astype(f32))
    s1, i1 = lax.top_k(scores[..., 0, :], PEER_TOPK)
    s2, i2 = lax.top_k(scores[..., 1, :], PEER_TOPK)
    n_cand = PEER_TOPK * PEER_TOPK
    cand = (s1[..., :, None] + s2[..., None, :]).reshape(bsz, s, PEER_HEADS, n_cand)
    cand_idx = (i1[..., :, None] * PEER_NKEYS + i2[..., None, :]).reshape(bsz, s, PEER_HEADS, n_cand)
    top, pos = lax.top_k(cand, PEER_TOPK)
    expert = jnp.take_along_axis(cand_idx, pos, axis=-1)
    gates = jax.nn.softmax(top, axis=-1)
    n_tok = bsz * s
    n_sel = PEER_HEADS * PEER_TOPK
    n_chunk = n_tok // PEER_TOK_CHUNK
    h_c = h.reshape(n_chunk, PEER_TOK_CHUNK, d)
    e_c = expert.reshape(n_chunk, PEER_TOK_CHUNK, n_sel)
    g_c = gates.reshape(n_chunk, PEER_TOK_CHUNK, n_sel)

    def one_chunk(args):
        hc, ec, gc = args
        act = jax.nn.gelu(jnp.einsum('td,ted->te', hc, u[ec]).astype(f32), approximate=False)
        return jnp.einsum('te,ted->td', (gc * act).astype(v.dtype), v[ec])

    out = lax.map(one_chunk, (h_c, e_c, g_c))
    return out.reshape(bsz, s, d).astype(h.dtype)

def first_inputs(seed: int = 0) -> dict:
    key = jax.random.key(seed)
    ks = jax.random.split(key, 24)
    f32 = jnp.float32
    D = D_MODEL

    def nrm(k, shape, scale):
        return jax.random.normal(k, shape, f32) * scale

    def gain(k, shape):
        return 1.0 + 0.02 * jax.random.normal(k, shape, f32)

    dt = jnp.exp(jax.random.uniform(ks[9], (N_EVEN, GDN_HEADS), f32, math.log(1e-3), math.log(1e-1)))
    return {
        'x': nrm(ks[0], (BATCH, SEQ, D), 1.0),
        'c': nrm(ks[1], (BATCH, D), 1.0),
        'positions': jnp.broadcast_to(jnp.arange(SEQ, dtype=jnp.int32), (BATCH, SEQ)),
        'mod_w': nrm(ks[2], (DEPTH, D, 6 * D), 0.5 * D ** -0.5),
        'mod_b': nrm(ks[3], (DEPTH, 6 * D), 0.02),
        'norm_mix': gain(ks[4], (DEPTH, D)),
        'norm_ffn': gain(ks[5], (DEPTH, D)),
        'hy_w_in': nrm(ks[6], (N_EVEN, D, HY_IN), D ** -0.5),
        'gdn_conv': nrm(ks[7], (N_EVEN, GDN_CONV, GDN_CONV_CH), GDN_CONV ** -0.5),
        'gdn_a_log': jnp.log(jax.random.uniform(ks[8], (N_EVEN, GDN_HEADS), f32, 1.0, 16.0)),
        'gdn_dt_bias': dt + jnp.log(-jnp.expm1(-dt)),
        'gdn_o_norm': gain(ks[10], (N_EVEN, GDN_DV)),
        'hy_w_out': nrm(ks[11], (N_EVEN, HY_OUT, D), HY_OUT ** -0.5),
        'mla_w_in': nrm(ks[12], (N_ODD, D, MLA_IN), D ** -0.5),
        'mla_q_norm': gain(ks[13], (N_ODD, MLA_Q_RANK)),
        'mla_kv_norm': gain(ks[14], (N_ODD, MLA_KV_RANK)),
        'mla_w_uq': nrm(ks[15], (N_ODD, MLA_Q_RANK, MLA_HEADS * (MLA_NOPE + MLA_ROPE)), MLA_Q_RANK ** -0.5),
        'mla_w_ukv': nrm(ks[16], (N_ODD, MLA_KV_RANK, MLA_HEADS * (MLA_NOPE + MLA_V)), MLA_KV_RANK ** -0.5),
        'mla_w_out': nrm(ks[17], (N_ODD, MLA_HEADS * MLA_V, D), (MLA_HEADS * MLA_V) ** -0.5),
        'peer_w_q': nrm(ks[18], (DEPTH, D, PEER_HEADS * PEER_DKEY), D ** -0.5),
        'peer_sub_keys': nrm(ks[19], (DEPTH, PEER_HEADS, 2, PEER_NKEYS, PEER_DKEY // 2), (PEER_DKEY // 2) ** -0.5),
        'peer_u': nrm(ks[20], (DEPTH, PEER_EXPERTS, D), D ** -0.5),
        'peer_v': nrm(ks[21], (DEPTH, PEER_EXPERTS, D), PEER_HEADS ** -0.5),
        'final_norm': gain(ks[22], (D,)),
    }

def first_block(x, c, positions, mod_w, mod_b, norm_mix, norm_ffn, hy_w_in, gdn_conv, gdn_a_log,
              gdn_dt_bias, gdn_o_norm, hy_w_out, mla_w_in, mla_q_norm, mla_kv_norm, mla_w_uq,
              mla_w_ukv, mla_w_out, peer_w_q, peer_sub_keys, peer_u, peer_v, final_norm):
    cond = jax.nn.silu(c)
    cos_b, sin_b = rope_tables(positions, MOBA_DH)
    cos_c, sin_c = rope_tables(positions, MLA_ROPE)
    for layer in range(DEPTH):
        mod = cond @ mod_w[layer] + mod_b[layer]
        sh1, sc1, g1, sh2, sc2, g2 = jnp.split(mod[:, None, :], 6, axis=-1)
        h = rmsnorm(x, norm_mix[layer]) * (1.0 + sc1) + sh1
        i = layer // 2
        if layer % 2 == 0:
            y = hybrid_mixer(h, cos_b, sin_b, hy_w_in[i], gdn_conv[i], gdn_a_log[i], gdn_dt_bias[i],
                             gdn_o_norm[i], hy_w_out[i])
        else:
            y = mla_mixer(h, cos_c, sin_c, mla_w_in[i], mla_q_norm[i], mla_kv_norm[i], mla_w_uq[i],
                          mla_w_ukv[i], mla_w_out[i])
        x = x + g1 * y
        h = rmsnorm(x, norm_ffn[layer]) * (1.0 + sc2) + sh2
        x = x + g2 * peer_ffn(h, peer_w_q[layer], peer_sub_keys[layer], peer_u[layer], peer_v[layer])
    return rmsnorm(x, final_norm)


GRID_W = 64
CTX_LEN = 256
N_EVEN_2 = (DEPTH + 1) // 2
N_ODD_2 = DEPTH // 2
H_A = 4
DK_A = 128
DV_A = 128
H_B = 4
DK_B = 64
DV_B = 128
CONV_W = 3
CHUNK = 32
MIX_W = H_A * DV_A + H_B * DV_B
N_HEADS_C = 8
N_KV_C = 2
GROUP_C = N_HEADS_C // N_KV_C
HEAD_DIM = 128
AXIS_DIM = HEAD_DIM // 2
D_QKV_C = (N_HEADS_C + 2 * N_KV_C) * HEAD_DIM
D_FF = ((8 * D_MODEL // 3 + 255) // 256) * 256
AB_SPLIT = (H_A * DK_A, H_A * DV_A, H_A * DV_A, H_A * DK_A, H_A * DK_A,
            2 * H_B * DK_B, H_B * DV_B, H_B * DV_B, 4 * H_B)
D_AB_IN = sum(AB_SPLIT)


def rmsnorm_2(x, g, eps=1e-6):
    xf = x.astype(jnp.float32)
    y = xf * lax.rsqrt(jnp.mean(xf * xf, axis=-1, keepdims=True) + eps)
    return (y * g.astype(jnp.float32)).astype(x.dtype)

def modulate(x, g, shift, scale):
    return rmsnorm_2(x, g) * (1 + scale) + shift

def ada_params(cvec, w, b):
    return jnp.split(jax.nn.silu(cvec) @ w + b, 6, axis=-1)

def swiglu(h, w_in, w_out):
    g, u = jnp.split(h @ w_in, 2, axis=-1)
    return (jax.nn.silu(g) * u) @ w_out

def conv_centred(x, w):
    return lax.conv_general_dilated(x, w[:, None, :], window_strides=(1,),
                                    padding=[(CONV_W // 2, CONV_W // 2)],
                                    dimension_numbers=('NWC', 'WIO', 'NWC'),
                                    feature_group_count=x.shape[-1])

def to_chunks(a):
    Bn, T = a.shape[:2]
    return jnp.moveaxis(a.reshape(Bn, T // CHUNK, CHUNK, *a.shape[2:]), 1, 0)

def from_chunks(a):
    nc, Bn, C = a.shape[:3]
    return jnp.moveaxis(a, 0, 1).reshape(Bn, nc * C, *a.shape[3:])

def hgrn2_chunk_scan(q, k, v, logf, state0):
    f32 = jnp.float32
    mask = jnp.tril(jnp.ones((CHUNK, CHUNK), bool))

    def step(S, xs):
        qc, kc, vc, fc = xs
        b = jnp.cumsum(fc, axis=1)
        b_mid = b[:, CHUNK // 2 - 1:CHUNK // 2]
        b_last = b[:, -1:]
        A = jnp.einsum('bthd,bshd->bhts', qc * jnp.exp(b - b_mid), kc * jnp.exp(b_mid - b))
        A = jnp.where(mask, A, 0.0)
        o = (jnp.einsum('bhts,bshe->bthe', A, vc)
             + jnp.einsum('bthd,bhde->bthe', qc * jnp.exp(b), S))
        S_new = (S * jnp.exp(b_last[:, 0])[..., None]
                 + jnp.einsum('bshd,bshe->bhde', kc * jnp.exp(b_last - b), vc))
        return S_new, o

    xs = tuple(to_chunks(a.astype(f32)) for a in (q, k, v, logf))
    S_fin, o = lax.scan(step, state0, xs)
    return from_chunks(o).astype(v.dtype), S_fin

def mlstm_chunk_scan(q, k, v, ig, logf, state0):
    f32 = jnp.float32
    mask = jnp.tril(jnp.ones((CHUNK, CHUNK), bool))

    def step(carry, xs):
        C, n, m = carry
        qc, kc, vc, igc, fc = xs
        bh = jnp.swapaxes(jnp.cumsum(fc, axis=1), 1, 2)
        igh = jnp.swapaxes(igc, 1, 2)
        D = jnp.where(mask, bh[..., :, None] - bh[..., None, :] + igh[..., None, :], -jnp.inf)
        m_inter = bh + m[..., None]
        m_t = jnp.maximum(D.max(-1), m_inter)
        S = jnp.einsum('bthd,bshd->bhts', qc, kc) * jnp.exp(D - m_t[..., None])
        w_inter = jnp.exp(m_inter - m_t)
        num = (jnp.einsum('bhts,bshe->bthe', S, vc)
               + jnp.swapaxes(w_inter, 1, 2)[..., None] * jnp.einsum('bthd,bhde->bthe', qc, C))
        den = S.sum(-1) + w_inter * jnp.einsum('bthd,bhd->bht', qc, n)
        h = num / jnp.swapaxes(jnp.maximum(jnp.abs(den), jnp.exp(-m_t)), 1, 2)[..., None]
        b_last = bh[..., -1]
        g = b_last[..., None] - bh + igh
        m_new = jnp.maximum(b_last + m, g.max(-1))
        wk = jnp.exp(g - m_new[..., None])
        decay = jnp.exp(b_last + m - m_new)
        C_new = decay[..., None, None] * C + jnp.einsum('bhs,bshd,bshe->bhde', wk, kc, vc)
        n_new = decay[..., None] * n + jnp.einsum('bhs,bshd->bhd', wk, kc)
        return (C_new, n_new, m_new), h

    xs = tuple(to_chunks(a.astype(f32)) for a in (q, k, v, ig, logf))
    state_fin, h = lax.scan(step, state0, xs)
    return from_chunks(h).astype(v.dtype), state_fin

def bidirectional_prefix(scan_fn, ctx_dirs, lat_dirs, state0):
    outs_c, outs_l = [], []
    for d, reverse in enumerate((False, True)):
        flip = (lambda a: jnp.flip(a, axis=1)) if reverse else (lambda a: a)
        o_c, st = scan_fn(*[flip(a) for a in ctx_dirs[d]], state0)
        o_l, _ = scan_fn(*[flip(a) for a in lat_dirs[d]], st)
        outs_c.append(flip(o_c))
        outs_l.append(flip(o_l))
    return outs_c[0] + outs_c[1], outs_l[0] + outs_l[1]

def mixer_ab(h_ctx, h_lat, w_in, conv_w, gate_b, lb, out_g, w_out, need_ctx):
    f32 = jnp.float32
    split_idx = [int(s) for s in np.cumsum(AB_SPLIT)[:-1]]

    def prep(h):
        Bn, T = h.shape[:2]
        aq, ai, ag, aff, afb, bqk, bv, bo, bg = jnp.split(h @ w_in, split_idx, axis=-1)
        z = jnp.stack([aff, afb], 0).astype(f32).reshape(2, Bn, T, H_A, DK_A)
        lbh = lb[:, None, None]
        logf_a = jnp.log(lbh + (1 - lbh) * jax.nn.sigmoid(z))
        k_a = (1 - lbh) * jax.nn.sigmoid(-z)
        q_a = aq.reshape(Bn, T, H_A, DK_A)
        v_a = ai.reshape(Bn, T, H_A, DV_A)
        q_b, k_b = jnp.split(jax.nn.silu(conv_centred(bqk, conv_w)), 2, axis=-1)
        q_b = q_b.reshape(Bn, T, H_B, DK_B) * (DK_B ** -0.5)
        k_b = k_b.reshape(Bn, T, H_B, DK_B)
        v_b = bv.reshape(Bn, T, H_B, DV_B)
        gates = bg.astype(f32).reshape(Bn, T, 4, H_B) + gate_b.astype(f32)
        ig_b = gates[:, :, 0::2]
        logf_b = jax.nn.log_sigmoid(gates[:, :, 1::2])
        hgrn_dirs = [(q_a, k_a[d], v_a, logf_a[d]) for d in range(2)]
        mlstm_dirs = [(q_b, k_b, v_b, ig_b[:, :, d], logf_b[:, :, d]) for d in range(2)]
        gate = jnp.concatenate([jax.nn.silu(ag), jax.nn.sigmoid(bo)], axis=-1)
        return hgrn_dirs, mlstm_dirs, gate

    ha_c, hb_c, gate_c = prep(h_ctx)
    ha_l, hb_l, gate_l = prep(h_lat)
    Bn = h_lat.shape[0]
    s0_a = jnp.zeros((Bn, H_A, DK_A, DV_A), f32)
    s0_b = (jnp.zeros((Bn, H_B, DK_B, DV_B), f32), jnp.zeros((Bn, H_B, DK_B), f32),
            jnp.zeros((Bn, H_B), f32))
    oa_c, oa_l = bidirectional_prefix(hgrn2_chunk_scan, ha_c, ha_l, s0_a)
    ob_c, ob_l = bidirectional_prefix(mlstm_chunk_scan, hb_c, hb_l, s0_b)

    def out(oa, ob, gate):
        o = jnp.concatenate([oa, ob], axis=2)
        o = rmsnorm_2(o, out_g.reshape(H_A + H_B, DV_A)).reshape(*o.shape[:2], MIX_W)
        return (o * gate) @ w_out

    y_lat = out(oa_l, ob_l, gate_l)
    y_ctx = out(oa_c, ob_c, gate_c) if need_ctx else None
    return y_ctx, y_lat

def axial_rope_angles(T):
    rows = T // GRID_W
    r, col = jnp.meshgrid(jnp.arange(rows, dtype=jnp.float32),
                          jnp.arange(GRID_W, dtype=jnp.float32), indexing='ij')
    inv = jnp.power(ROPE_THETA, -jnp.arange(0, AXIS_DIM, 2, dtype=jnp.float32) / AXIS_DIM)
    return jnp.stack([r.reshape(-1)[:, None] * inv, col.reshape(-1)[:, None] * inv], axis=1)

def rope2d(x, ang):
    Bn, T, H, _ = x.shape
    xf = x.astype(jnp.float32).reshape(Bn, T, H, 2, AXIS_DIM)
    x1, x2 = xf[..., :AXIS_DIM // 2], xf[..., AXIS_DIM // 2:]
    cos, sin = jnp.cos(ang)[None, :, None], jnp.sin(ang)[None, :, None]
    out = jnp.concatenate([x1 * cos - x2 * sin, x2 * cos + x1 * sin], axis=-1)
    return out.reshape(Bn, T, H, HEAD_DIM).astype(x.dtype)

def attend(q, k, v):
    s = jnp.einsum('bqhgd,bkhd->bhgqk', q, k).astype(jnp.float32)
    p = jax.nn.softmax(s, axis=-1).astype(v.dtype)
    return jnp.einsum('bhgqk,bkhd->bqhgd', p, v)

def blocked_attention(q, k, v):
    Bn, T = q.shape[:2]
    qb = jnp.moveaxis(q.reshape(Bn, T // Q_BLOCK, Q_BLOCK, *q.shape[2:]), 1, 0)
    o = lax.map(lambda qi: attend(qi, k, v), qb)
    return jnp.moveaxis(o, 0, 1).reshape(Bn, T, N_HEADS_C * HEAD_DIM)

def mixer_c(h_ctx, h_lat, w_qkv, qk_g, w_out, ang, need_ctx):
    def prep(h, use_rope):
        Bn, T = h.shape[:2]
        q, k, v = jnp.split(h @ w_qkv, [N_HEADS_C * HEAD_DIM, (N_HEADS_C + N_KV_C) * HEAD_DIM], axis=-1)
        q = rmsnorm_2(q.reshape(Bn, T, N_HEADS_C, HEAD_DIM), qk_g[0])
        k = rmsnorm_2(k.reshape(Bn, T, N_KV_C, HEAD_DIM), qk_g[1])
        v = v.reshape(Bn, T, N_KV_C, HEAD_DIM)
        if use_rope:
            q, k = rope2d(q, ang), rope2d(k, ang)
        q = q.reshape(Bn, T, N_KV_C, GROUP_C, HEAD_DIM) * (HEAD_DIM ** -0.5)
        return q, k, v

    q_c, k_c, v_c = prep(h_ctx, False)
    q_l, k_l, v_l = prep(h_lat, True)
    k_all = jnp.concatenate([k_c, k_l], axis=1)
    v_all = jnp.concatenate([v_c, v_l], axis=1)
    y_lat = blocked_attention(q_l, k_all, v_all) @ w_out
    y_ctx = None
    if need_ctx:
        Bn, Tc = h_ctx.shape[:2]
        y_ctx = attend(q_c, k_c, v_c).reshape(Bn, Tc, N_HEADS_C * HEAD_DIM) @ w_out
    return y_ctx, y_lat

def second_inputs(seed: int = 0) -> dict:
    key = jax.random.key(seed)
    ks = jax.random.split(key, 20)
    f32 = jnp.float32

    def nrm(k, shape, s):
        return jax.random.normal(k, shape, f32) * s

    ig_b = nrm(ks[11], (N_EVEN_2, 2, H_B), 0.01)
    fg_b = jnp.linspace(3.0, 6.0, H_B, dtype=f32) + nrm(ks[12], (N_EVEN_2, 2, H_B), 0.01)
    return {
        "x": nrm(ks[0], (BATCH, SEQ, D_MODEL), 1.0),
        "c": nrm(ks[1], (BATCH, D_MODEL), 1.0),
        "ctx": nrm(ks[2], (BATCH, CTX_LEN, D_MODEL), 1.0),
        "c_ctx": nrm(ks[3], (D_MODEL,), 1.0),
        "ada_w": nrm(ks[4], (DEPTH, D_MODEL, 6 * D_MODEL), 0.5 * D_MODEL ** -0.5),
        "ada_b": nrm(ks[5], (DEPTH, 6 * D_MODEL), 0.02),
        "norm_g": 1.0 + nrm(ks[6], (DEPTH, 4, D_MODEL), 0.02),
        "ffn_w_in": nrm(ks[7], (DEPTH, D_MODEL, 2 * D_FF), D_MODEL ** -0.5),
        "ffn_w_out": nrm(ks[8], (DEPTH, D_FF, D_MODEL), D_FF ** -0.5),
        "ab_w_in": nrm(ks[9], (N_EVEN_2, D_MODEL, D_AB_IN), D_MODEL ** -0.5),
        "ab_conv": nrm(ks[10], (N_EVEN_2, CONV_W, 2 * H_B * DK_B), CONV_W ** -0.5),
        "ab_gate_b": jnp.stack([ig_b, fg_b], axis=2).reshape(N_EVEN_2, 4, H_B),
        "hgrn_lb": nrm(ks[13], (2, DEPTH + 1, H_A * DK_A), 0.1),
        "ab_out_g": 1.0 + nrm(ks[14], (N_EVEN_2, MIX_W), 0.02),
        "ab_w_out": nrm(ks[15], (N_EVEN_2, MIX_W, D_MODEL), MIX_W ** -0.5),
        "attn_w_qkv": nrm(ks[16], (N_ODD_2, D_MODEL, D_QKV_C), D_MODEL ** -0.5),
        "attn_qk_g": 1.0 + nrm(ks[17], (N_ODD_2, 2, HEAD_DIM), 0.02),
        "attn_w_out": nrm(ks[18], (N_ODD_2, N_HEADS_C * HEAD_DIM, D_MODEL), (N_HEADS_C * HEAD_DIM) ** -0.5),
    }

def second_block(x, c, ctx, c_ctx, ada_w, ada_b, norm_g, ffn_w_in, ffn_w_out, ab_w_in, ab_conv,
              ab_gate_b, hgrn_lb, ab_out_g, ab_w_out, attn_w_qkv, attn_qk_g, attn_w_out):
    T = x.shape[1]
    ang = axial_rope_angles(T)
    lb_all = jnp.cumsum(jax.nn.softmax(hgrn_lb.astype(jnp.float32), axis=1), axis=1)
    for l in range(DEPTH):
        need_ctx = l < DEPTH - 1
        sh1, sc1, g1, sh2, sc2, g2 = [a[:, None, :] for a in ada_params(c, ada_w[l], ada_b[l])]
        csh1, csc1, cg1, csh2, csc2, cg2 = ada_params(c_ctx, ada_w[l], ada_b[l])
        h_lat = modulate(x, norm_g[l, 0], sh1, sc1)
        h_ctx = modulate(ctx, norm_g[l, 0], csh1, csc1)
        if l % 2 == 0:
            e = l // 2
            y_ctx, y_lat = mixer_ab(h_ctx, h_lat, ab_w_in[e], ab_conv[e], ab_gate_b[e],
                                    lb_all[:, l].reshape(2, H_A, DK_A), ab_out_g[e], ab_w_out[e],
                                    need_ctx)
        else:
            o = l // 2
            y_ctx, y_lat = mixer_c(h_ctx, h_lat, attn_w_qkv[o], attn_qk_g[o], attn_w_out[o], ang,
                                   need_ctx)
        x = x + g1 * rmsnorm_2(y_lat, norm_g[l, 1])
        x = x + g2 * rmsnorm_2(swiglu(modulate(x, norm_g[l, 2], sh2, sc2), ffn_w_in[l], ffn_w_out[l]),
                             norm_g[l, 3])
        if need_ctx:
            ctx = ctx + cg1 * rmsnorm_2(y_ctx, norm_g[l, 1])
            ctx = ctx + cg2 * rmsnorm_2(swiglu(modulate(ctx, norm_g[l, 2], csh2, csc2), ffn_w_in[l],
                                             ffn_w_out[l]), norm_g[l, 3])
    return x


def setup_inputs(seed=0):
    out = dict(first_inputs(seed))
    for name, value in second_inputs(seed + 1).items():
        if name != "x":
            out[name + "_2"] = value
    return out


def reference(
    x, c, positions, mod_w, mod_b, norm_mix, norm_ffn, hy_w_in, gdn_conv, gdn_a_log,
    gdn_dt_bias, gdn_o_norm, hy_w_out, mla_w_in, mla_q_norm, mla_kv_norm, mla_w_uq, mla_w_ukv,
    mla_w_out, peer_w_q, peer_sub_keys, peer_u, peer_v, final_norm, c_2, ctx_2, c_ctx_2,
    ada_w_2, ada_b_2, norm_g_2, ffn_w_in_2, ffn_w_out_2, ab_w_in_2, ab_conv_2, ab_gate_b_2,
    hgrn_lb_2, ab_out_g_2, ab_w_out_2, attn_w_qkv_2, attn_qk_g_2, attn_w_out_2,
):
    x = first_block(
        x, c, positions, mod_w, mod_b, norm_mix, norm_ffn, hy_w_in, gdn_conv, gdn_a_log,
        gdn_dt_bias, gdn_o_norm, hy_w_out, mla_w_in, mla_q_norm, mla_kv_norm, mla_w_uq,
        mla_w_ukv, mla_w_out, peer_w_q, peer_sub_keys, peer_u, peer_v, final_norm,
    )
    return second_block(
        x, c_2, ctx_2, c_ctx_2, ada_w_2, ada_b_2, norm_g_2, ffn_w_in_2, ffn_w_out_2, ab_w_in_2,
        ab_conv_2, ab_gate_b_2, hgrn_lb_2, ab_out_g_2, ab_w_out_2, attn_w_qkv_2, attn_qk_g_2,
        attn_w_out_2,
    )


_drawn_inputs = setup_inputs


def setup_inputs(seed=0):
    import zlib

    import numpy as np

    out = dict(_drawn_inputs(seed))
    spreads = {}
    factors = {'norm_mix': 6.027,
     'norm_ffn': 4.104,
     'gdn_o_norm': 8.0,
     'mla_q_norm': 8.0,
     'mla_kv_norm': 8.0,
     'norm_g_2': 2.801,
     'hgrn_lb_2': 5.147,
     'ab_out_g_2': 8.0,
     'attn_qk_g_2': 8.0}
    for name, (base, spread) in spreads.items():
        noise = np.random.default_rng([zlib.crc32(name.encode()), seed]).standard_normal(out[name].shape)
        drawn = base * np.exp(spread * noise) if base else spread * noise
        out[name] = jnp.asarray(drawn.astype(out[name].dtype))
    for name, factor in factors.items():
        out[name] = (out[name] * factor).astype(out[name].dtype)
    return out
```

```python
from contextlib import ExitStack

import numpy as np

import concourse.bass as bass
from concourse import mybir

F32 = mybir.dt.float32
U32 = mybir.dt.uint32
I32 = mybir.dt.int32
ALU = mybir.AluOpType
ACT = mybir.ActivationFunctionType
AX_X = mybir.AxisListType.X

P = 128
D = 1024
KT = D // P
T = 256
TC = 256
TA = T + TC
TT = T // P
LAT = slice(TC, TA)
EPS = 1e-6
RING = 8
UNIT = 1024
TPU = UNIT // P
BANKS = 4
HEADS = 4
CHUNK = 64
HCHUNK = 32
KEYS = 128
PH = 8
TOPK = 16
FF = 2816
FT = FF // P
MLA_H = 8
GQ_H, GQ_KV = 8, 2
TWO_PI = 2.0 * np.pi
PI_A = 6.28125
PI_B = float(np.float32(TWO_PI - PI_A) // 2.0 ** -20 * 2.0 ** -20)
PI_C = float(TWO_PI - PI_A - PI_B)
PI_MAX = 3.1415925
ROUND = 1.5 * 2.0 ** 23
NEG = -1e30
LOWEST = -3e38


class Signal:

    def __init__(self, nc, ctx, name):
        self.sem = ctx.enter_context(nc.semaphore(name))
        self.n = 0

    def up(self, by=1):
        self.n += by
        return self.n


class Space:

    def __init__(self, tensor, size):
        self.tensor, self.size, self.at = tensor, size, 0

    def take(self, *shape, dt=None):
        n = int(np.prod(shape))
        assert self.at + n <= self.size, (self.at, n, self.size)
        ap = self.tensor[:, self.at:self.at + n]
        self.at += n
        if dt is not None:
            ap = ap.bitcast(dt)
        if len(shape) == 2:
            ap = ap.rearrange("p (a b) -> p a b", a=shape[0])
        elif len(shape) == 3:
            ap = ap.rearrange("p (a b c) -> p a b c", a=shape[0], b=shape[1])
        return ap


def flat(ap):
    return ap.rearrange("p a b -> p (a b)")


class Core:
    def __init__(self, nc, ctx, dram, order):
        self.nc, self.dram = nc, dram
        sb = lambda name, n: ctx.enter_context(nc.sbuf_tensor(name, [P, n], F32))
        self.ring = sb("ring", RING * UNIT)
        self.arena = Space(sb("arena", 32768), 32768)
        self.small = Space(sb("small", 3900), 3900)
        self.xT = sb("x_sb", KT * TA)[:, :].rearrange("p (k t) -> p k t", k=KT)
        self.hT = sb("h_sb", KT * TA)[:, :].rearrange("p (k t) -> p k t", k=KT)
        self.ps = ctx.enter_context(nc.psum_tensor("ps", [P, 8, 512], F32))
        sig = lambda name: Signal(nc, ctx, name)
        self.arrived = [sig(f"slot{i}_arrived") for i in range(RING)]
        self.unit_used = sig("unit_used")
        self.tile_done = sig("tile_done")
        self.bank_free = sig("bank_free")
        self.pair_free = [sig("even_bank_free"), sig("odd_bank_free")]
        self.loaded = sig("small_loaded")
        self.stored = sig("stored")
        self.dve_done, self.act_done, self.pool_done = sig("dve_done"), sig("act_done"), sig("pool_done")
        self.a, self.b, self.c, self.d = sig("hand_a"), sig("hand_b"), sig("hand_c"), sig("hand_d")
        self.order = [(name, i) for name in order for i in range(dram[name].shape[0])]
        self.n_loaded = self.n_used = 0

    def block(self):
        return self.nc.Block(no_gpsimd_drain=True)

    def slot(self, u):
        s = u % RING
        return self.ring[:, s * UNIT:(s + 1) * UNIT]

    def stream(self, sp, n_units):
        end = min(self.n_used + n_units + RING, len(self.order))
        u = self.n_loaded
        while u < end:
            name, i0 = self.order[u]
            run = 1
            while u + run < end and self.order[u + run][0] == name:
                run += 1
            loops = run // RING
            if u >= RING and loops >= 2:
                with sp.Fori(0, loops) as i:
                    for s in range(RING):
                        sp.wait_ge(self.unit_used.sem, i * RING + (u + s + 1 - RING))
                        sp.dma_start(self.slot(u + s),
                                     self.dram[name][bass.ds(i * RING + (i0 + s), 1)].rearrange("o p c -> p (o c)")
                                     ).then_inc(self.arrived[(u + s) % RING].sem, 16)
                u += loops * RING
            else:
                for s in range(min(run, RING)):
                    if u >= RING:
                        sp.wait_ge(self.unit_used.sem, u + 1 - RING)
                    sp.dma_start(self.slot(u), self.dram[name][i0 + s]).then_inc(self.arrived[u % RING].sem, 16)
                    u += 1
        self.n_loaded = u

    def await_unit(self, pe, u, turns=0):
        pe.wait_ge(self.arrived[u % RING].sem, turns * 16 + 16 * (u // RING + 1))

    def project(self, n_m, kt, tile, takes, out_of="scalar"):
        units = n_m * kt // TPU
        assert n_m * kt % TPU == 0
        loops = n_m // 8 if kt == TPU and n_m >= 16 else 0
        pair = out_of == "pair"
        u0, t0 = self.n_used, self.tile_done.n
        free = self.pair_free if pair else [self.bank_free] * 2
        f0 = [x.n for x in free]
        ends = [(s + 1) * kt % TPU == 0 for s in range(n_m)]
        inner = np.cumsum([0] + [not e for e in ends])

        def products(pe, s, i):
            if pair:
                pe.wait_ge(free[s % 2].sem, (i * 4 if i is not None else 0) + (f0[s % 2] + s // 2 + 1 - BANKS // 2))
            else:
                pe.wait_ge(free[0].sem, (i * 8 if i is not None else 0) + (f0[0] + s + 1 - BANKS))
            for k in range(kt):
                q = s * kt + k
                u = u0 + q // TPU
                if q % TPU == 0:
                    self.await_unit(pe, u, i if i is not None else 0)
                ins = tile(k, self.slot(u)[:, q % TPU * P:(q % TPU + 1) * P], s % BANKS, k == 0, k == kt - 1)
                if q % TPU == TPU - 1:
                    ins.then_inc(self.unit_used.sem, 1)
            if not ends[s]:
                ins.then_inc(self.tile_done.sem, 1)

        def take(eng, s, i):
            turn = i * 8 if i is not None else 0
            if ends[s]:
                eng.wait_ge(self.unit_used.sem, turn + (u0 + (s + 1) * kt // TPU))
            else:
                eng.wait_ge(self.tile_done.sem, t0 + int(inner[s + 1]))
            takes(eng, turn + s, s, i).then_inc(free[s % 2].sem, 1)

        def whole(eng, step, which=(0, 1)):
            if loops:
                with eng.Fori(0, loops) as i:
                    for s in range(8):
                        if s % 2 in which:
                            step(eng, s, i)
            for s in range(loops * 8, n_m):
                if s % 2 in which:
                    step(eng, s, None)

        with self.block() as block:
            @block.sync
            def _(sp):
                self.stream(sp, units)

            @block.tensor
            def _(pe):
                whole(pe, products)

            if out_of == "scalar":
                @block.scalar
                def _(act):
                    whole(act, take)
            elif out_of == "vector":
                @block.vector
                def _(dve):
                    whole(dve, take)
            else:
                @block.scalar
                def _(act):
                    whole(act, take, (0,))

                @block.vector
                def _(dve):
                    whole(dve, take, (1,))
        self.n_used += units
        self.tile_done.n += int(inner[-1])
        if pair:
            for x in free:
                x.n += n_m // 2
        else:
            self.bank_free.n += n_m

    def linear(self, n_m, kt, h, cols, out, post=None):
        nc = self.nc
        n = cols.stop - cols.start

        def tile(k, w, bank, first, last):
            return nc.tensor.matmul(self.ps[:, bank, 0:n], w, h[:, k, cols], start=first, stop=last)

        def takes(act, m, s, i):
            return nc.scalar.activation(out(m), self.ps[:, s % BANKS, 0:n], ACT.Copy)
        self.project(n_m, kt, tile, takes)

    def linear_tokens(self, n_m, kt, h, tiles, out):
        nc = self.nc
        assert TPU % kt == 0
        held = []

        def tile(k, w, bank, first, last):
            held.append(w)
            if not last:
                return None
            for j, t in enumerate(tiles):
                for kk in range(kt):
                    ins = nc.tensor.matmul(self.ps[:, bank, j * P:(j + 1) * P], h[:, kk, t * P:(t + 1) * P],
                                           held[kk], start=(kk == 0), stop=(kk == kt - 1))
            held.clear()
            return ins

        def takes(act, m, s, i):
            return nc.scalar.activation(out(m), self.ps[:, s % BANKS, 0:len(tiles) * P]
                                        .rearrange("p (a b) -> p a b", a=len(tiles)), ACT.Copy)
        self.project(n_m, kt, tile, takes)

    def column_sums(self, blocks, n, accumulate, bank=4):
        nc = self.nc
        with self.block() as block:
            @block.tensor
            def _(pe):
                for j, x in enumerate(blocks):
                    dst = self.ps[:, bank, 0:n] if accumulate else self.ps[:, bank + j, 0:n]
                    nc.tensor.matmul(dst, self.ones, x, start=(j == 0 or not accumulate),
                                     stop=(j == len(blocks) - 1 or not accumulate))

    def inverse_root(self, out, sums, scale, eps=EPS):
        nc = self.nc
        a = self.a
        with self.block() as block:
            @block.vector
            def _(dve):
                nc.vector.tensor_scalar(out, sums, scale, eps, ALU.mult, ALU.add).then_inc(self.dve_done.sem, 1)
                dve.wait_ge(self.dve_done.sem, self.dve_done.up())
                nc.vector.reciprocal(out, out).then_inc(a.sem, 1)

            @block.scalar
            def _(act):
                act.wait_ge(a.sem, a.n + 1)
                nc.scalar.activation(out, out, ACT.Sqrt)
        a.n += 1

    def norm_rows(self, x, cols, sq, rstd):
        nc = self.nc
        n = cols.stop - cols.start
        with self.block() as block:
            @block.scalar
            def _(act):
                nc.scalar.activation(sq, x[:, :, cols], ACT.Square)
        self.column_sums([sq[:, k, :] for k in range(x.shape[1])], n, True)
        self.inverse_root(rstd, self.ps[:, 4, 0:n], 1.0 / (x.shape[1] * P))

    def modulated(self, cols, gain, scale, shift):
        nc = self.nc
        n = cols.stop - cols.start
        x, h = self.xT, self.hT
        mark = self.arena.at
        rstd = self.arena.take(n)
        col = self.small_cols
        self.norm_rows(x, cols, h[:, :, cols], rstd)
        a = self.a
        with self.block() as block:
            @block.vector
            def _(dve):
                nc.vector.scalar_tensor_tensor(col, scale, 1.0, gain, ALU.add, ALU.mult).then_inc(self.dve_done.sem, 1)
                dve.wait_ge(self.dve_done.sem, self.dve_done.up())
                for k in range(KT):
                    nc.vector.scalar_tensor_tensor(h[:, k, cols], x[:, k, cols], col[:, k:k + 1], rstd,
                                                   ALU.mult, ALU.mult).then_inc(a.sem, 1)

            @block.scalar
            def _(act):
                for k in range(KT):
                    act.wait_ge(a.sem, a.n + k + 1)
                    nc.scalar.activation(h[:, k, cols], h[:, k, cols], ACT.Identity, bias=shift[:, k:k + 1])
        a.n += KT
        self.arena.at = mark

    def modulation(self, out, cond, n_c, bias):
        nc = self.nc
        u0 = self.n_used
        n_m = 6 * KT
        with self.block() as block:
            @block.sync
            def _(sp):
                self.stream(sp, n_m)

            @block.tensor
            def _(pe):
                with pe.Fori(0, n_m // RING) as i:
                    for s in range(RING):
                        self.await_unit(pe, u0 + s, i)
                        w = self.slot(u0 + s)
                        for k in range(KT):
                            ins = nc.tensor.matmul(self.ps[:, 7, bass.ds(i * (RING * n_c) + s * n_c, n_c)],
                                                   w[:, k * P:(k + 1) * P], cond[:, k, :],
                                                   start=(k == 0), stop=(k == KT - 1))
                        ins.then_inc(self.unit_used.sem, 1)
        self.n_used += n_m
        psm = self.ps[:, 7, 0:n_m * n_c].rearrange("p (m c) -> p m c", c=n_c)
        with self.block() as block:
            @block.vector
            def _(dve):
                for c in range(n_c):
                    nc.vector.tensor_tensor(out[:, :, c], psm[:, :, c], bias, ALU.add)

    def mask(self, out, conditions):
        nc = self.nc
        with self.block() as block:
            @block.gpsimd
            def _(pool):
                nc.gpsimd.memset(out, 1.0).then_inc(self.pool_done.sem, 1)
                pool.wait_ge(self.pool_done.sem, self.pool_done.up())
                for base, cm, pattern in conditions:
                    v = out
                    if len(pattern) == 2:
                        v = out.rearrange("p (a b) -> p a b", a=pattern[0][1])
                    nc.gpsimd.affine_select(
                        out=v, in_=v, compare_op=ALU.is_ge, fill=0.0, base=base, pattern=pattern,
                        channel_multiplier=cm).then_inc(self.pool_done.sem, 1)
                    pool.wait_ge(self.pool_done.sem, self.pool_done.up())

    def constants(self):
        nc, s = self.nc, self.small
        self.one, self.ident, self.iota = s.take(P), s.take(P), s.take(P)
        self.ones = self.one
        self.causal_add = s.take(T + P)
        with self.block() as block:
            @block.gpsimd
            def _(pool):
                nc.gpsimd.memset(self.ones, 1.0)
                nc.gpsimd.memset(self.ident, 0.0).then_inc(self.pool_done.sem, 1)
                pool.wait_ge(self.pool_done.sem, self.pool_done.up())
                nc.gpsimd.affine_select(
                    out=self.ident, in_=self.ident, compare_op=ALU.not_equal, fill=1.0, base=0,
                    pattern=[[-1, P]], channel_multiplier=1).then_inc(self.pool_done.sem, 1)
                pool.wait_ge(self.pool_done.sem, self.pool_done.up())
                nc.gpsimd.iota(
                    self.iota, pattern=[[1, P]], base=0, channel_multiplier=0,
                    allow_small_or_imprecise_dtypes=True).then_inc(self.pool_done.sem, 1)
                pool.wait_ge(self.pool_done.sem, self.pool_done.up())

            @block.vector
            def _(dve):
                nc.vector.memset(self.causal_add, 0.0).then_inc(self.bank_free.sem, BANKS)
                for j, x in enumerate(self.pair_free):
                    nc.vector.memset(self.hT[:, j, 0:1], 0.0).then_inc(x.sem, BANKS // 2)
        self.bank_free.n = BANKS
        for x in self.pair_free:
            x.n = BANKS // 2
        with self.block() as block:
            @block.gpsimd
            def _(pool):
                nc.gpsimd.affine_select(out=self.causal_add, in_=self.causal_add, compare_op=ALU.is_ge,
                                        fill=NEG, base=P, pattern=[[-1, T + P]], channel_multiplier=1)

    def load(self, pairs):
        nc = self.nc
        with self.block() as block:
            @block.scalar
            def _(act):
                for dst, src in pairs:
                    act.dma_start(dst, src).then_inc(self.loaded.sem, 16)
                act.wait_ge(self.loaded.sem, self.loaded.n + 16 * len(pairs))
        self.loaded.n += 16 * len(pairs)

    def attention(self, heads, n_keys, scale, scores, value, out, causal):
        nc, ps = self.nc, self.ps
        nk = n_keys // P
        G = 2 * TT
        mark = self.arena.at
        prob = self.arena.take(G, n_keys)
        turned = self.arena.take(2 * nk, T)
        top, total = self.arena.take(G), self.arena.take(G)
        width = G * n_keys
        sview = ps[:, 0:width // 512, :].rearrange("p b c -> p (b c)")
        a, b = self.a, self.b
        for h0 in range(0, heads, 2):
            with self.block() as block:
                @block.tensor
                def _(pe):
                    for g in range(G):
                        scores(h0 + g // TT, g % TT, sview[:, g * n_keys:(g + 1) * n_keys]).then_inc(a.sem, 1)

                @block.vector
                def _(dve):
                    for g in range(G):
                        dve.wait_ge(a.sem, a.n + (g | (512 // n_keys - 1)) + 1)
                        src = sview[:, g * n_keys:(g + 1) * n_keys]
                        if causal:
                            qt = g % TT
                            ins = nc.vector.tensor_tensor(prob[:, g, :], src,
                                                          self.causal_add[:, P - qt * P:P - qt * P + n_keys], ALU.add)
                        else:
                            ins = nc.vector.tensor_copy(prob[:, g, :], src)
                    ins.then_inc(self.dve_done.sem, 1)
                    dve.wait_ge(self.dve_done.sem, self.dve_done.up())
                    nc.vector.tensor_reduce(top, prob, AX_X, ALU.max).then_inc(self.dve_done.sem, 1)
                    dve.wait_ge(self.dve_done.sem, self.dve_done.up())
                    nc.vector.tensor_scalar(top, top, -scale, None, ALU.mult).then_inc(b.sem, 1)

                @block.scalar
                def _(act):
                    act.wait_ge(b.sem, b.n + 1)
                    for g in range(G):
                        nc.scalar.activation(prob[:, g, :], prob[:, g, :], ACT.Exp, bias=top[:, g:g + 1],
                                             scale=scale, accum_out=total[:, g:g + 1])
            a.n += G
            b.n += 1
            with self.block() as block:
                @block.vector
                def _(dve):
                    nc.vector.reciprocal(total, total).then_inc(self.dve_done.sem, 1)
                    dve.wait_ge(self.dve_done.sem, self.dve_done.up())
                    nc.vector.tensor_tensor(prob, prob, total.unsqueeze(2).broadcast_to([P, G, n_keys]),
                                            ALU.mult)
            tview = ps[:, 0:2 * nk * T // 512, :].rearrange("p b c -> p (b c)")
            oview = ps[:, 6, :]
            with self.block() as block:
                @block.tensor
                def _(pe):
                    for h in range(2):
                        for k in range(nk):
                            for qt in range(TT):
                                at = (h * nk + k) * T + qt * P
                                ins = nc.tensor.transpose(tview[:, at:at + P],
                                                          prob[:, h * TT + qt, k * P:(k + 1) * P], self.ident)
                    ins.then_inc(a.sem, 1)
                    pe.wait_ge(b.sem, b.n + 1)
                    for h in range(2):
                        for k in range(nk):
                            ins = nc.tensor.matmul(oview[:, h * T:(h + 1) * T], value(h0 + h, k),
                                                   turned[:, h * nk + k, :], start=(k == 0), stop=(k == nk - 1))
                    ins.then_inc(a.sem, 1)

                @block.vector
                def _(dve):
                    dve.wait_ge(a.sem, a.n + 1)
                    nc.vector.tensor_copy(flat(turned), tview).then_inc(b.sem, 1)

                @block.scalar
                def _(act):
                    act.wait_ge(a.sem, a.n + 2)
                    for h in range(2):
                        nc.scalar.activation(out(h0 + h), oview[:, h * T:(h + 1) * T], ACT.Copy)
            a.n += 2
            b.n += 1
        self.arena.at = mark

    def rope_tables(self, pos, freq, cos, sin):
        nc = self.nc
        mark = self.arena.at
        ang, n = self.arena.take(T), self.arena.take(T)
        v = nc.vector
        for out, quarter in ((sin, 0.0), (cos, 0.25)):
            with self.block() as block:
                @block.vector
                def _(dve):
                    v.tensor_scalar(ang, pos, freq, None, ALU.mult).then_inc(self.dve_done.sem, 1)
                    dve.wait_ge(self.dve_done.sem, self.dve_done.up())
                    v.tensor_scalar(n, ang, 1.0 / TWO_PI, quarter, ALU.mult, ALU.add).then_inc(self.dve_done.sem, 1)
                    dve.wait_ge(self.dve_done.sem, self.dve_done.up())
                    v.tensor_scalar(n, n, ROUND, -ROUND, ALU.add, ALU.add).then_inc(self.dve_done.sem, 1)
                    dve.wait_ge(self.dve_done.sem, self.dve_done.up())
                    v.scalar_tensor_tensor(ang, n, -PI_A, ang, ALU.mult, ALU.add).then_inc(self.dve_done.sem, 1)
                    dve.wait_ge(self.dve_done.sem, self.dve_done.up())
                    v.scalar_tensor_tensor(ang, n, -PI_B, ang, ALU.mult, ALU.add).then_inc(self.dve_done.sem, 1)
                    dve.wait_ge(self.dve_done.sem, self.dve_done.up())
                    v.scalar_tensor_tensor(ang, n, -PI_C, ang, ALU.mult, ALU.add).then_inc(self.dve_done.sem, 1)
                    dve.wait_ge(self.dve_done.sem, self.dve_done.up())
                    v.tensor_scalar(ang, ang, quarter * TWO_PI, PI_MAX, ALU.add, ALU.min).then_inc(self.dve_done.sem, 1)
                    dve.wait_ge(self.dve_done.sem, self.dve_done.up())
                    v.tensor_scalar(ang, ang, -PI_MAX, None, ALU.max)
            with self.block() as block:
                @block.scalar
                def _(act):
                    nc.scalar.activation(out, ang, ACT.Sin)
        self.arena.at = mark

    def rotation(self, out, half):
        nc = self.nc
        g = P // (2 * half)
        with self.block() as block:
            @block.gpsimd
            def _(pool):
                nc.gpsimd.memset(out, 0.0).then_inc(self.pool_done.sem, 1)
                pool.wait_ge(self.pool_done.sem, self.pool_done.up())
                v = out.rearrange("p (g s h) -> p g s h", g=g, s=2)
                for side, sign, off in ((0, -1.0, half), (1, 1.0, 0)):
                    nc.gpsimd.affine_select(
                        out=v[:, :, side, :], in_=v[:, :, side, :], compare_op=ALU.not_equal, fill=sign,
                        base=-off, pattern=[[-2 * half, g], [-1, half]], channel_multiplier=1).then_inc(self.pool_done.sem, 1)
                    pool.wait_ge(self.pool_done.sem, self.pool_done.up())

    def rope(self, x, rot, cos, sin, cols=None):
        nc = self.nc
        n = x.shape[1]
        a, b = self.a, self.b
        mark = self.arena.at
        tmp = self.arena.take(n, T)
        with self.block() as block:
            @block.tensor
            def _(pe):
                for j in range(n):
                    nc.tensor.matmul(self.ps[:, j // 2, j % 2 * T:(j % 2 + 1) * T], rot, x[:, j, :],
                                     start=True, stop=True)
        psv = self.ps[:, 0:(n + 1) // 2, :].rearrange("p b (c t) -> p (b c) t", t=T)[:, 0:n, :]
        wide = lambda t: t.unsqueeze(1).broadcast_to([P, n, T])
        with self.block() as block:
            @block.vector
            def _(dve):
                nc.vector.tensor_tensor(tmp, psv, wide(sin), ALU.mult).then_inc(self.dve_done.sem, 1)
                dve.wait_ge(self.dve_done.sem, self.dve_done.up())
                nc.vector.tensor_tensor(x, x, wide(cos), ALU.mult).then_inc(self.dve_done.sem, 1)
                dve.wait_ge(self.dve_done.sem, self.dve_done.up())
                nc.vector.tensor_tensor(x, x, tmp, ALU.add)
        self.arena.at = mark

    def scaled_root(self, x2d, m, scale, out, eps=EPS):
        nc = self.nc
        with self.block() as block:
            @block.scalar
            def _(act):
                nc.scalar.activation(out, x2d, ACT.Square)
        w = min(m, 512)
        self.column_sums([out[:, i:i + w] for i in range(0, m, w)], w, False, bank=0)
        self.inverse_root(out, self.ps[:, 0:m // w, 0:w].rearrange("p b c -> p (b c)") if m > w
                          else self.ps[:, 0, 0:m], scale, eps)

    def hybrid(self, c):
        nc, ps, A = self.nc, self.ps, self.arena
        v, s = nc.vector, nc.scalar
        mark = A.at
        PR = HEADS * TT
        o = A.take(2 * HEADS, T)
        ztile = A.take(HEADS, T)
        qkb = A.take(2 * HEADS, T)
        vb_tok = A.take(TT, HEADS * P)
        proj = A.take(24, T)
        self.linear(24, KT, self.hT, LAT, lambda m: flat(proj)[:, bass.ds(m * T, T)])
        self.linear_tokens(HEADS, KT, self.hT[:, :, LAT], range(TT), lambda m: vb_tok[:, :, m * P:(m + 1) * P])
        with self.block() as block:
            @block.tensor
            def _(pe):
                for t in range(TT):
                    for k in range(KT):
                        nc.tensor.matmul(ps[:, 4, t * 8:(t + 1) * 8],
                                         self.hT[:, k, TC + t * P:TC + (t + 1) * P],
                                         c["gates"][:, k, :], start=(k == 0), stop=(k == KT - 1))
        beta, g, tmp, absx = A.take(HEADS, TT), A.take(HEADS, TT), A.take(HEADS, TT), A.take(HEADS, TT)
        ab = ps[:, 4, 0:2 * HEADS * TT].rearrange("p (t s h) -> p s h t", t=TT, s=2)
        wide = lambda x: x.unsqueeze(2).broadcast_to([P, HEADS, TT])
        with self.block() as block:
            @block.scalar
            def _(act):
                s.activation(beta, ab[:, 0], ACT.Sigmoid).then_inc(self.act_done.sem, 1)
                act.wait_ge(self.act_done.sem, self.act_done.up())
                s.activation(c["decay"], c["a_log"], ACT.Exp)
        with self.block() as block:
            @block.vector
            def _(dve):
                v.tensor_tensor(g, ab[:, 1], wide(c["dt_bias"]), ALU.add).then_inc(self.dve_done.sem, 1)
                dve.wait_ge(self.dve_done.sem, self.dve_done.up())
                v.tensor_scalar(tmp, g, -1.0, None, ALU.mult).then_inc(self.dve_done.sem, 1)
                dve.wait_ge(self.dve_done.sem, self.dve_done.up())
                v.tensor_tensor(absx, g, tmp, ALU.max)
        with self.block() as block:
            @block.scalar
            def _(act):
                s.activation(tmp, absx, ACT.Exp, scale=-1.0).then_inc(self.act_done.sem, 1)
                act.wait_ge(self.act_done.sem, self.act_done.up())
                s.activation(tmp, tmp, ACT.Ln, bias=1.0)
        with self.block() as block:
            @block.vector
            def _(dve):
                v.scalar_tensor_tensor(g, g, 0.0, tmp, ALU.max, ALU.add).then_inc(self.dve_done.sem, 1)
                dve.wait_ge(self.dve_done.sem, self.dve_done.up())
                v.scalar_tensor_tensor(g, g, -1.0, wide(c["decay"]), ALU.mult, ALU.mult)
        conv = A.take(12, T)
        w = c["conv"]
        with self.block() as block:
            @block.vector
            def _(dve):
                for j in range(4):
                    for m in range(12):
                        if j == 0:
                            ins = v.tensor_scalar(conv[:, m, :], proj[:, m, :], w[:, m, 3:4], None, ALU.mult)
                        else:
                            ins = v.scalar_tensor_tensor(conv[:, m, j:T], proj[:, m, 0:T - j], w[:, m, 3 - j:4 - j],
                                                         conv[:, m, j:T], ALU.mult, ALU.add)
                    ins.then_inc(self.dve_done.sem, 1)
                    dve.wait_ge(self.dve_done.sem, self.dve_done.up())

            @block.scalar
            def _(act):
                s.activation(ztile, proj[:, 12:16, :], ACT.Silu)

            @block.gpsimd
            def _(pool):
                nc.gpsimd.tensor_copy(qkb, proj[:, 16:24, :])
        with self.block() as block:
            @block.scalar
            def _(act):
                s.activation(conv, conv, ACT.Silu)
        root = flat(proj)[:, 0:8 * T]
        self.scaled_root(flat(conv[:, 0:8, :]), 8 * T, 1.0, root)
        with self.block() as block:
            @block.vector
            def _(dve):
                v.tensor_tensor(flat(conv[:, 0:8, :]), flat(conv[:, 0:8, :]), root, ALU.mult)
        pairs = lambda x: x.rearrange("p h (t c) -> p (h t) c", c=P)
        qT, kT, vT = (pairs(conv[:, 4 * i:4 * i + 4, :]) for i in range(3))

        A2 = Space(proj.tensor, self.arena.size)
        A2.at = A.at
        base = A.at
        upto, within, strict = A.take(P), A.take(P), A.take(P)
        nch = P // CHUNK
        same = [(0, 1, [[-CHUNK, nch], [0, CHUNK]]), (CHUNK - 1, -1, [[CHUNK, nch], [0, CHUNK]])]
        self.mask(within, same)
        self.mask(upto, same + [(0, -1, [[1, P]])])
        self.mask(strict, same + [(-1, 1, [[-1, P]])])
        gp, bp = g.rearrange("p h t -> p (h t)"), beta.rearrange("p h t -> p (h t)")
        gb = A.take(PR, P)
        cum, tot, kdec_c, kbe_c = (A.take(PR) for _ in range(4))
        with self.block() as block:
            @block.vector
            def _(dve):
                for p in range(PR):
                    v.tensor_scalar(gb[:, p, :], self.ones, gp[:, p:p + 1], None, ALU.mult)
        with self.block() as block:
            @block.tensor
            def _(pe):
                nc.tensor.matmul(ps[:, 6, 0:PR], upto, gp, start=True, stop=True)
                nc.tensor.matmul(ps[:, 7, 0:PR], within, gp, start=True, stop=True)
                for p in range(PR):
                    nc.tensor.matmul(ps[:, p // 4, p % 4 * P:(p % 4 + 1) * P], gb[:, p, :], upto, start=True, stop=True)
                for p in range(PR):
                    nc.tensor.matmul(ps[:, 2 + p // 4, p % 4 * P:(p % 4 + 1) * P], kT[:, p, :], kT[:, p, :],
                                     start=True, stop=True)
                for p in range(PR):
                    nc.tensor.matmul(ps[:, 4 + p // 4, p % 4 * P:(p % 4 + 1) * P], kT[:, p, :], qT[:, p, :],
                                     start=True, stop=True)
        two = lambda b: ps[:, b:b + 2, :].rearrange("p b (c m) -> p (b c) m", m=P)
        rows, kk, kq = two(0), two(2), ps[:, 4:6, :].rearrange("p b (c m) -> p (b c) m", m=P)
        rowexp, dec, decT = A.take(PR, P), gb, A.take(PR, P)
        a = self.a
        with self.block() as block:
            @block.vector
            def _(dve):
                v.tensor_copy(cum, ps[:, 6, 0:PR]).then_inc(self.dve_done.sem, 1)
                dve.wait_ge(self.dve_done.sem, self.dve_done.up())
                v.tensor_copy(tot, ps[:, 7, 0:PR]).then_inc(self.dve_done.sem, 1)
                dve.wait_ge(self.dve_done.sem, self.dve_done.up())
                v.tensor_tensor(kdec_c, tot, cum, ALU.subtract)
        with self.block() as block:
            @block.vector
            def _(dve):
                for p in range(PR):
                    v.tensor_scalar(dec[:, p, :], rows[:, p, :], cum[:, p:p + 1], 0.0, ALU.subtract, ALU.max)
                    v.tensor_scalar(decT[:, p, :], rows[:, p, :], cum[:, p:p + 1], 0.0, ALU.subtract, ALU.min)

        with self.block() as block:
            @block.scalar
            def _(act):
                s.activation(rowexp, rows, ACT.Exp)
                s.activation(dec, dec, ACT.Exp, scale=-1.0)
                s.activation(decT, decT, ACT.Exp)
                s.activation(kdec_c, kdec_c, ACT.Exp)
                s.activation(kbe_c, cum, ACT.Exp)
        bwide = lambda x: x.unsqueeze(1).broadcast_to([P, PR, P])
        pw, pwT, invT = A.take(PR, P), A.take(PR, P), A.take(PR, P)
        qk = decT
        DKS = float(P) ** -0.5
        with self.block() as block:
            @block.vector
            def _(dve):
                v.tensor_tensor(kbe_c, kbe_c, bp, ALU.mult).then_inc(self.dve_done.sem, 1)
                dve.wait_ge(self.dve_done.sem, self.dve_done.up())
                v.tensor_tensor(dec, dec, bwide(strict), ALU.mult).then_inc(self.dve_done.sem, 1)
                dve.wait_ge(self.dve_done.sem, self.dve_done.up())
                v.tensor_tensor(dec, dec, bp.unsqueeze(2).broadcast_to([P, PR, P]), ALU.mult).then_inc(self.dve_done.sem, 1)
                dve.wait_ge(self.dve_done.sem, self.dve_done.up())
                v.scalar_tensor_tensor(flat(pw), flat(dec), -1.0, flat(kk), ALU.mult, ALU.mult).then_inc(self.dve_done.sem, 1)
                dve.wait_ge(self.dve_done.sem, self.dve_done.up())
                v.tensor_tensor(decT, decT, bwide(upto), ALU.mult).then_inc(self.dve_done.sem, 1)
                dve.wait_ge(self.dve_done.sem, self.dve_done.up())
                v.scalar_tensor_tensor(flat(qk), flat(decT), DKS, flat(kq), ALU.mult, ALU.mult).then_inc(self.dve_done.sem, 1)
                dve.wait_ge(self.dve_done.sem, self.dve_done.up())
                v.scalar_tensor_tensor(flat(qT), flat(qT), DKS, flat(rowexp), ALU.mult, ALU.mult)

        def turn(src, bank):
            with self.block() as block:
                @block.tensor
                def _(pe):
                    for p in range(PR):
                        nc.tensor.transpose(ps[:, bank + p // 4, p % 4 * P:(p % 4 + 1) * P], src[:, p, :], self.ident)

        def times(lhsT, rhs, bank):
            for p in range(PR):
                nc.tensor.matmul(ps[:, bank + p // 4, p % 4 * P:(p % 4 + 1) * P], lhsT[:, p, :], rhs[:, p, :],
                                 start=True, stop=True)
        turn(pw, 0)
        with self.block() as block:
            @block.vector
            def _(dve):
                v.tensor_copy(pwT, two(0)).then_inc(self.dve_done.sem, 1)
                dve.wait_ge(self.dve_done.sem, self.dve_done.up())
                v.tensor_tensor(invT, pwT, bwide(self.ident), ALU.add)
        span = 2
        while span < CHUNK:
            with self.block() as block:
                @block.tensor
                def _(pe):
                    times(pwT, pw, 0)
                    times(pw, pwT, 2)
            with self.block() as block:
                @block.vector
                def _(dve):
                    v.tensor_copy(pw, two(0))

                @block.scalar
                def _(act):
                    s.activation(pwT, two(2), ACT.Copy)
            with self.block() as block:
                @block.tensor
                def _(pe):
                    times(pw, invT, 4)
            with self.block() as block:
                @block.vector
                def _(dve):
                    v.tensor_tensor(invT, invT, two(4), ALU.add)
            span *= 2
        vbeta, kbe, kdec = pw, pwT, dec
        turn(kT, 0)
        turn(vT, 2)
        with self.block() as block:
            @block.vector
            def _(dve):
                for p in range(PR):
                    v.tensor_scalar(kbe[:, p, :], two(0)[:, p, :], kbe_c[:, p:p + 1], None, ALU.mult)
                    v.tensor_scalar(kdec[:, p, :], two(0)[:, p, :], kdec_c[:, p:p + 1], None, ALU.mult)
                    v.tensor_scalar(vbeta[:, p, :], two(2)[:, p, :], bp[:, p:p + 1], None, ALU.mult)
        with self.block() as block:
            @block.tensor
            def _(pe):
                times(invT, vbeta, 4)
                times(kbe, invT, 6)
        u, wT = A.take(PR, P), A.take(PR, P)
        with self.block() as block:
            @block.vector
            def _(dve):
                v.tensor_copy(u, two(4))

            @block.scalar
            def _(act):
                s.activation(wT, two(6), ACT.Copy)
        state = A.take(HEADS, P)
        vnew = vbeta
        hv = lambda x: x.rearrange("p (h t) c -> p h t c", t=TT)
        oview = two(4)
        for n in range(T // CHUNK):
            t, r = n // nch, slice(n % nch * CHUNK, (n % nch + 1) * CHUNK)
            if n:
                with self.block() as block:
                    @block.tensor
                    def _(pe):
                        for h in range(HEADS):
                            nc.tensor.matmul(ps[:, 0, h * P:(h + 1) * P], wT[:, h * TT + t, :], state[:, h, :],
                                             start=True, stop=True)
                with self.block() as block:
                    @block.vector
                    def _(dve):
                        v.tensor_tensor(hv(vnew)[r, :, t, :], hv(u)[r, :, t, :],
                                        ps[r, 0, :].rearrange("p (h c) -> p h c", h=HEADS), ALU.subtract)
            else:
                with self.block() as block:
                    @block.vector
                    def _(dve):
                        v.tensor_copy(hv(vnew)[r, :, t, :], hv(u)[r, :, t, :])
            with self.block() as block:
                @block.tensor
                def _(pe):
                    for h in range(HEADS):
                        p = h * TT + t
                        if n:
                            nc.tensor.matmul(oview[:, p, r], state[:, h, :], qT[:, p, r], start=True, stop=False)
                        nc.tensor.matmul(oview[:, p, r], vnew[r, p, :], qk[r, p, r], start=(n == 0), stop=True)
                    for h in range(HEADS):
                        p = h * TT + t
                        nc.tensor.matmul(ps[:, 6, h * P:(h + 1) * P], kdec[r, p, :], vnew[r, p, :],
                                         start=True, stop=True)
            with self.block() as block:
                @block.vector
                def _(dve):
                    for h in range(HEADS):
                        upd = ps[:, 6, h * P:(h + 1) * P]
                        if n:
                            v.scalar_tensor_tensor(state[:, h, :], state[:, h, :],
                                                   rowexp[:, h * TT + t, r.stop - 1:r.stop], upd, ALU.mult, ALU.add)
                        else:
                            v.tensor_copy(state[:, h, :], upd)
        oa = o[:, 0:HEADS, :]
        with self.block() as block:
            @block.scalar
            def _(act):
                s.activation(pairs(oa), oview, ACT.Copy)
        root = flat(proj)[:, 0:HEADS * T]
        self.scaled_root(flat(oa), HEADS * T, 1.0 / P, root)
        with self.block() as block:
            @block.vector
            def _(dve):
                v.scalar_tensor_tensor(flat(oa), flat(oa), c["o_norm"], root, ALU.mult, ALU.mult).then_inc(self.dve_done.sem, 1)
                dve.wait_ge(self.dve_done.sem, self.dve_done.up())
                v.tensor_tensor(flat(oa), flat(oa), flat(ztile), ALU.mult)
        A.at = base
        self.rope(qkb, c["rot"], c["cos"], c["sin"])

        def scores(h, qt, dst):
            return nc.tensor.matmul(dst, qkb[:, h, qt * P:(qt + 1) * P], qkb[:, HEADS + h, :], start=True, stop=True)
        self.attention(HEADS, T, DKS, scores, lambda h, k: vb_tok[:, k, h * P:(h + 1) * P],
                       lambda h: o[:, HEADS + h, :], True)
        self.output(o, LAT, c["g1"])
        A.at = mark

    def output(self, o, cols, gate):
        nc = self.nc
        n = cols.stop - cols.start

        def tile(k, w, bank, first, last):
            return nc.tensor.matmul(self.ps[:, bank, 0:n], w, o[:, k, :], start=first, stop=last)

        def takes(dve, m, s, i):
            x = self.xT[:, m, cols]
            return nc.vector.scalar_tensor_tensor(x, self.ps[:, s % BANKS, 0:n], gate[:, m:m + 1], x, ALU.mult, ALU.add)
        self.project(KT, o.shape[1], tile, takes, "vector")

    def peer_routes(self, subkeys):
        nc, ps, A = self.nc, self.ps, self.arena
        v = nc.vector
        mark = A.at
        SIDES = 2 * PH
        qT = A.take(SIDES, T)
        keys = A.take(SIDES, KEYS)
        self.load([(keys, subkeys)])
        self.linear(SIDES, KT, self.hT, LAT, lambda m: flat(qT)[:, bass.ds(m * T, T)])
        score, work = A.take(SIDES, KEYS), A.take(KEYS)
        val, idx = A.take(SIDES, TOPK), A.take(SIDES, TOPK)
        idx_u = A.take(SIDES, TOPK, dt=U32)
        cand, cwork = A.take(PH, TOPK * TOPK), A.take(TOPK * TOPK)
        top, gate = A.take(PH, TOPK), A.take(PH, TOPK)
        pos_u, part_u = A.take(PH, TOPK, dt=U32), A.take(PH, TOPK, dt=U32)
        part = A.take(PH, TOPK)
        onehot = A.take(PH * TOPK, TOPK)
        mx, total = A.take(PH), A.take(PH)
        expert = A.take(2, PH * TOPK)
        ps2 = ps[:, 0:4, :].rearrange("p b (c n) -> p (b c) n", n=KEYS)

        def top16(dve, values, scratch, out, out_idx):
            lo, hi = slice(0, 8), slice(8, 16)
            v.max(out[:, lo], values).then_inc(self.dve_done.sem, 1)
            dve.wait_ge(self.dve_done.sem, self.dve_done.up())
            v.max_index(out_idx[:, lo], out[:, lo], values)
            v.match_replace(out=scratch, in_to_replace=out[:, lo],
                                                           in_values=values, imm_value=LOWEST).then_inc(self.dve_done.sem, 1)
            dve.wait_ge(self.dve_done.sem, self.dve_done.up())
            v.max(out[:, hi], scratch).then_inc(self.dve_done.sem, 1)
            dve.wait_ge(self.dve_done.sem, self.dve_done.up())
            v.max_index(out_idx[:, hi], out[:, hi], scratch)

        for t in range(TT):
            with self.block() as block:
                @block.tensor
                def _(pe):
                    for j in range(SIDES):
                        nc.tensor.matmul(ps2[:, j, :], qT[:, j, t * P:(t + 1) * P], keys[:, j, :],
                                         start=True, stop=True)
            with self.block() as block:
                @block.scalar
                def _(act):
                    nc.scalar.activation(score, ps2, ACT.Copy)
            with self.block() as block:
                @block.vector
                def _(dve):
                    for j in range(SIDES):
                        top16(dve, score[:, j, :], work, val[:, j, :], idx_u[:, j, :])
            sides = val.rearrange("p (h s) k -> p s h k", s=2)
            full = [P, PH, TOPK, TOPK]
            with self.block() as block:
                @block.vector
                def _(dve):
                    v.tensor_copy(idx, idx_u).then_inc(self.dve_done.sem, 1)
                    dve.wait_ge(self.dve_done.sem, self.dve_done.up())
                    v.tensor_tensor(cand.rearrange("p h (a b) -> p h a b", a=TOPK),
                                    sides[:, 0].unsqueeze(3).broadcast_to(full),
                                    sides[:, 1].unsqueeze(2).broadcast_to(full), ALU.add)
            with self.block() as block:
                @block.vector
                def _(dve):
                    for h in range(PH):
                        top16(dve, cand[:, h, :], cwork, top[:, h, :], pos_u[:, h, :])
            hw = lambda x: x.unsqueeze(2).broadcast_to([P, PH, TOPK])
            with self.block() as block:
                @block.vector
                def _(dve):
                    v.tensor_copy(mx, top[:, :, 0]).then_inc(self.dve_done.sem, 1)
                    dve.wait_ge(self.dve_done.sem, self.dve_done.up())
                    v.tensor_tensor(gate, top, hw(mx), ALU.subtract)
            with self.block() as block:
                @block.scalar
                def _(act):
                    nc.scalar.activation(gate, gate, ACT.Exp)
            with self.block() as block:
                @block.vector
                def _(dve):
                    v.tensor_reduce(total, gate, AX_X, ALU.add).then_inc(self.dve_done.sem, 1)
                    dve.wait_ge(self.dve_done.sem, self.dve_done.up())
                    v.reciprocal(total, total).then_inc(self.dve_done.sem, 1)
                    dve.wait_ge(self.dve_done.sem, self.dve_done.up())
                    v.tensor_tensor(gate, gate, hw(total), ALU.mult)
            idxs = idx.rearrange("p (h s) k -> p s h k", s=2)
            big = [P, PH * TOPK, TOPK]
            oh4 = onehot.rearrange("p (h k) a -> p h k a", h=PH)
            for side, (op, by) in enumerate(((ALU.logical_shift_right, 4), (ALU.bitwise_and, 15))):
                with self.block() as block:
                    @block.vector
                    def _(dve):
                        v.tensor_scalar(part_u, pos_u, by, None, op).then_inc(self.dve_done.sem, 1)
                        dve.wait_ge(self.dve_done.sem, self.dve_done.up())
                        v.tensor_copy(part, part_u).then_inc(self.dve_done.sem, 1)
                        dve.wait_ge(self.dve_done.sem, self.dve_done.up())
                        v.tensor_tensor(onehot, part.rearrange("p h k -> p (h k)").unsqueeze(2).broadcast_to(big),
                                        self.iota[:, 0:TOPK].unsqueeze(1).broadcast_to(big), ALU.is_equal).then_inc(self.dve_done.sem, 1)
                        dve.wait_ge(self.dve_done.sem, self.dve_done.up())
                        v.tensor_tensor(oh4, oh4, idxs[:, side].unsqueeze(2).broadcast_to(full), ALU.mult).then_inc(self.dve_done.sem, 1)
                        dve.wait_ge(self.dve_done.sem, self.dve_done.up())
                        v.tensor_reduce(expert[:, side, :], onehot, AX_X, ALU.add)
            with self.block() as block:
                @block.tensor
                def _(pe):
                    for j, x in enumerate((expert[:, 0, :], expert[:, 1, :], flat(gate))):
                        nc.tensor.transpose(ps[:, 5, j * P:(j + 1) * P], x, self.ident)
            with self.block() as block:
                @block.vector
                def _(dve):
                    v.tensor_copy(self.selT[:, :, t * P:(t + 1) * P],
                                  ps[:, 5, 0:3 * P].rearrange("p (a b) -> p a b", a=3))
        A.at = mark

    def peer_experts(self, gate_col):
        nc, ps, A = self.nc, self.ps, self.arena
        v, s = nc.vector, nc.scalar
        mark = A.at
        G = A.take(T, KEYS)
        gflat = flat(G)
        B = 4
        spare = self.xT[:, :, 0:TC]
        row1 = lambda i, j: spare[:, 2 * i + j // 2, j % 2 * P:(j % 2 + 1) * P]
        row2 = lambda i, j: spare[:, 4 + 2 * i + j // 2, j % 2 * P:(j % 2 + 1) * P]
        onehots, placed, taken = self.a, self.b, self.c
        a0, b0, c0 = onehots.n, placed.n, taken.n
        sel = self.selT
        with self.block() as block:
            @block.vector
            def _(dve):
                v.memset(row1(0, 0), 0.0).then_inc(placed.sem, 2)
                v.memset(row1(1, 0), 0.0).then_inc(taken.sem, 2)
        b0 += 2
        c0 += 2
        TURNS = T // B // 2
        with self.block() as block:
            @block.vector
            def _(dve):
                with dve.Fori(0, TURNS) as i:
                    for half in range(2):
                        dve.wait_ge(placed.sem, i * 2 + (b0 + half - 1))
                        for j in range(B):
                            t = i * (2 * B) + (half * B + j)
                            v.tensor_scalar(row1(half, j), self.iota, sel[:, 0, bass.ds(t, 1)],
                                            sel[:, 2, bass.ds(t, 1)], ALU.is_equal, ALU.mult)
                            ins = v.tensor_scalar(row2(half, j), self.iota, sel[:, 1, bass.ds(t, 1)], None,
                                                  ALU.is_equal)
                        ins.then_inc(onehots.sem, 1)

            @block.tensor
            def _(pe):
                with pe.Fori(0, TURNS) as i:
                    for half in range(2):
                        pe.wait_ge(onehots.sem, i * 2 + (a0 + half + 1))
                        pe.wait_ge(taken.sem, i * 2 + (c0 + half - 1))
                        for j in range(B):
                            ins = nc.tensor.matmul(ps[:, half, j * P:(j + 1) * P], row1(half, j), row2(half, j),
                                                   start=True, stop=True)
                        ins.then_inc(placed.sem, 1)

            @block.scalar
            def _(act):
                with act.Fori(0, TURNS) as i:
                    for half in range(2):
                        act.wait_ge(placed.sem, i * 2 + (b0 + half + 1))
                        s.activation(gflat[:, bass.ds(i * (2 * B * P) + half * B * P, B * P)], ps[:, half, :],
                                     ACT.Copy).then_inc(taken.sem, 1)
        onehots.n, placed.n, taken.n = a0 + 2 * TURNS, b0 + 2 * TURNS, c0 + 2 * TURNS

        act_sb = [spare[:, i, :] for i in range(2)]
        w_sb = [spare[:, 2 + i, :] for i in range(2)]
        gelu_done, w_done = self.b, self.c
        b0, c0 = gelu_done.n, w_done.n
        unit0 = self.n_used
        LOOPS = (KEYS - 4) // 4

        def peeled(eng, first, step, last):
            first()
            with eng.Fori(0, LOOPS) as i:
                for q in range(4):
                    step(i * 4 + (1 + q), (1 + q) % 2, i, q)
            for j in range(4 * LOOPS + 1, KEYS - 1):
                step(j, j % 2, None, 0)
            last()

        with self.block() as block:
            @block.sync
            def _(sp):
                self.stream(sp, 2 * KEYS)

            @block.tensor
            def _(pe):
                def hidden(par, u, turn):
                    self.await_unit(pe, u, turn)
                    w = self.slot(u)
                    for k in range(KT):
                        ins = nc.tensor.matmul(ps[:, 4 + par, 0:T], w[:, k * P:(k + 1) * P], self.hT[:, k, LAT],
                                               start=(k == 0), stop=(k == KT - 1))
                    ins.then_inc(self.unit_used.sem, 1)

                def expand(j, par, u, turn, first, last):
                    self.await_unit(pe, u, turn)
                    pe.wait_ge(w_done.sem, j + (c0 + 1))
                    w = self.slot(u)
                    for m in range(KT):
                        ins = nc.tensor.matmul(ps[:, m // 2, m % 2 * T:(m % 2 + 1) * T], w[:, m * P:(m + 1) * P],
                                               w_sb[par], start=(first and m % 2 == 0), stop=last,
                                               skip_group_check=True)
                    ins.then_inc(self.unit_used.sem, 1)

                def step(j, par, i, q):
                    pe.wait_ge(gelu_done.sem, j + b0)
                    u = unit0 + 2 * j + 1 if i is None else unit0 + 3 + 2 * q
                    turn = 0 if i is None else i
                    hidden((par + 1) % 2, u, turn)
                    expand(j, par, u + 1, turn, False, False)

                def first():
                    hidden(0, unit0, 0)
                    hidden(1, unit0 + 1, 0)
                    expand(0, 0, unit0 + 2, 0, True, False)
                peeled(pe, first, step,
                       lambda: expand(KEYS - 1, (KEYS - 1) % 2, unit0 + 2 * KEYS - 1, 0, False, True))

            @block.scalar
            def _(act):
                def gelu(j, par, reused=True):
                    first = isinstance(j, int) and j == 0
                    act.wait_ge(self.unit_used.sem, j * 2 + (unit0 + first))
                    if reused:
                        act.wait_ge(w_done.sem, j + (c0 - 1))
                    s.activation(act_sb[par], ps[:, 4 + par, 0:T], ACT.Gelu).then_inc(gelu_done.sem, 1)
                peeled(act, lambda: (gelu(0, 0, False), gelu(1, 1, False)),
                       lambda j, par, i, q: gelu(j + 1, (par + 1) % 2), lambda: None)

            @block.vector
            def _(dve):
                def weigh(j, par, i=None, q=0):
                    dve.wait_ge(gelu_done.sem, j + (b0 + 1))
                    if not isinstance(j, int) or j >= 2:
                        dve.wait_ge(self.unit_used.sem, j * 2 + (unit0 - 1))
                    v.tensor_tensor(w_sb[par], act_sb[par], G[:, :, bass.ds(j, 1)].rearrange("p t o -> p (t o)"),
                                    ALU.mult).then_inc(w_done.sem, 1)
                peeled(dve, lambda: weigh(0, 0), weigh,
                       lambda: weigh(KEYS - 1, (KEYS - 1) % 2))
        self.n_used += 2 * KEYS
        gelu_done.n, w_done.n = b0 + KEYS, c0 + KEYS
        with self.block() as block:
            @block.vector
            def _(dve):
                for m in range(KT):
                    x = self.xT[:, m, LAT]
                    v.scalar_tensor_tensor(x, ps[:, m // 2, m % 2 * T:(m % 2 + 1) * T], gate_col[:, m:m + 1], x,
                                           ALU.mult, ALU.add)
        A.at = mark

    def latent_attention(self, c):
        nc, ps, A = self.nc, self.ps, self.arena
        v = nc.vector
        mark = A.at
        low = A.take(7, T)
        q, kn = A.take(12, T), A.take(MLA_H, T)
        vt = A.take(TT, MLA_H * P)
        o = A.take(MLA_H, T)
        sq, root = A.take(4, T), A.take(T)
        self.linear(7, KT, self.hT, LAT, lambda m: low[:, m, :])
        for a0, n in ((0, 4), (4, 2)):
            part = low[:, a0:a0 + n, :]
            self.norm_rows(part, slice(0, T), sq[:, 0:n, :], root)
            with self.block() as block:
                @block.vector
                def _(dve):
                    for k in range(n):
                        v.scalar_tensor_tensor(part[:, k, :], part[:, k, :], c["norms"][:, a0 + k:a0 + k + 1], root,
                                               ALU.mult, ALU.mult)
        self.linear(12, 4, low, slice(0, T), lambda m: q[:, m, :])
        self.linear(MLA_H, 2, low[:, 4:6, :], slice(0, T), lambda m: kn[:, m, :])
        self.linear_tokens(MLA_H, 2, low[:, 4:6, :], range(TT), lambda m: vt[:, :, m * P:(m + 1) * P])
        self.rope(q[:, 8:12, :], c["rot"], c["cos"], c["sin"])
        self.rope(low[:, 6:7, :], c["rot"], c["cos"], c["sin"])

        def scores(h, qt, dst):
            r = slice(h % 2 * 64, h % 2 * 64 + 64)
            tok = slice(qt * P, (qt + 1) * P)
            nc.tensor.matmul(dst, q[:, h, tok], kn[:, h, :], start=True, stop=False)
            return nc.tensor.matmul(dst, q[r, 8 + h // 2, tok], low[r, 6, :], start=False, stop=True)
        self.attention(MLA_H, T, float(192) ** -0.5, scores, lambda h, k: vt[:, k, h * P:(h + 1) * P],
                       lambda h: o[:, h, :], True)
        self.output(o, LAT, c["g1"])
        A.at = mark

    def add_normed(self, y, parts, gain):
        nc = self.nc
        v = nc.vector
        mark = self.arena.at
        c0, c1 = parts[0][0].start, parts[-1][0].stop
        sq, root, col = self.arena.take(KT, c1 - c0), self.arena.take(c1 - c0), self.arena.take(len(parts), KT)
        self.norm_rows(y, slice(0, c1 - c0), sq, root)
        with self.block() as block:
            @block.vector
            def _(dve):
                for j, (cols, g) in enumerate(parts):
                    ins = v.tensor_tensor(col[:, j, :], g, gain, ALU.mult)
                ins.then_inc(self.dve_done.sem, 1)
                dve.wait_ge(self.dve_done.sem, self.dve_done.up())
                for j, (cols, g) in enumerate(parts):
                    at = slice(cols.start - c0, cols.stop - c0)
                    for k in range(KT):
                        ins = v.scalar_tensor_tensor(sq[:, k, at], y[:, k, at], col[:, j, k:k + 1], root[:, at],
                                                     ALU.mult, ALU.mult)
                ins.then_inc(self.dve_done.sem, 1)
                dve.wait_ge(self.dve_done.sem, self.dve_done.up())
                x = self.xT[:, :, c0:c1]
                v.tensor_tensor(x, x, sq, ALU.add)
        self.arena.at = mark

    def swiglu(self, parts, gain_in, gain_out):
        nc, A = self.nc, self.arena
        for cols, shift, scale, _ in parts:
            self.modulated(cols, gain_in, scale, shift)
        mark = A.at
        cols = slice(parts[0][0].start, parts[-1][0].stop)
        n = cols.stop - cols.start
        hidden = A.take(FT, n)
        lit = A.take(2, n)
        y = A.take(KT, n)
        silu_done = self.pair_free[0]
        s0, f0 = silu_done.n, self.pair_free[1].n

        def tile(k, w, bank, first, last):
            return nc.tensor.matmul(self.ps[:, bank, 0:n], w, self.hT[:, k, cols], start=first, stop=last)

        def takes(eng, m, s, i):
            p = (i * 4 if i is not None else 0) + s // 2
            src = self.ps[:, s % BANKS, 0:n]
            if s % 2 == 0:
                eng.wait_ge(self.pair_free[1].sem, p + (f0 - 1))
                return nc.scalar.activation(lit[:, s // 2 % 2, :], src, ACT.Silu)
            eng.wait_ge(silu_done.sem, p + (s0 + 1))
            return nc.vector.tensor_tensor(flat(hidden)[:, bass.ds(p * n, n)], src, lit[:, s // 2 % 2, :], ALU.mult)
        self.project(2 * FT, KT, tile, takes, "pair")
        self.linear(KT, FT, hidden, slice(0, n), lambda m: y[:, m, :])
        self.add_normed(y, [(c, g) for c, _, _, g in parts], gain_out)
        A.at = mark

    def hgrn_head(self, h, q, k, logf, value, resets, masks, out, tmp):
        nc, ps = self.nc, self.ps
        v, s = nc.vector, nc.scalar
        NC = TA // HCHUNK
        b, e_mid, e_inv, e_b, e_last, dec, att, ktok, state = tmp
        ch = lambda x: x.rearrange("p (c t) -> p c t", t=HCHUNK)
        tl = lambda x: x.rearrange("p (c t) -> p c t", t=P)
        for d in range(2):
            mid, last = (HCHUNK // 2 - 1, HCHUNK - 1) if d == 0 else (HCHUNK // 2, 0)
            way = (lambda x: x) if d == 0 else (lambda x: x[:, ::-1])
            wide = lambda i: ch(b)[:, :, i:i + 1].broadcast_to([P, NC, HCHUNK])
            with self.block() as block:
                @block.vector
                def _(dve):
                    v.tensor_tensor_scan(way(b), way(resets[d]), way(logf[d]), 0.0, ALU.mult, ALU.add).then_inc(self.dve_done.sem, 1)
                    dve.wait_ge(self.dve_done.sem, self.dve_done.up())
                    v.tensor_tensor(ch(e_mid), ch(b), wide(mid), ALU.subtract).then_inc(self.dve_done.sem, 1)
                    dve.wait_ge(self.dve_done.sem, self.dve_done.up())
                    v.tensor_tensor(ch(e_last), wide(last), ch(b), ALU.subtract)
            with self.block() as block:
                @block.scalar
                def _(act):
                    s.activation(e_inv, e_mid, ACT.Exp, scale=-1.0)
                    s.activation(e_b, b, ACT.Exp)
                    s.activation(dec, ch(b)[:, :, last], ACT.Exp)
                    s.activation(e_last, e_last, ACT.Exp).then_inc(self.act_done.sem, 1)
                    act.wait_ge(self.act_done.sem, self.act_done.up())
                    s.activation(e_mid, e_mid, ACT.Exp)
            with self.block() as block:
                @block.vector
                def _(dve):
                    v.tensor_tensor(e_mid, e_mid, q, ALU.mult)
                    v.tensor_tensor(e_inv, e_inv, k[d], ALU.mult)
                    v.tensor_tensor(e_last, e_last, k[d], ALU.mult)
                    v.tensor_tensor(e_b, e_b, q, ALU.mult)
                    v.memset(att, 0.0)
            with self.block() as block:
                @block.tensor
                def _(pe):
                    for j in range(TA // P):
                        c = slice(j * P, (j + 1) * P)
                        nc.tensor.matmul(ps[:, 0, c], e_inv[:, c], e_mid[:, c], start=True, stop=True)
                    for j in range(TA // P):
                        c = slice(j * P, (j + 1) * P)
                        nc.tensor.transpose(ps[:, 1, c], e_last[:, c], self.ident)
            with self.block() as block:
                @block.vector
                def _(dve):
                    for j in range(TA // P):
                        c = slice(j * P, (j + 1) * P)
                        v.copy_predicated(att[:, c], masks[d].bitcast(U32), ps[:, 0, c])

                @block.scalar
                def _(act):
                    s.activation(ktok, ps[:, 1, :], ACT.Copy)
            order = list(range(NC)) if d == 0 else list(range(NC // 2 - 1, -1, -1)) + list(range(NC - 1, NC // 2 - 1, -1))
            rows = lambda c: slice(c * HCHUNK % P, c * HCHUNK % P + HCHUNK)
            upd = lambda c: ps[:, 2 + c % 4, c // 4 * P:(c // 4 + 1) * P]
            with self.block() as block:
                @block.tensor
                def _(pe):
                    for c in order[:-1]:
                        r, j = rows(c), c * HCHUNK // P
                        nc.tensor.matmul(upd(c), ktok[r, j * P:(j + 1) * P],
                                         value[r, j, h * P:(h + 1) * P], start=True, stop=True)
            with self.block() as block:
                @block.vector
                def _(dve):
                    v.tensor_copy(state[:, order[0], :], upd(order[0])).then_inc(self.dve_done.sem, 1)
                    for n in range(1, NC - 1):
                        dve.wait_ge(self.dve_done.sem, self.dve_done.up())
                        v.scalar_tensor_tensor(state[:, order[n], :], state[:, order[n - 1], :],
                                               dec[:, order[n]:order[n] + 1], upd(order[n]), ALU.mult, ALU.add
                                               ).then_inc(self.dve_done.sem, 1)
            self.dve_done.up()
            with self.block() as block:
                @block.tensor
                def _(pe):
                    for j in range(TA // P):
                        c = slice(j * P, (j + 1) * P)
                        nc.tensor.matmul(ps[:, 6, c], value[:, j, h * P:(h + 1) * P], att[:, c],
                                         start=(d == 0 and j == 0), stop=False, skip_group_check=True)
                    for n, c in enumerate(order[1:]):
                        t = slice(c * HCHUNK, (c + 1) * HCHUNK)
                        nc.tensor.matmul(ps[:, 6, t], state[:, order[n], :], e_b[:, t], start=False,
                                         stop=(d == 1 and n == NC - 2), skip_group_check=True)
        with self.block() as block:
            @block.scalar
            def _(act):
                s.activation(out, ps[:, 6, :], ACT.Copy)

    def mlstm(self, c, qk, v_tok, out):
        nc, ps, A = self.nc, self.ps, self.arena
        v, s = nc.vector, nc.scalar
        mark = A.at
        W = 64
        rows = [A.take(TA)[0:W, :] for _ in range(5)]
        ig, lf, F, m, tmp = rows
        unit = A.take(TA)
        with self.block() as block:
            @block.tensor
            def _(pe):
                for g in range(2):
                    for k in range(KT):
                        nc.tensor.matmul(ps[0:W, g, :], c["gates"][:, k, g * W:(g + 1) * W], self.hT[:, k, :],
                                         start=(k == 0), stop=(k == KT - 1))
        gb = c["gate_b"]
        with self.block() as block:
            @block.vector
            def _(dve):
                v.tensor_scalar(ig, ps[0:W, 0, :], gb[0:W, 0:1], None, ALU.add).then_inc(self.dve_done.sem, 1)
                dve.wait_ge(self.dve_done.sem, self.dve_done.up())
                v.tensor_scalar(lf, ps[0:W, 1, :], gb[0:W, 1:2], None, ALU.add).then_inc(self.dve_done.sem, 1)
                dve.wait_ge(self.dve_done.sem, self.dve_done.up())
                v.tensor_scalar(tmp, lf, -1.0, None, ALU.mult).then_inc(self.dve_done.sem, 1)
                dve.wait_ge(self.dve_done.sem, self.dve_done.up())
                v.tensor_tensor(tmp, tmp, lf, ALU.max).then_inc(self.dve_done.sem, 1)
                dve.wait_ge(self.dve_done.sem, self.dve_done.up())
                v.memset(unit, 1.0)
        with self.block() as block:
            @block.scalar
            def _(act):
                s.activation(tmp, tmp, ACT.Exp, scale=-1.0).then_inc(self.act_done.sem, 1)
                act.wait_ge(self.act_done.sem, self.act_done.up())
                s.activation(tmp, tmp, ACT.Ln, bias=1.0)
        fw, bw = slice(0, 32), slice(32, 64)
        back, back_lat = slice(TC - 1, None, -1), slice(TA - 1, TC - 1, -1)
        done = self.dve_done
        with self.block() as block:
            @block.vector
            def _(dve):
                v.scalar_tensor_tensor(lf, lf, 0.0, tmp, ALU.min, ALU.subtract).then_inc(done.sem, 1)
                dve.wait_ge(done.sem, done.up())
                v.tensor_tensor_scan(F[fw], unit[fw], lf[fw], 0.0, ALU.mult, ALU.add)
                v.tensor_tensor_scan(m[fw], lf[fw], ig[fw], 0.0, ALU.add, ALU.max)
                v.tensor_tensor_scan(F[bw, back], unit[bw, back], lf[bw, back], 0.0, ALU.mult, ALU.add)
                v.tensor_tensor_scan(m[bw, back], lf[bw, back], ig[bw, back], 0.0, ALU.add, ALU.max
                                     ).then_inc(done.sem, 1)
                dve.wait_ge(done.sem, done.up())
                v.tensor_tensor_scan(F[bw, back_lat], unit[bw, back_lat], lf[bw, back_lat], F[bw, 0:1],
                                     ALU.mult, ALU.add)
                v.tensor_tensor_scan(m[bw, back_lat], lf[bw, back_lat], ig[bw, back_lat], m[bw, 0:1],
                                     ALU.add, ALU.max).then_inc(done.sem, 1)
                dve.wait_ge(done.sem, done.up())
                v.tensor_tensor(tmp, F, m, ALU.subtract)
                v.tensor_tensor(ig, ig, F, ALU.subtract).then_inc(done.sem, 1)
                dve.wait_ge(done.sem, done.up())
                v.tensor_scalar(m, m, -1.0, None, ALU.mult)
        key = A.take(TA // P, W)
        pick = A.take(8, P)
        with self.block() as block:
            @block.tensor
            def _(pe):
                for j in range(TA // P):
                    nc.tensor.transpose(ps[:, 2, j * W:(j + 1) * W], ig[:, j * P:(j + 1) * P], self.ident[0:W, 0:W])

            @block.vector
            def _(dve):
                for d in range(2):
                    for h in range(HEADS):
                        r = 32 * d + h
                        v.tensor_copy(pick[0:W, d * HEADS + h, :], self.ident[0:W, r:r + 1].broadcast_to([W, P]))
        with self.block() as block:
            @block.vector
            def _(dve):
                v.tensor_copy(flat(key), ps[:, 2, 0:TA // P * W])
        weight = A.take(TA // P, TA)
        floor, den, num = A.take(TA), A.take(TA), A.take(TA)
        NT, LT = TA // P, TC // P
        for h in range(HEADS):
            for d in range(2):
                if d == 0:
                    seen = [(j, j * P, TA) for j in range(NT)]
                else:
                    seen = [(j, 0, (j + 1) * P) for j in range(LT)] + [(j, TC, TA) for j in range(LT)]
                    seen += [(j, TC, (j + 1) * P) for j in range(LT, NT)]
                r, half = 32 * d + h, slice(h % 2 * 64, h % 2 * 64 + 64)
                with self.block() as block:
                    @block.tensor
                    def _(pe):
                        nc.tensor.matmul(ps[:, 0, :], pick[0:W, d * HEADS + h, :], tmp, start=True, stop=True)
                        nc.tensor.matmul(ps[:, 1, :], pick[0:W, d * HEADS + h, :], m, start=True, stop=True)
                        for j, t0, t1 in seen:
                            nc.tensor.matmul(ps[:, 2 + j, t0:t1], qk[half, 2 + h // 2, j * P:(j + 1) * P],
                                             qk[half, h // 2, t0:t1], start=True, stop=True)
                with self.block() as block:
                    @block.vector
                    def _(dve):
                        for j, t0, t1 in seen:
                            v.tensor_scalar(weight[:, j, t0:t1], ps[:, 0, t0:t1], key[:, j, r:r + 1], 0.0,
                                            ALU.add, ALU.min)

                    @block.scalar
                    def _(act):
                        s.activation(floor, ps[:, 1, :], ACT.Exp)
                with self.block() as block:
                    @block.scalar
                    def _(act):
                        for j, t0, t1 in seen:
                            s.activation(weight[:, j, t0:t1], weight[:, j, t0:t1], ACT.Exp)
                with self.block() as block:
                    @block.vector
                    def _(dve):
                        for j in range(NT):
                            diag = weight[:, j, j * P:(j + 1) * P]
                            ins = v.tensor_tensor(diag, diag, c["tri"][d], ALU.mult)
                        ins.then_inc(self.dve_done.sem, 1)
                        dve.wait_ge(self.dve_done.sem, self.dve_done.up())
                        for j, t0, t1 in seen:
                            v.scalar_tensor_tensor(weight[:, j, t0:t1], ps[:, 2 + j, t0:t1], float(64) ** -0.5,
                                                   weight[:, j, t0:t1], ALU.mult, ALU.mult)
                with self.block() as block:
                    @block.tensor
                    def _(pe):
                        for bank, lhs in ((6, lambda j: v_tok[:, j, h * P:(h + 1) * P]), (7, lambda j: self.ones)):
                            for n, (j, t0, t1) in enumerate(seen):
                                nc.tensor.matmul(ps[:, bank, t0:t1], lhs(j), weight[:, j, t0:t1], start=(n == 0),
                                                 stop=(n == len(seen) - 1), skip_group_check=True)
                with self.block() as block:
                    @block.vector
                    def _(dve):
                        v.tensor_scalar(den, ps[:, 7, :], -1.0, None, ALU.mult).then_inc(done.sem, 1)
                        dve.wait_ge(done.sem, done.up())
                        v.tensor_tensor(den, den, ps[:, 7, :], ALU.max).then_inc(done.sem, 1)
                        dve.wait_ge(done.sem, done.up())
                        v.tensor_tensor(den, den, floor, ALU.max).then_inc(done.sem, 1)
                        dve.wait_ge(done.sem, done.up())
                        v.reciprocal(den, den).then_inc(done.sem, 1)
                        dve.wait_ge(done.sem, done.up())
                        if d == 0:
                            v.tensor_tensor(out(h), ps[:, 6, :], den, ALU.mult)
                        else:
                            v.tensor_tensor(num, ps[:, 6, :], den, ALU.mult).then_inc(done.sem, 1)
                            dve.wait_ge(done.sem, done.up())
                            v.tensor_tensor(out(h), out(h), num, ALU.add)
        A.at = mark

    def recurrent(self, c, gains, mods):
        nc, ps, A = self.nc, self.ps, self.arena
        v, s = nc.vector, nc.scalar
        mark = A.at
        everything = slice(0, TA)
        o = A.take(2 * HEADS, TA)
        vt = A.take(TA // P, 2 * HEADS * P)
        proj = A.take(24, TA)
        self.linear(24, KT, self.hT, everything, lambda m: flat(proj)[:, bass.ds(m * TA, TA)])
        self.linear_tokens(2 * HEADS, KT, self.hT, range(TA // P), lambda m: vt[:, :, m * P:(m + 1) * P])
        q, gate_a, z, gate_b = proj[:, 0:4, :], proj[:, 4:8, :], proj[:, 8:16, :], proj[:, 20:24, :]
        qk = proj[:, 16:20, :]
        inner = A.at
        conv = A.take(4, TA)
        w = c["conv"]
        with self.block() as block:
            @block.vector
            def _(dve):
                for tap in (1, 0, 2):
                    for j in range(4):
                        for c0 in (0, TC):
                            a, b = c0 + (tap == 0), c0 + TC - (tap == 2)
                            src = qk[:, j, a + tap - 1:b + tap - 1]
                            if tap == 1:
                                ins = v.tensor_scalar(conv[:, j, a:b], src, w[:, j, 1:2], None, ALU.mult)
                            else:
                                ins = v.scalar_tensor_tensor(conv[:, j, a:b], src, w[:, j, tap:tap + 1],
                                                             conv[:, j, a:b], ALU.mult, ALU.add)
                    ins.then_inc(self.dve_done.sem, 1)
                    dve.wait_ge(self.dve_done.sem, self.dve_done.up())
        with self.block() as block:
            @block.scalar
            def _(act):
                s.activation(qk, conv, ACT.Silu)
                s.activation(gate_a, gate_a, ACT.Silu)
                s.activation(gate_b, gate_b, ACT.Sigmoid)
        A.at = inner
        self.mlstm(c, qk, vt[:, :, HEADS * P:], lambda h: o[:, HEADS + h, :])
        lb, rest = c["lb_c"], c["rest"]
        raw = c["lb"]
        wide = lambda x: x.unsqueeze(2).broadcast_to([P, 8, 3])
        with self.block() as block:
            @block.vector
            def _(dve):
                v.tensor_reduce(lb, raw, AX_X, ALU.max).then_inc(self.dve_done.sem, 1)
                dve.wait_ge(self.dve_done.sem, self.dve_done.up())
                v.tensor_tensor(raw, raw, wide(lb), ALU.subtract)
        with self.block() as block:
            @block.scalar
            def _(act):
                s.activation(raw, raw, ACT.Exp)
        with self.block() as block:
            @block.vector
            def _(dve):
                v.tensor_reduce(rest, raw, AX_X, ALU.add).then_inc(self.dve_done.sem, 1)
                dve.wait_ge(self.dve_done.sem, self.dve_done.up())
                v.reciprocal(rest, rest).then_inc(self.dve_done.sem, 1)
                dve.wait_ge(self.dve_done.sem, self.dve_done.up())
                v.tensor_tensor(lb, raw[:, :, 0], rest, ALU.mult).then_inc(self.dve_done.sem, 1)
                dve.wait_ge(self.dve_done.sem, self.dve_done.up())
                v.tensor_scalar(rest, lb, -1.0, 1.0, ALU.mult, ALU.add)
        logf = self.hT
        with self.block() as block:
            @block.scalar
            def _(act):
                s.activation(logf, z, ACT.Sigmoid)
                s.activation(conv[:, 0, 0:1], self.ones[:, 0:1], ACT.Copy).then_inc(self.act_done.sem, 1)
                act.wait_ge(self.act_done.sem, self.act_done.up())
                s.activation(z, z, ACT.Sigmoid, scale=-1.0)
        with self.block() as block:
            @block.vector
            def _(dve):
                for j in range(8):
                    v.tensor_scalar(logf[:, j, :], logf[:, j, :], rest[:, j:j + 1], lb[:, j:j + 1], ALU.mult, ALU.add)
                    v.tensor_scalar(z[:, j, :], z[:, j, :], rest[:, j:j + 1], None, ALU.mult)
        with self.block() as block:
            @block.scalar
            def _(act):
                s.activation(logf, logf, ACT.Ln)
        resets = [A.take(TA) for _ in range(2)]
        for d, edge in ((0, 0), (1, HCHUNK - 1)):
            with self.block() as block:
                @block.vector
                def _(dve):
                    v.memset(resets[d], 1.0).then_inc(self.dve_done.sem, 1)
                    dve.wait_ge(self.dve_done.sem, self.dve_done.up())
                    v.memset(resets[d].rearrange("p (c t) -> p c t", t=HCHUNK)[:, :, edge], 0.0)
        tmp = [A.take(TA) for _ in range(5)] + [A.take(TA // HCHUNK), A.take(TA), A.take(TA),
                                                A.take(TA // HCHUNK, P)]
        for h in range(HEADS):
            self.hgrn_head(h, q[:, h, :], [z[:, d * HEADS + h, :] for d in range(2)],
                           [logf[:, d * HEADS + h, :] for d in range(2)], vt, resets, c["chunk_mask"],
                           o[:, h, :], tmp)
        A.at = inner
        for j, gate in ((0, gate_a), (HEADS, gate_b)):
            root = A.take(HEADS * TA)
            part = o[:, j:j + HEADS, :]
            self.scaled_root(flat(part), HEADS * TA, 1.0 / P, root)
            rt = root.rearrange("p (h t) -> p h t", h=HEADS)
            with self.block() as block:
                @block.vector
                def _(dve):
                    for h in range(HEADS):
                        ins = v.scalar_tensor_tensor(part[:, h, :], part[:, h, :], c["out_g"][:, j + h:j + h + 1],
                                                     rt[:, h, :], ALU.mult, ALU.mult)
                    ins.then_inc(self.dve_done.sem, 1)
                    dve.wait_ge(self.dve_done.sem, self.dve_done.up())
                    v.tensor_tensor(part, part, gate, ALU.mult)
            A.at = inner
        self.linear(KT, KT, o, everything, lambda m: self.hT[:, m, :])
        A.at = mark
        self.add_normed(self.hT, [(slice(0, TC), mods[2][1]), (LAT, mods[2][0])], gains[1])

    def grouped_attention(self, c, gains, mods):
        nc, ps, A = self.nc, self.ps, self.arena
        v = nc.vector
        mark = A.at
        q, k, vt, o = A.take(GQ_H, T), A.take(GQ_KV, TA), A.take(TA // P, GQ_KV * P), A.take(GQ_H, T)
        self.linear(GQ_H, KT, self.hT, LAT, lambda m: q[:, m, :])
        self.linear(GQ_KV, KT, self.hT, slice(0, TA), lambda m: k[:, m, :])
        self.linear_tokens(GQ_KV, KT, self.hT, range(TA // P), lambda m: vt[:, :, m * P:(m + 1) * P])
        inner = A.at
        for x, n, j in ((q, GQ_H * T, 0), (k, GQ_KV * TA, 1)):
            root = A.take(n)
            self.scaled_root(flat(x), n, 1.0 / P, root)
            with self.block() as block:
                @block.vector
                def _(dve):
                    v.scalar_tensor_tensor(flat(x), flat(x), c["qk_g"][:, j:j + 1], root,
                                           ALU.mult, ALU.mult)
            A.at = inner
        cos, sin = c["axial"][:, 0, :], c["axial"][:, 1, :]
        self.rope(q, c["rot"], cos, sin)
        self.rope(k[:, :, LAT], c["rot"], cos, sin)

        def scores(h, qt, dst):
            return nc.tensor.matmul(dst, q[:, h, qt * P:(qt + 1) * P], k[:, h * GQ_KV // GQ_H, :],
                                    start=True, stop=True)

        def value(h, kt):
            g = h * GQ_KV // GQ_H
            return vt[:, kt, g * P:(g + 1) * P]
        self.attention(GQ_H, TA, float(P) ** -0.5, scores, value, lambda h: o[:, h, :], False)
        y = A.take(KT, T)
        self.linear(KT, KT, o, slice(0, T), lambda m: y[:, m, :])
        self.add_normed(y, [(LAT, mods[2][0])], gains[1])
        A.at = mark


ORDER = ["mod_0", "hy_in", "hy_out", "peer_q_0", "experts_0",
         "mod_1", "mla_in", "mla_uq", "mla_ukv", "mla_out", "peer_q_1", "experts_1",
         "ada_0", "ab_in", "ab_out", "ffn_in_0", "ffn_out_0",
         "ada_1", "gq_in", "gq_out", "ffn_in_1", "ffn_out_1"]


def program(nc, dram, stop=None):
    with ExitStack() as ctx:
        core = Core(nc, ctx, dram, ORDER)
        s = core.small
        core.constants()
        core.small_cols = s.take(KT)
        core.selT = s.take(3, T)
        xL = core.xT[:, :, LAT]
        cond = s.take(KT, 3)
        mod = s.take(6 * KT, 2)
        bias = s.take(6 * KT)
        gains = s.take(KT, 5)
        core.load([(xL, dram["xT"]), (cond, dram["cond"]), (gains, dram["gains"]), (bias, dram["mod_b_0"])])
        with core.block() as block:
            @block.scalar
            def _(act):
                nc.scalar.activation(cond, cond, ACT.Silu)
        first_layer_mark = s.at

        c = {"gates": s.take(KT, 8), "conv": s.take(12, 4), "a_log": s.take(HEADS), "dt_bias": s.take(HEADS),
             "decay": s.take(HEADS), "o_norm": s.take(1), "rot": s.take(P), "cos": s.take(T), "sin": s.take(T)}
        pos_i, pos = s.take(T, dt=I32), s.take(T)
        freq = s.take(2)
        core.load([(c["gates"], dram["hy_gates"]), (c["conv"], dram["conv"]), (c["a_log"], dram["a_log"]),
                   (c["dt_bias"], dram["dt_bias"]), (c["o_norm"], dram["o_norm"]), (pos_i, dram["positions"]),
                   (freq, dram["freq"])])
        with core.block() as block:
            @block.vector
            def _(dve):
                nc.vector.tensor_copy(pos, pos_i)
        core.rotation(c["rot"], 64)
        core.rope_tables(pos, freq[:, 0:1], c["cos"], c["sin"])
        m = [mod[:, i * KT:(i + 1) * KT, 0] for i in range(6)]
        core.modulation(mod[:, :, 0:1], cond[:, :, 0:1], 1, bias)
        core.modulated(LAT, gains[:, :, 0], m[1], m[0])
        c["g1"] = m[2]
        core.hybrid(c)
        if stop == 1:
            return finish(core, dram)
        core.modulated(LAT, gains[:, :, 2], m[4], m[3])
        core.peer_routes(dram["subkeys_0"])
        core.peer_experts(m[5])
        if stop == 2:
            return finish(core, dram)

        s.at = first_layer_mark
        c = {"norms": s.take(6), "rot": s.take(P), "cos": s.take(T), "sin": s.take(T)}
        pos_i, pos = s.take(T, dt=I32), s.take(T)
        freq = s.take(2)
        core.load([(c["norms"], dram["mla_norms"]), (pos_i, dram["positions"]), (freq, dram["freq"]),
                   (bias, dram["mod_b_1"])])
        with core.block() as block:
            @block.vector
            def _(dve):
                nc.vector.tensor_copy(pos, pos_i)
        core.rotation(c["rot"], 32)
        core.rope_tables(pos, freq[:, 1:2], c["cos"], c["sin"])
        core.modulation(mod[:, :, 0:1], cond[:, :, 0:1], 1, bias)
        core.modulated(LAT, gains[:, :, 1], m[1], m[0])
        c["g1"] = m[2]
        core.latent_attention(c)
        if stop == 3:
            return finish(core, dram)
        core.modulated(LAT, gains[:, :, 3], m[4], m[3])
        core.peer_routes(dram["subkeys_1"])
        core.peer_experts(m[5])
        if stop == 4:
            return finish(core, dram)
        root = core.arena.take(T)
        core.norm_rows(xL, slice(0, T), core.hT[:, :, LAT], root)
        with core.block() as block:
            @block.vector
            def _(dve):
                for k in range(KT):
                    nc.vector.scalar_tensor_tensor(xL[:, k, :], xL[:, k, :], gains[:, k, 4:5], root,
                                                   ALU.mult, ALU.mult)
        core.arena.at = 0
        if stop == 5:
            return finish(core, dram)

        s.at = first_layer_mark
        c = {"gates": s.take(KT, P), "gate_b": s.take(2), "conv": s.take(4, 3), "lb": s.take(8, 3), "lb_c": s.take(8),
             "rest": s.take(8), "out_g": s.take(8)}
        norm_g = s.take(KT, 8)
        core.load([(core.xT[:, :, 0:TC], dram["ctxT"]), (c["gates"], dram["ab_gates"]),
                   (c["gate_b"][0:64, :], dram["gate_b"]), (c["conv"], dram["ab_conv"]), (c["lb"], dram["lb"]),
                   (c["out_g"], dram["ab_out_g"]), (norm_g, dram["norm_g"]), (bias, dram["ada_b_0"])])
        core.modulation(mod, cond[:, :, 1:3], 2, bias)
        mods = [[mod[:, i * KT:(i + 1) * KT, j] for j in range(2)] for i in range(6)]
        CTX = slice(0, TC)
        gain = [norm_g[:, :, i] for i in range(4)]
        for cols, j in ((CTX, 1), (LAT, 0)):
            core.modulated(cols, gain[0], mods[1][j], mods[0][j])
        c["tri"] = [core.selT[:, 0, 0:P], core.selT[:, 0, P:]]
        c["chunk_mask"] = [core.selT[:, 1, 0:P], core.selT[:, 1, P:]]
        orders = [(0, -1, [[1, P]]), (0, 1, [[-1, P]])]
        n = P // HCHUNK
        for d in range(2):
            core.mask(c["tri"][d], [orders[d]])
            core.mask(c["chunk_mask"][d], [(0, 1, [[-HCHUNK, n], [0, HCHUNK]]),
                                           (HCHUNK - 1, -1, [[HCHUNK, n], [0, HCHUNK]]), orders[d]])
        core.recurrent(c, gain, mods)
        if stop == 6:
            return finish(core, dram)
        core.swiglu([(CTX, mods[3][1], mods[4][1], mods[5][1]), (LAT, mods[3][0], mods[4][0], mods[5][0])],
                    gain[2], gain[3])
        if stop == 7:
            return finish(core, dram)

        s.at = first_layer_mark + 1500
        c = {"qk_g": s.take(2), "rot": s.take(P), "axial": s.take(2, T)}
        core.load([(c["qk_g"], dram["qk_g"]), (c["axial"], dram["axial"]), (bias, dram["ada_b_1"])])
        core.rotation(c["rot"], 32)
        core.modulation(mod, cond[:, :, 1:3], 2, bias)
        gain = [norm_g[:, :, 4 + i] for i in range(4)]
        for cols, j in ((CTX, 1), (LAT, 0)):
            core.modulated(cols, gain[0], mods[1][j], mods[0][j])
        core.grouped_attention(c, gain, mods)
        core.swiglu([(LAT, mods[3][0], mods[4][0], mods[5][0])], gain[2], gain[3])
        finish(core, dram)


def finish(core, dram):
    nc = core.nc
    with core.block() as block:
        @block.sync
        def _(sp):
            sp.dma_start(dram["out"], core.xT[:, :, LAT]).then_inc(core.stored.sem, 16)
            sp.wait_ge(core.stored.sem, 16)


def tiles(w):
    k, n = w.shape
    w = w.reshape(k // P, P, n // P, P).transpose(2, 0, 1, 3)
    w = w.reshape(-1, TPU, P, P).transpose(0, 2, 1, 3)
    return np.ascontiguousarray(w).reshape(-1, P, UNIT)


def columns(v):
    v = v.reshape(v.shape[:-1] + (-1, P))
    return np.ascontiguousarray(np.moveaxis(np.moveaxis(v, -1, 0), -1, 1))


def rows(v):
    return np.ascontiguousarray(np.broadcast_to(v, (P,) + v.shape))


def experts(u, v):
    u = u.reshape(KEYS, KEYS, KT, P).transpose(1, 3, 2, 0).reshape(KEYS, P, UNIT)
    v = v.reshape(KEYS, KEYS, UNIT).transpose(1, 0, 2)
    out = np.empty((2 * KEYS, P, UNIT), u.dtype)
    out[0] = u[0]
    out[1:-1:2] = u[1:]
    out[2:-1:2] = v[:-1]
    out[-1] = v[-1]
    return out


def layout(i):
    c = np.concatenate
    a = {}
    a["xT"] = np.ascontiguousarray(i["x"][0].T.reshape(KT, P, T).transpose(1, 0, 2))
    a["cond"] = np.stack([columns(i["c"][0]), columns(i["c_2"][0]), columns(i["c_ctx_2"])], -1)
    a["gains"] = np.stack([columns(v) for v in (i["norm_mix"][0], i["norm_mix"][1], i["norm_ffn"][0],
                                                i["norm_ffn"][1], i["final_norm"])], -1)
    for l in range(2):
        a[f"mod_{l}"], a[f"mod_b_{l}"] = tiles(i["mod_w"][l]), columns(i["mod_b"][l])
        a[f"ada_{l}"], a[f"ada_b_{l}"] = tiles(i["ada_w_2"][l]), columns(i["ada_b_2"][l])
        a[f"peer_q_{l}"] = tiles(i["peer_w_q"][l])
        a[f"subkeys_{l}"] = np.ascontiguousarray(i["peer_sub_keys"][l].reshape(2 * PH, KEYS, P).transpose(2, 0, 1))
        a[f"experts_{l}"] = experts(i["peer_u"][l], i["peer_v"][l])
        f = i["ffn_w_in_2"][l].reshape(D, 2, FT, P).transpose(0, 2, 1, 3).reshape(D, 2 * FF)
        a[f"ffn_in_{l}"], a[f"ffn_out_{l}"] = tiles(f), tiles(i["ffn_w_out_2"][l])
    w = i["hy_w_in"][0]
    a["hy_in"] = tiles(c([w[:, 0:2048], w[:, 2056:3592]], 1))
    a["hy_gates"] = np.ascontiguousarray(w[:, 2048:2056].reshape(KT, P, 8).transpose(1, 0, 2))
    a["hy_out"] = tiles(i["hy_w_out"][0])
    a["conv"] = np.ascontiguousarray(i["gdn_conv"][0].reshape(4, 12, P).transpose(2, 1, 0))
    a["a_log"], a["dt_bias"] = rows(i["gdn_a_log"][0]), rows(i["gdn_dt_bias"][0])
    a["o_norm"] = np.ascontiguousarray(i["gdn_o_norm"][0].reshape(P, 1))
    a["positions"] = rows(i["positions"][0])
    f = [10000.0 ** (-(np.arange(P) % h) * 2 / (2 * h)) for h in (64, 32)]
    a["freq"] = np.stack(f, -1).astype(np.float32)
    w = i["mla_w_in"][0]
    a["mla_in"] = tiles(c([w, w[:, 768:832]], 1))
    w = i["mla_w_uq"][0].reshape(512, MLA_H, 192)
    a["mla_uq"] = tiles(c([w[:, :, 0:128].reshape(512, -1), w[:, :, 128:].reshape(512, -1)], 1))
    w = i["mla_w_ukv"][0].reshape(256, MLA_H, 256)
    a["mla_ukv"] = tiles(c([w[:, :, 0:128].reshape(256, -1), w[:, :, 128:].reshape(256, -1)], 1))
    a["mla_out"] = tiles(i["mla_w_out"][0])
    a["mla_norms"] = c([columns(i["mla_q_norm"][0]), columns(i["mla_kv_norm"][0])], 1)
    a["ctxT"] = np.ascontiguousarray(i["ctx_2"][0].T.reshape(KT, P, TC).transpose(1, 0, 2))
    a["norm_g"] = columns(i["norm_g_2"]).reshape(P, KT, 8)
    w = i["ab_w_in_2"][0]
    at = np.cumsum([0, 512, 512, 512, 512, 512, 512, 512, 512])
    cut = lambda n: w[:, at[n]:at[n + 1]]
    a["ab_in"] = tiles(c([cut(0), cut(2), cut(3), cut(4), cut(5), cut(7), cut(1), cut(6)], 1))
    g = w[:, 4096:4112].reshape(KT, P, 2, 2, 4).transpose(1, 0, 3, 2, 4)
    a["ab_gates"] = np.zeros((P, KT, 2, 2, 32), np.float32)
    a["ab_gates"][..., 0:4] = g
    a["ab_gates"] = a["ab_gates"].reshape(P, KT, P)
    a["gate_b"] = np.zeros((2, 32, 2), np.float32)
    a["gate_b"][:, 0:4, :] = i["ab_gate_b_2"][0].reshape(2, 2, 4).transpose(0, 2, 1)
    a["gate_b"] = a["gate_b"].reshape(64, 2)
    a["ab_conv"] = np.ascontiguousarray(i["ab_conv_2"][0].reshape(3, 4, P).transpose(2, 1, 0))
    a["lb"] = np.ascontiguousarray(i["hgrn_lb_2"].reshape(2, 3, 4, P).transpose(3, 0, 2, 1)).reshape(P, 8, 3)
    a["ab_out_g"] = columns(i["ab_out_g_2"][0])
    a["ab_out"] = tiles(i["ab_w_out_2"][0])
    a["gq_in"] = tiles(i["attn_w_qkv_2"][0])
    a["qk_g"] = np.ascontiguousarray(i["attn_qk_g_2"][0].T)
    a["gq_out"] = tiles(i["attn_w_out_2"][0])
    inv = np.power(np.float32(10000.0), -np.arange(0, 64, 2, dtype=np.float32) / 64)
    t = np.arange(T)
    ang = np.stack([(t // 64).astype(np.float32)[:, None] * inv, (t % 64).astype(np.float32)[:, None] * inv], 1)
    ang = np.stack([ang, ang], 2).reshape(T, P).T
    a["axial"] = np.ascontiguousarray(np.stack([np.cos(ang), np.sin(ang)], 1).astype(np.float32))
    return a


def kernel(**inputs):
    import concourse.bacc as bacc
    from concourse.bass_utils import run_bass_kernel_spmd

    nc = bacc.Bacc("TRN2", target_bir_lowering=False, num_devices=1)
    arrays = layout({k: np.asarray(v) for k, v in inputs.items()})
    dram = {n: nc.dram_tensor(f"in_{n}", a.shape, mybir.dt.from_np(a.dtype), kind="ExternalInput").ap()
            for n, a in arrays.items()}
    dram["out"] = nc.dram_tensor("out", (P, KT, T), F32, kind="ExternalOutput").ap()
    program(nc, dram)
    r = run_bass_kernel_spmd(nc, [{f"in_{n}": a for n, a in arrays.items()}], core_ids=[0])
    out = r.results[0]["out"]
    return np.ascontiguousarray(out.transpose(2, 1, 0)).reshape(1, T, D)
```

```python
from contextlib import ExitStack

import numpy as np

import concourse.bass as bass
from concourse import mybir

F32 = mybir.dt.float32
F32R = mybir.dt.float32r
U32 = mybir.dt.uint32
I32 = mybir.dt.int32
ALU = mybir.AluOpType
ACT = mybir.ActivationFunctionType
AX_X = mybir.AxisListType.X

P = 128
D = 1024
KT = D // P
T = 256
TC = 256
TA = T + TC
TT = T // P
LAT = slice(TC, TA)
EPS = 1e-6
RING = 4
MSPLITS = 4
SPLITS = 3
UNIT = 1024
TPU = UNIT // P
BANKS = 4
HEADS = 4
CHUNK = 64
HCHUNK = 32
KEYS = 128
PH = 8
TOPK = 16
FF = 2816
FT = FF // P
MLA_H = 8
GQ_H, GQ_KV = 8, 2
TWO_PI = 2.0 * np.pi
PI_A = 6.28125
PI_B = float(np.float32(TWO_PI - PI_A) // 2.0 ** -20 * 2.0 ** -20)
PI_C = float(TWO_PI - PI_A - PI_B)
PI_MAX = 3.1415925
ROUND = 1.5 * 2.0 ** 23
NEG = -1e30
LOWEST = -3e38


class Signal:

    def __init__(self, nc, ctx, name):
        self.sem = ctx.enter_context(nc.semaphore(name))
        self.n = 0

    def up(self, by=1):
        self.n += by
        return self.n


class Space:

    def __init__(self, tensor, size):
        self.tensor, self.size, self.at = tensor, size, 0

    def take(self, *shape, dt=None):
        n = int(np.prod(shape))
        assert self.at + n <= self.size, (self.at, n, self.size)
        ap = self.tensor[:, self.at:self.at + n]
        self.at += n
        if dt is not None:
            ap = ap.bitcast(dt)
        if len(shape) == 2:
            ap = ap.rearrange("p (a b) -> p a b", a=shape[0])
        elif len(shape) == 3:
            ap = ap.rearrange("p (a b c) -> p a b c", a=shape[0], b=shape[1])
        return ap


def flat(ap):
    return ap.rearrange("p a b -> p (a b)")


class Core:
    def __init__(self, nc, ctx, dram, order):
        self.nc, self.dram = nc, dram
        sb = lambda name, n: ctx.enter_context(nc.sbuf_tensor(name, [P, n], F32))
        self.ring = sb("ring", RING * UNIT)
        self.small = Space(sb("small", 1440), 1440)
        self.xT = sb("x_sb", KT * TA)[:, :].rearrange("p (k t) -> p k t", k=KT)
        self.hsplit = ctx.enter_context(nc.sbuf_tensor("h_split", [P, 2, KT, T], F32R))
        self.cond_split = ctx.enter_context(nc.sbuf_tensor("cond_split", [P, KT, 6], F32R))
        self.ps = ctx.enter_context(nc.psum_tensor("ps", [P, 8, 512], F32))
        sig = lambda name: Signal(nc, ctx, name)
        self.arrived = [sig(f"slot{i}_arrived") for i in range(RING)]
        self.unit_used = sig("unit_used")
        self.tile_done = sig("tile_done")
        self.bank_free = sig("bank_free")
        self.pair_free = [sig("even_bank_free"), sig("odd_bank_free")]
        self.loaded = sig("small_loaded")
        self.stored = sig("stored")
        self.dve_done, self.act_done, self.pool_done = sig("dve_done"), sig("act_done"), sig("pool_done")
        self.a, self.b, self.c, self.d, self.e, self.f, self.g = (sig(f"handover_{x}") for x in "abcdefg")
        self.order = [(name, i) for name in order for i in range(dram[name].shape[0])]
        self.n_loaded = self.n_used = 0

    def open_work(self, name, arena, slots):
        self.work = ExitStack()
        sb = lambda what, n: self.work.enter_context(self.nc.sbuf_tensor(f"{what}_{name}", [P, n], F32))
        self.arena = Space(sb("arena", arena), arena)
        self.extra = Space(sb("extra", 1696), 1696)
        self.hT = sb("h", KT * TA)[:, :].rearrange("p (k t) -> p k t", k=KT)

        if slots:
            self.split = self.work.enter_context(self.nc.sbuf_tensor(f"projection_split_{name}", [P, slots, 2, UNIT], F32R))

    def close_work(self):
        self.work.close()

    def block(self):
        return self.nc.Block(no_gpsimd_drain=True)

    def slot(self, u):
        s = u % RING
        return self.ring[:, s * UNIT:(s + 1) * UNIT]

    def stream(self, sp, n_units):
        end = min(self.n_used + n_units + RING, len(self.order))
        u = self.n_loaded
        while u < end:
            name, i0 = self.order[u]
            run = 1
            while u + run < end and self.order[u + run][0] == name:
                run += 1
            loops = run // RING
            if u >= RING and loops >= 2:
                with sp.Fori(0, loops) as i:
                    for s in range(RING):
                        sp.wait_ge(self.unit_used.sem, i * RING + (u + s + 1 - RING))
                        sp.dma_start(self.slot(u + s),
                                     self.dram[name][bass.ds(i * RING + (i0 + s), 1)].rearrange("o p c -> p (o c)")
                                     ).then_inc(self.arrived[(u + s) % RING].sem, 16)
                u += loops * RING
            else:
                for s in range(min(run, RING)):
                    if u >= RING:
                        sp.wait_ge(self.unit_used.sem, u + 1 - RING)
                    sp.dma_start(self.slot(u), self.dram[name][i0 + s]).then_inc(self.arrived[u % RING].sem, 16)
                    u += 1
        self.n_loaded = u

    def await_unit(self, eng, u, turns=0, per_turn=8):
        eng.wait_ge(self.arrived[u % RING].sem, turns * (16 * per_turn // RING) + 16 * (u // RING + 1))

    def project(self, n_m, kt, tile, takes, out_of="scalar"):
        units = n_m * kt // TPU
        assert n_m * kt % TPU == 0
        loops = n_m // 8 if kt == TPU and n_m >= 16 else 0
        pair = out_of == "pair"
        u0, t0 = self.n_used, self.tile_done.n
        free = self.pair_free if pair else [self.bank_free] * 2
        f0 = [x.n for x in free]
        ends = [(s + 1) * kt % TPU == 0 for s in range(n_m)]
        inner = np.cumsum([0] + [not e for e in ends])

        def products(pe, s, i):
            if pair:
                pe.wait_ge(free[s % 2].sem, (i * 4 if i is not None else 0) + (f0[s % 2] + s // 2 + 1 - BANKS // 2))
            else:
                pe.wait_ge(free[0].sem, (i * 8 if i is not None else 0) + (f0[0] + s + 1 - BANKS))
            for k in range(kt):
                q = s * kt + k
                u = u0 + q // TPU
                if q % TPU == 0:
                    self.await_unit(pe, u, i if i is not None else 0)
                ins = tile(k, self.slot(u)[:, q % TPU * P:(q % TPU + 1) * P], s % BANKS, k == 0, k == kt - 1)
                if q % TPU == TPU - 1:
                    ins.then_inc(self.unit_used.sem, 1)
            if not ends[s]:
                ins.then_inc(self.tile_done.sem, 1)

        def take(eng, s, i):
            turn = i * 8 if i is not None else 0
            if ends[s]:
                eng.wait_ge(self.unit_used.sem, turn + (u0 + (s + 1) * kt // TPU))
            else:
                eng.wait_ge(self.tile_done.sem, t0 + int(inner[s + 1]))
            takes(eng, turn + s, s, i).then_inc(free[s % 2].sem, 1)

        def whole(eng, step, which=(0, 1)):
            if loops:
                with eng.Fori(0, loops) as i:
                    for s in range(8):
                        if s % 2 in which:
                            step(eng, s, i)
            for s in range(loops * 8, n_m):
                if s % 2 in which:
                    step(eng, s, None)

        with self.block() as block:
            @block.sync
            def _(sp):
                self.stream(sp, units)

            @block.tensor
            def _(pe):
                whole(pe, products)

            if out_of == "scalar":
                @block.scalar
                def _(act):
                    whole(act, take)
            elif out_of == "vector":
                @block.vector
                def _(dve):
                    whole(dve, take)
            else:
                @block.scalar
                def _(act):
                    whole(act, take, (0,))

                @block.vector
                def _(dve):
                    whole(dve, take, (1,))
        self.n_used += units
        self.tile_done.n += int(inner[-1])
        if pair:
            for x in free:
                x.n += n_m // 2
        else:
            self.bank_free.n += n_m

    def linear(self, n_m, kt, h, cols, out):
        nc = self.nc
        n = cols.stop - cols.start

        def tile(k, w, bank, first, last):
            return nc.tensor.matmul(self.ps[:, bank, 0:n], w, h[:, k, cols], start=first, stop=last)

        def takes(act, m, s, i):
            return nc.scalar.activation(out(m), self.ps[:, s % BANKS, 0:n], ACT.Copy)
        self.project(n_m, kt, tile, takes)

    def linear_tokens(self, n_m, kt, h, tiles, out):
        nc = self.nc
        assert TPU % kt == 0
        held = []

        def tile(k, w, bank, first, last):
            held.append(w)
            if not last:
                return None
            for j, t in enumerate(tiles):
                for kk in range(kt):
                    ins = nc.tensor.matmul(self.ps[:, bank, j * P:(j + 1) * P], h[:, kk, t * P:(t + 1) * P],
                                           held[kk], start=(kk == 0), stop=(kk == kt - 1))
            held.clear()
            return ins

        def takes(act, m, s, i):
            return nc.scalar.activation(out(m), self.ps[:, s % BANKS, 0:len(tiles) * P]
                                        .rearrange("p (a b) -> p a b", a=len(tiles)), ACT.Copy)
        self.project(n_m, kt, tile, takes)

    def project_parts(self, split, n_m, kt, moving, takes_act, takes_dve=None, then_dve=None):
        nc, ps = self.nc, self.ps
        units, slots = n_m * kt // TPU, split.shape[1]
        assert n_m * kt % TPU == 0
        turns = (units - 1) // 8 if kt == TPU and units > 16 else 0
        u0 = self.n_used
        n = moving(0, 0).shape[-1]
        pair = takes_dve is not None
        free = self.pair_free if pair else [self.bank_free] * 2
        f0 = [x.n for x in free]
        hi_done, mul_done = self.a, self.c
        hi0, mul0 = hi_done.n, mul_done.n + slots
        per = 2 if pair else 1

        def whole(eng, step):
            step(0, None)
            if turns:
                with eng.Fori(0, turns) as i:
                    for s in range(1, 9):
                        step(s, i)
            for s in range(turns * 8 + 1, units):
                step(s, None)
        at = lambda i, each: i * each if i is not None else 0

        def finished(s):
            return range((s * TPU) // kt, ((s + 1) * TPU) // kt) if s >= 0 else ()

        def take(eng, s, i, which, one):
            for m in finished(s):
                if m % 2 in which:
                    eng.wait_ge(mul_done.sem, at(i, 8) + (mul0 + s + 1))
                    one(at(i, 8) + m, m, i).then_inc(free[m % 2].sem, 1)
                    if one is takes_dve:
                        then_dve(at(i, 8) + m, m, i)

        with self.block() as block:
            @block.sync
            def _(sp):
                self.stream(sp, units)

            @block.scalar
            def _(act):
                def step(s, i):
                    self.await_unit(act, u0 + s, at(i, 1))
                    act.wait_ge(mul_done.sem, at(i, 8) + (mul0 + s + 1 - slots))
                    nc.scalar.activation(split[:, s % slots, 0, :], self.slot(u0 + s), ACT.Copy).then_inc(hi_done.sem, 1)
                    take(act, s - 1, i, (0,) if pair else (0, 1), takes_act)
                whole(act, step)
                take(act, units - 1, None, (0,) if pair else (0, 1), takes_act)

            @block.vector
            def _(dve):
                def step(s, i):
                    dve.wait_ge(hi_done.sem, at(i, 8) + (hi0 + s + 1))
                    nc.vector.tensor_tensor(split[:, s % slots, 1, :], self.slot(u0 + s),
                                            split[:, s % slots, 0, :].bitcast(F32), ALU.subtract
                                            ).then_inc(self.unit_used.sem, 1)
                    if pair:
                        take(dve, s - 1, i, (1,), takes_dve)
                nc.vector.tensor_copy(self.small_cols[:, 0:1], self.ones[:, 0:1]).then_inc(mul_done.sem, slots)
                whole(dve, step)
                if pair:
                    take(dve, units - 1, None, (1,), takes_dve)

            @block.tensor
            def _(pe):
                def step(s, i):
                    pe.wait_ge(self.unit_used.sem, at(i, 8) + (u0 + s + 1))
                    w = split[:, s % slots]
                    for t in range(TPU):
                        m, k = (s * TPU + t) // kt, (s * TPU + t) % kt
                        if k == 0:
                            pe.wait_ge(free[m % 2].sem, at(i, 8 // per) + (f0[m % 2] + m // per + 1 - BANKS // per))
                        c = slice(t * P, (t + 1) * P)
                        for j, (a, b) in enumerate(((w[:, 0, c], moving(0, k)), (w[:, 0, c], moving(1, k)),
                                                    (w[:, 1, c], moving(0, k)))):
                            ins = nc.tensor.matmul(ps[:, m % BANKS, 0:n], a, b, start=(k == 0 and j == 0),
                                                   stop=(k == kt - 1 and j == 2))
                    ins.then_inc(mul_done.sem, 1)
                pe.wait_ge(mul_done.sem, mul0)
                whole(pe, step)
        self.n_used += units
        hi_done.up(units), mul_done.up(units + slots)
        for j, x in enumerate(self.pair_free if pair else [self.bank_free]):
            x.n += n_m // per

    def linear_parts(self, split, n_m, kt, moving, out):
        n = moving(0, 0).shape[-1]
        self.project_parts(split, n_m, kt, moving, lambda m, s, i: self.nc.scalar.activation(
            out(m), self.ps[:, s % BANKS, 0:n], ACT.Copy))

    def column_sums(self, blocks, n, accumulate, bank=4):
        nc = self.nc
        with self.block() as block:
            @block.tensor
            def _(pe):
                for j, x in enumerate(blocks):
                    dst = self.ps[:, bank, 0:n] if accumulate else self.ps[:, bank + j, 0:n]
                    nc.tensor.matmul(dst, self.ones, x, start=(j == 0 or not accumulate),
                                     stop=(j == len(blocks) - 1 or not accumulate))

    def inverse_root(self, out, sums, scale, eps=EPS):
        nc = self.nc
        a = self.a
        with self.block() as block:
            @block.vector
            def _(dve):
                nc.vector.tensor_scalar(out, sums, scale, eps, ALU.mult, ALU.add).then_inc(self.dve_done.sem, 1)
                dve.wait_ge(self.dve_done.sem, self.dve_done.up())
                nc.vector.reciprocal(out, out).then_inc(a.sem, 1)

            @block.scalar
            def _(act):
                act.wait_ge(a.sem, a.n + 1)
                nc.scalar.activation(out, out, ACT.Sqrt)
        a.n += 1

    def norm_rows(self, x, cols, sq, rstd):
        nc = self.nc
        n = cols.stop - cols.start
        with self.block() as block:
            @block.scalar
            def _(act):
                nc.scalar.activation(sq, x[:, :, cols], ACT.Square)
        self.column_sums([sq[:, k, :] for k in range(x.shape[1])], n, True)
        self.inverse_root(rstd, self.ps[:, 4, 0:n], 1.0 / (x.shape[1] * P))

    def modulated(self, cols, gain, scale, shift, h=None, rstd=None):
        nc = self.nc
        n = cols.stop - cols.start
        x = self.xT
        if h is None:
            h, rstd = self.hT[:, :, cols], self.arena.tensor[:, self.arena.at:self.arena.at + n]
        col = self.small_cols
        self.norm_rows(x, cols, h, rstd)
        a = self.a
        with self.block() as block:
            @block.vector
            def _(dve):
                nc.vector.scalar_tensor_tensor(col, scale, 1.0, gain, ALU.add, ALU.mult).then_inc(self.dve_done.sem, 1)
                dve.wait_ge(self.dve_done.sem, self.dve_done.up())
                for k in range(KT):
                    nc.vector.scalar_tensor_tensor(h[:, k, :], x[:, k, cols], col[:, k:k + 1], rstd,
                                                   ALU.mult, ALU.mult).then_inc(a.sem, 1)

            @block.scalar
            def _(act):
                for k in range(KT):
                    act.wait_ge(a.sem, a.n + k + 1)
                    nc.scalar.activation(h[:, k, :], h[:, k, :], ACT.Identity, bias=shift[:, k:k + 1])
        a.n += KT

    def split_cond(self, cond):
        nc = self.nc
        parts = self.cond_split[:, :, :].rearrange("p k (c s) -> p k c s", s=2)
        with self.block() as block:
            @block.vector
            def _(dve):
                nc.vector.tensor_copy(parts[:, :, :, 0], cond).then_inc(self.dve_done.sem, 1)
                dve.wait_ge(self.dve_done.sem, self.dve_done.up())
                nc.vector.tensor_tensor(parts[:, :, :, 1], cond, parts[:, :, :, 0].bitcast(F32), ALU.subtract)

    def modulation(self, name, out, c0, n_c, bias):
        nc, ps = self.nc, self.ps
        M = 2 * n_c
        GROUPS = 6 * D // UNIT
        work = ExitStack()
        split = work.enter_context(nc.sbuf_tensor(f"split_{name}", [P, MSPLITS, 2, UNIT], F32R))
        rows = work.enter_context(nc.sbuf_tensor(f"rows_{name}", [M, 2 * UNIT], F32))
        pair = work.enter_context(nc.sbuf_tensor(f"pair_{name}", [M, n_c], F32))
        stationary = lambda k: self.cond_split[:, k, 2 * c0:2 * c0 + M]
        hi_done, mul_done, rows_done, pair_done = self.a, self.c, self.d, self.e
        hi0, mul0, rows0, pair0 = hi_done.n, mul_done.n, rows_done.n, pair_done.n
        u0 = self.n_used
        TURN = 2 * KT
        assert GROUPS % 2 == 0 and TURN % RING == 0 and TURN % MSPLITS == 0
        with self.block() as block:
            @block.sync
            def _(sp):
                self.stream(sp, GROUPS * KT)

            @block.scalar
            def _(act):
                with act.Fori(0, GROUPS // 2) as i:
                    for u in range(TURN):
                        self.await_unit(act, u0 + u, i, TURN)
                        act.wait_ge(mul_done.sem, i * TURN + (mul0 + MSPLITS + u + 1 - MSPLITS))
                        nc.scalar.activation(split[:, u % MSPLITS, 0, :], self.slot(u0 + u), ACT.Copy
                                             ).then_inc(hi_done.sem, 1)
                        if u % KT == KT - 1:
                            g = u // KT
                            act.wait_ge(mul_done.sem, i * TURN + (mul0 + MSPLITS + u + 1))
                            nc.scalar.activation(rows[:, g * UNIT:(g + 1) * UNIT],
                                                 ps[0:M, 2 * g:2 * g + 2, :].rearrange("p a b -> p (a b)"),
                                                 ACT.Copy).then_inc(rows_done.sem, 1)

            @block.vector
            def _(dve):
                nc.vector.tensor_tensor(pair[:, :], self.ident[0:M, 0:M:2], self.ident[0:M, 1:M:2], ALU.add
                                        ).then_inc(pair_done.sem, 1)
                nc.vector.tensor_copy(self.small_cols[:, 0:1], self.ones[:, 0:1]).then_inc(mul_done.sem, MSPLITS)
                with dve.Fori(0, GROUPS // 2) as i:
                    for u in range(TURN):
                        dve.wait_ge(hi_done.sem, i * TURN + (hi0 + u + 1))
                        nc.vector.tensor_tensor(split[:, u % MSPLITS, 1, :], self.slot(u0 + u),
                                                split[:, u % MSPLITS, 0, :].bitcast(F32), ALU.subtract
                                                ).then_inc(self.unit_used.sem, 1)

            @block.tensor
            def _(pe):
                pe.wait_ge(pair_done.sem, pair0 + 1)
                pe.wait_ge(mul_done.sem, mul0 + MSPLITS)

                def to_columns(g, i):
                    pe.wait_ge(rows_done.sem, i * 2 + (rows0 + g + 1))
                    for m in range(TPU):
                        tile = i * (2 * TPU) + (g * TPU + m)
                        nc.tensor.matmul(ps[:, 4, bass.ds(tile * n_c, n_c)], rows[:, (g * TPU + m) * P:(g * TPU + m + 1) * P],
                                         pair[:, :], start=True, stop=True)
                with pe.Fori(0, GROUPS // 2) as i:
                    for u in range(TURN):
                        g, k = u // KT, u % KT
                        pe.wait_ge(self.unit_used.sem, i * TURN + (u0 + u + 1))
                        for half in range(2):
                            for part in range(2):
                                ins = nc.tensor.matmul(ps[0:M, 2 * g + half, :], stationary(k),
                                                       split[:, u % MSPLITS, part, half * 512:(half + 1) * 512],
                                                       start=(k == 0 and part == 0), stop=(k == KT - 1 and part == 1))
                        ins.then_inc(mul_done.sem, 1)
                        if u == KT + 2:
                            to_columns(0, i)
                    to_columns(1, i)
        self.n_used += GROUPS * KT
        hi_done.up(GROUPS * KT), mul_done.up(GROUPS * KT + MSPLITS), rows_done.up(GROUPS), pair_done.up()
        psm = ps[:, 4, 0:GROUPS * TPU * n_c].rearrange("p (m c) -> p m c", c=n_c)
        with self.block() as block:
            @block.vector
            def _(dve):
                for c in range(n_c):
                    nc.vector.tensor_tensor(out[:, :, c], psm[:, :, c], bias, ALU.add)
        work.close()

    def mask(self, out, conditions):
        nc = self.nc
        with self.block() as block:
            @block.gpsimd
            def _(pool):
                nc.gpsimd.memset(out, 1.0).then_inc(self.pool_done.sem, 1)
                pool.wait_ge(self.pool_done.sem, self.pool_done.up())
                for base, cm, pattern in conditions:
                    v = out
                    if len(pattern) == 2:
                        v = out.rearrange("p (a b) -> p a b", a=pattern[0][1])
                    nc.gpsimd.affine_select(
                        out=v, in_=v, compare_op=ALU.is_ge, fill=0.0, base=base, pattern=pattern,
                        channel_multiplier=cm).then_inc(self.pool_done.sem, 1)
                    pool.wait_ge(self.pool_done.sem, self.pool_done.up())

    def constants(self):
        nc, s = self.nc, self.small
        self.one, self.ident, self.iota = s.take(P), s.take(P), s.take(P)
        self.ones = self.one
        with self.block() as block:
            @block.gpsimd
            def _(pool):
                nc.gpsimd.memset(self.ones, 1.0)
                nc.gpsimd.memset(self.ident, 0.0).then_inc(self.pool_done.sem, 1)
                pool.wait_ge(self.pool_done.sem, self.pool_done.up())
                nc.gpsimd.affine_select(
                    out=self.ident, in_=self.ident, compare_op=ALU.not_equal, fill=1.0, base=0,
                    pattern=[[-1, P]], channel_multiplier=1).then_inc(self.pool_done.sem, 1)
                pool.wait_ge(self.pool_done.sem, self.pool_done.up())
                nc.gpsimd.iota(
                    self.iota, pattern=[[1, P]], base=0, channel_multiplier=0,
                    allow_small_or_imprecise_dtypes=True).then_inc(self.pool_done.sem, 1)
                pool.wait_ge(self.pool_done.sem, self.pool_done.up())

            @block.vector
            def _(dve):
                nc.vector.memset(self.xT[:, 2, 0:1], 0.0).then_inc(self.bank_free.sem, BANKS)
                for j, x in enumerate(self.pair_free):
                    nc.vector.memset(self.xT[:, j, 0:1], 0.0).then_inc(x.sem, BANKS // 2)
        self.bank_free.n = BANKS
        for x in self.pair_free:
            x.n = BANKS // 2

    def causal_mask(self):
        nc = self.nc
        self.causal_add = self.extra.take(T + P)
        with self.block() as block:
            @block.gpsimd
            def _(pool):
                nc.gpsimd.memset(self.causal_add, 0.0).then_inc(self.pool_done.sem, 1)
                pool.wait_ge(self.pool_done.sem, self.pool_done.up())
                nc.gpsimd.affine_select(out=self.causal_add, in_=self.causal_add, compare_op=ALU.is_ge,
                                        fill=NEG, base=P, pattern=[[-1, T + P]], channel_multiplier=1)

    def load(self, pairs):
        nc = self.nc
        with self.block() as block:
            @block.scalar
            def _(act):
                for dst, src in pairs:
                    act.dma_start(dst, src).then_inc(self.loaded.sem, 16)
                act.wait_ge(self.loaded.sem, self.loaded.n + 16 * len(pairs))
        self.loaded.n += 16 * len(pairs)

    def attention(self, heads, n_keys, scale, scores, value, out, causal):
        nc, ps = self.nc, self.ps
        nk = n_keys // P
        G = 2 * TT
        mark = self.arena.at
        prob = self.arena.take(G, n_keys)
        turned = self.arena.take(2 * nk, T)
        top, total = self.arena.take(G), self.arena.take(G)
        width = G * n_keys
        sview = ps[:, 0:width // 512, :].rearrange("p b c -> p (b c)")
        a, b = self.a, self.b
        for h0 in range(0, heads, 2):
            with self.block() as block:
                @block.tensor
                def _(pe):
                    for g in range(G):
                        scores(h0 + g // TT, g % TT, sview[:, g * n_keys:(g + 1) * n_keys]).then_inc(a.sem, 1)

                @block.vector
                def _(dve):
                    for g in range(G):
                        dve.wait_ge(a.sem, a.n + (g | (512 // n_keys - 1)) + 1)
                        src = sview[:, g * n_keys:(g + 1) * n_keys]
                        if causal:
                            qt = g % TT
                            ins = nc.vector.tensor_tensor(prob[:, g, :], src,
                                                          self.causal_add[:, P - qt * P:P - qt * P + n_keys], ALU.add)
                        else:
                            ins = nc.vector.tensor_copy(prob[:, g, :], src)
                    ins.then_inc(self.dve_done.sem, 1)
                    dve.wait_ge(self.dve_done.sem, self.dve_done.up())
                    nc.vector.tensor_reduce(top, prob, AX_X, ALU.max).then_inc(self.dve_done.sem, 1)
                    dve.wait_ge(self.dve_done.sem, self.dve_done.up())
                    nc.vector.tensor_scalar(top, top, -scale, None, ALU.mult).then_inc(b.sem, 1)

                @block.scalar
                def _(act):
                    act.wait_ge(b.sem, b.n + 1)
                    for g in range(G):
                        nc.scalar.activation(prob[:, g, :], prob[:, g, :], ACT.Exp, bias=top[:, g:g + 1],
                                             scale=scale, accum_out=total[:, g:g + 1])
            a.n += G
            b.n += 1
            with self.block() as block:
                @block.vector
                def _(dve):
                    nc.vector.reciprocal(total, total).then_inc(self.dve_done.sem, 1)
                    dve.wait_ge(self.dve_done.sem, self.dve_done.up())
                    nc.vector.tensor_tensor(prob, prob, total.unsqueeze(2).broadcast_to([P, G, n_keys]),
                                            ALU.mult)
            tview = ps[:, 0:2 * nk * T // 512, :].rearrange("p b c -> p (b c)")
            oview = ps[:, 6, :]
            with self.block() as block:
                @block.tensor
                def _(pe):
                    for h in range(2):
                        for k in range(nk):
                            for qt in range(TT):
                                at = (h * nk + k) * T + qt * P
                                ins = nc.tensor.transpose(tview[:, at:at + P],
                                                          prob[:, h * TT + qt, k * P:(k + 1) * P], self.ident)
                    ins.then_inc(a.sem, 1)
                    pe.wait_ge(b.sem, b.n + 1)
                    for h in range(2):
                        for k in range(nk):
                            ins = nc.tensor.matmul(oview[:, h * T:(h + 1) * T], value(h0 + h, k),
                                                   turned[:, h * nk + k, :], start=(k == 0), stop=(k == nk - 1))
                    ins.then_inc(a.sem, 1)

                @block.vector
                def _(dve):
                    dve.wait_ge(a.sem, a.n + 1)
                    nc.vector.tensor_copy(flat(turned), tview).then_inc(b.sem, 1)

                @block.scalar
                def _(act):
                    act.wait_ge(a.sem, a.n + 2)
                    for h in range(2):
                        nc.scalar.activation(out(h0 + h), oview[:, h * T:(h + 1) * T], ACT.Copy)
            a.n += 2
            b.n += 1
        self.arena.at = mark

    def rope_tables(self, pos, freq, cos, sin):
        nc = self.nc
        mark = self.arena.at
        ang, n = self.arena.take(T), self.arena.take(T)
        v = nc.vector
        for out, quarter in ((sin, 0.0), (cos, 0.25)):
            with self.block() as block:
                @block.vector
                def _(dve):
                    v.tensor_scalar(ang, pos, freq, None, ALU.mult).then_inc(self.dve_done.sem, 1)
                    dve.wait_ge(self.dve_done.sem, self.dve_done.up())
                    v.tensor_scalar(n, ang, 1.0 / TWO_PI, quarter, ALU.mult, ALU.add).then_inc(self.dve_done.sem, 1)
                    dve.wait_ge(self.dve_done.sem, self.dve_done.up())
                    v.tensor_scalar(n, n, ROUND, -ROUND, ALU.add, ALU.add).then_inc(self.dve_done.sem, 1)
                    dve.wait_ge(self.dve_done.sem, self.dve_done.up())
                    v.scalar_tensor_tensor(ang, n, -PI_A, ang, ALU.mult, ALU.add).then_inc(self.dve_done.sem, 1)
                    dve.wait_ge(self.dve_done.sem, self.dve_done.up())
                    v.scalar_tensor_tensor(ang, n, -PI_B, ang, ALU.mult, ALU.add).then_inc(self.dve_done.sem, 1)
                    dve.wait_ge(self.dve_done.sem, self.dve_done.up())
                    v.scalar_tensor_tensor(ang, n, -PI_C, ang, ALU.mult, ALU.add).then_inc(self.dve_done.sem, 1)
                    dve.wait_ge(self.dve_done.sem, self.dve_done.up())
                    v.tensor_scalar(ang, ang, quarter * TWO_PI, PI_MAX, ALU.add, ALU.min).then_inc(self.dve_done.sem, 1)
                    dve.wait_ge(self.dve_done.sem, self.dve_done.up())
                    v.tensor_scalar(ang, ang, -PI_MAX, None, ALU.max)
            with self.block() as block:
                @block.scalar
                def _(act):
                    nc.scalar.activation(out, ang, ACT.Sin)
        self.arena.at = mark

    def rotation(self, out, half):
        nc = self.nc
        g = P // (2 * half)
        with self.block() as block:
            @block.gpsimd
            def _(pool):
                nc.gpsimd.memset(out, 0.0).then_inc(self.pool_done.sem, 1)
                pool.wait_ge(self.pool_done.sem, self.pool_done.up())
                v = out.rearrange("p (g s h) -> p g s h", g=g, s=2)
                for side, sign, off in ((0, -1.0, half), (1, 1.0, 0)):
                    nc.gpsimd.affine_select(
                        out=v[:, :, side, :], in_=v[:, :, side, :], compare_op=ALU.not_equal, fill=sign,
                        base=-off, pattern=[[-2 * half, g], [-1, half]], channel_multiplier=1).then_inc(self.pool_done.sem, 1)
                    pool.wait_ge(self.pool_done.sem, self.pool_done.up())

    def rope(self, x, rot, cos, sin, cols=None):
        nc = self.nc
        n = x.shape[1]
        a, b = self.a, self.b
        mark = self.arena.at
        tmp = self.arena.take(n, T)
        with self.block() as block:
            @block.tensor
            def _(pe):
                for j in range(n):
                    nc.tensor.matmul(self.ps[:, j // 2, j % 2 * T:(j % 2 + 1) * T], rot, x[:, j, :],
                                     start=True, stop=True)
        psv = self.ps[:, 0:(n + 1) // 2, :].rearrange("p b (c t) -> p (b c) t", t=T)[:, 0:n, :]
        wide = lambda t: t.unsqueeze(1).broadcast_to([P, n, T])
        with self.block() as block:
            @block.vector
            def _(dve):
                nc.vector.tensor_tensor(tmp, psv, wide(sin), ALU.mult).then_inc(self.dve_done.sem, 1)
                dve.wait_ge(self.dve_done.sem, self.dve_done.up())
                nc.vector.tensor_tensor(x, x, wide(cos), ALU.mult).then_inc(self.dve_done.sem, 1)
                dve.wait_ge(self.dve_done.sem, self.dve_done.up())
                nc.vector.tensor_tensor(x, x, tmp, ALU.add)
        self.arena.at = mark

    def scaled_root(self, x2d, m, scale, out, eps=EPS):
        nc = self.nc
        with self.block() as block:
            @block.scalar
            def _(act):
                nc.scalar.activation(out, x2d, ACT.Square)
        w = min(m, 512)
        self.column_sums([out[:, i:i + w] for i in range(0, m, w)], w, False, bank=0)
        self.inverse_root(out, self.ps[:, 0:m // w, 0:w].rearrange("p b c -> p (b c)") if m > w
                          else self.ps[:, 0, 0:m], scale, eps)

    def hybrid(self, c):
        nc, ps, A = self.nc, self.ps, self.arena
        v, s = nc.vector, nc.scalar
        mark = A.at
        PR = HEADS * TT
        o = A.take(2 * HEADS, T)
        ztile = A.take(HEADS, T)
        qkb = A.take(2 * HEADS, T)
        vb_tok = A.take(TT, HEADS * P)
        proj = A.take(24, T)
        self.split_h()
        self.linear_parts(self.split, 24, KT, self.latent_part, lambda m: flat(proj)[:, bass.ds(m * T, T)])
        self.linear_tokens(HEADS, KT, self.hT[:, :, LAT], range(TT), lambda m: vb_tok[:, :, m * P:(m + 1) * P])
        with self.block() as block:
            @block.tensor
            def _(pe):
                for t in range(TT):
                    for k in range(KT):
                        nc.tensor.matmul(ps[:, 4, t * 8:(t + 1) * 8],
                                         self.hT[:, k, TC + t * P:TC + (t + 1) * P],
                                         c["gates"][:, k, :], start=(k == 0), stop=(k == KT - 1))
        beta, g, tmp, absx = A.take(HEADS, TT), A.take(HEADS, TT), A.take(HEADS, TT), A.take(HEADS, TT)
        ab = ps[:, 4, 0:2 * HEADS * TT].rearrange("p (t s h) -> p s h t", t=TT, s=2)
        wide = lambda x: x.unsqueeze(2).broadcast_to([P, HEADS, TT])
        with self.block() as block:
            @block.scalar
            def _(act):
                s.activation(beta, ab[:, 0], ACT.Sigmoid).then_inc(self.act_done.sem, 1)
                act.wait_ge(self.act_done.sem, self.act_done.up())
                s.activation(c["decay"], c["a_log"], ACT.Exp)
        with self.block() as block:
            @block.vector
            def _(dve):
                v.tensor_tensor(g, ab[:, 1], wide(c["dt_bias"]), ALU.add).then_inc(self.dve_done.sem, 1)
                dve.wait_ge(self.dve_done.sem, self.dve_done.up())
                v.tensor_scalar(tmp, g, -1.0, None, ALU.mult).then_inc(self.dve_done.sem, 1)
                dve.wait_ge(self.dve_done.sem, self.dve_done.up())
                v.tensor_tensor(absx, g, tmp, ALU.max)
        with self.block() as block:
            @block.scalar
            def _(act):
                s.activation(tmp, absx, ACT.Exp, scale=-1.0).then_inc(self.act_done.sem, 1)
                act.wait_ge(self.act_done.sem, self.act_done.up())
                s.activation(tmp, tmp, ACT.Ln, bias=1.0)
        with self.block() as block:
            @block.vector
            def _(dve):
                v.scalar_tensor_tensor(g, g, 0.0, tmp, ALU.max, ALU.add).then_inc(self.dve_done.sem, 1)
                dve.wait_ge(self.dve_done.sem, self.dve_done.up())
                v.scalar_tensor_tensor(g, g, -1.0, wide(c["decay"]), ALU.mult, ALU.mult)
        conv = A.take(12, T)
        w = c["conv"]
        with self.block() as block:
            @block.vector
            def _(dve):
                for j in range(4):
                    for m in range(12):
                        if j == 0:
                            ins = v.tensor_scalar(conv[:, m, :], proj[:, m, :], w[:, m, 3:4], None, ALU.mult)
                        else:
                            ins = v.scalar_tensor_tensor(conv[:, m, j:T], proj[:, m, 0:T - j], w[:, m, 3 - j:4 - j],
                                                         conv[:, m, j:T], ALU.mult, ALU.add)
                    ins.then_inc(self.dve_done.sem, 1)
                    dve.wait_ge(self.dve_done.sem, self.dve_done.up())

            @block.scalar
            def _(act):
                s.activation(ztile, proj[:, 12:16, :], ACT.Silu)

            @block.gpsimd
            def _(pool):
                nc.gpsimd.tensor_copy(qkb, proj[:, 16:24, :])
        with self.block() as block:
            @block.scalar
            def _(act):
                s.activation(conv, conv, ACT.Silu)
        root = flat(proj)[:, 0:8 * T]
        self.scaled_root(flat(conv[:, 0:8, :]), 8 * T, 1.0, root)
        with self.block() as block:
            @block.vector
            def _(dve):
                v.tensor_tensor(flat(conv[:, 0:8, :]), flat(conv[:, 0:8, :]), root, ALU.mult)
        pairs = lambda x: x.rearrange("p h (t c) -> p (h t) c", c=P)
        qT, kT, vT = (pairs(conv[:, 4 * i:4 * i + 4, :]) for i in range(3))

        base = A.at
        upto, within, strict = A.take(P), A.take(P), A.take(P)
        nch = P // CHUNK
        same = [(0, 1, [[-CHUNK, nch], [0, CHUNK]]), (CHUNK - 1, -1, [[CHUNK, nch], [0, CHUNK]])]
        self.mask(within, same)
        self.mask(upto, same + [(0, -1, [[1, P]])])
        self.mask(strict, same + [(-1, 1, [[-1, P]])])
        gp, bp = g.rearrange("p h t -> p (h t)"), beta.rearrange("p h t -> p (h t)")
        gb = A.take(PR, P)
        cum, tot, kdec_c, kbe_c = (A.take(PR) for _ in range(4))
        with self.block() as block:
            @block.vector
            def _(dve):
                for p in range(PR):
                    v.tensor_scalar(gb[:, p, :], self.ones, gp[:, p:p + 1], None, ALU.mult)
        with self.block() as block:
            @block.tensor
            def _(pe):
                nc.tensor.matmul(ps[:, 6, 0:PR], upto, gp, start=True, stop=True)
                nc.tensor.matmul(ps[:, 7, 0:PR], within, gp, start=True, stop=True)
                for p in range(PR):
                    nc.tensor.matmul(ps[:, p // 4, p % 4 * P:(p % 4 + 1) * P], gb[:, p, :], upto, start=True, stop=True)
                for p in range(PR):
                    nc.tensor.matmul(ps[:, 2 + p // 4, p % 4 * P:(p % 4 + 1) * P], kT[:, p, :], kT[:, p, :],
                                     start=True, stop=True)
                for p in range(PR):
                    nc.tensor.matmul(ps[:, 4 + p // 4, p % 4 * P:(p % 4 + 1) * P], kT[:, p, :], qT[:, p, :],
                                     start=True, stop=True)
        two = lambda b: ps[:, b:b + 2, :].rearrange("p b (c m) -> p (b c) m", m=P)
        rows, kk, kq = two(0), two(2), ps[:, 4:6, :].rearrange("p b (c m) -> p (b c) m", m=P)
        rowexp, dec, decT = A.take(PR, P), gb, A.take(PR, P)
        a = self.a
        with self.block() as block:
            @block.vector
            def _(dve):
                v.tensor_copy(cum, ps[:, 6, 0:PR]).then_inc(self.dve_done.sem, 1)
                dve.wait_ge(self.dve_done.sem, self.dve_done.up())
                v.tensor_copy(tot, ps[:, 7, 0:PR]).then_inc(self.dve_done.sem, 1)
                dve.wait_ge(self.dve_done.sem, self.dve_done.up())
                v.tensor_tensor(kdec_c, tot, cum, ALU.subtract)
        with self.block() as block:
            @block.vector
            def _(dve):
                for p in range(PR):
                    v.tensor_scalar(dec[:, p, :], rows[:, p, :], cum[:, p:p + 1], 0.0, ALU.subtract, ALU.max)
                    v.tensor_scalar(decT[:, p, :], rows[:, p, :], cum[:, p:p + 1], 0.0, ALU.subtract, ALU.min)

        with self.block() as block:
            @block.scalar
            def _(act):
                s.activation(rowexp, rows, ACT.Exp)
                s.activation(dec, dec, ACT.Exp, scale=-1.0)
                s.activation(decT, decT, ACT.Exp)
                s.activation(kdec_c, kdec_c, ACT.Exp)
                s.activation(kbe_c, cum, ACT.Exp)
        bwide = lambda x: x.unsqueeze(1).broadcast_to([P, PR, P])
        pw, pwT, invT = A.take(PR, P), A.take(PR, P), A.take(PR, P)
        qk = decT
        DKS = float(P) ** -0.5
        with self.block() as block:
            @block.vector
            def _(dve):
                v.tensor_tensor(kbe_c, kbe_c, bp, ALU.mult).then_inc(self.dve_done.sem, 1)
                dve.wait_ge(self.dve_done.sem, self.dve_done.up())
                v.tensor_tensor(dec, dec, bwide(strict), ALU.mult).then_inc(self.dve_done.sem, 1)
                dve.wait_ge(self.dve_done.sem, self.dve_done.up())
                v.tensor_tensor(dec, dec, bp.unsqueeze(2).broadcast_to([P, PR, P]), ALU.mult).then_inc(self.dve_done.sem, 1)
                dve.wait_ge(self.dve_done.sem, self.dve_done.up())
                v.scalar_tensor_tensor(flat(pw), flat(dec), -1.0, flat(kk), ALU.mult, ALU.mult).then_inc(self.dve_done.sem, 1)
                dve.wait_ge(self.dve_done.sem, self.dve_done.up())
                v.tensor_tensor(decT, decT, bwide(upto), ALU.mult).then_inc(self.dve_done.sem, 1)
                dve.wait_ge(self.dve_done.sem, self.dve_done.up())
                v.scalar_tensor_tensor(flat(qk), flat(decT), DKS, flat(kq), ALU.mult, ALU.mult).then_inc(self.dve_done.sem, 1)
                dve.wait_ge(self.dve_done.sem, self.dve_done.up())
                v.scalar_tensor_tensor(flat(qT), flat(qT), DKS, flat(rowexp), ALU.mult, ALU.mult)

        def turn(src, bank):
            with self.block() as block:
                @block.tensor
                def _(pe):
                    for p in range(PR):
                        nc.tensor.transpose(ps[:, bank + p // 4, p % 4 * P:(p % 4 + 1) * P], src[:, p, :], self.ident)

        def times(lhsT, rhs, bank):
            for p in range(PR):
                nc.tensor.matmul(ps[:, bank + p // 4, p % 4 * P:(p % 4 + 1) * P], lhsT[:, p, :], rhs[:, p, :],
                                 start=True, stop=True)
        turn(pw, 0)
        with self.block() as block:
            @block.vector
            def _(dve):
                v.tensor_copy(pwT, two(0)).then_inc(self.dve_done.sem, 1)
                dve.wait_ge(self.dve_done.sem, self.dve_done.up())
                v.tensor_tensor(invT, pwT, bwide(self.ident), ALU.add)
        span = 2
        while span < CHUNK:
            with self.block() as block:
                @block.tensor
                def _(pe):
                    times(pwT, pw, 0)
                    times(pw, pwT, 2)
            with self.block() as block:
                @block.vector
                def _(dve):
                    v.tensor_copy(pw, two(0))

                @block.scalar
                def _(act):
                    s.activation(pwT, two(2), ACT.Copy)
            with self.block() as block:
                @block.tensor
                def _(pe):
                    times(pw, invT, 4)
            with self.block() as block:
                @block.vector
                def _(dve):
                    v.tensor_tensor(invT, invT, two(4), ALU.add)
            span *= 2
        vbeta, kbe, kdec = pw, pwT, dec
        turn(kT, 0)
        turn(vT, 2)
        with self.block() as block:
            @block.vector
            def _(dve):
                for p in range(PR):
                    v.tensor_scalar(kbe[:, p, :], two(0)[:, p, :], kbe_c[:, p:p + 1], None, ALU.mult)
                    v.tensor_scalar(kdec[:, p, :], two(0)[:, p, :], kdec_c[:, p:p + 1], None, ALU.mult)
                    v.tensor_scalar(vbeta[:, p, :], two(2)[:, p, :], bp[:, p:p + 1], None, ALU.mult)
        with self.block() as block:
            @block.tensor
            def _(pe):
                times(invT, vbeta, 4)
                times(kbe, invT, 6)
        u, wT = A.take(PR, P), A.take(PR, P)
        with self.block() as block:
            @block.vector
            def _(dve):
                v.tensor_copy(u, two(4))

            @block.scalar
            def _(act):
                s.activation(wT, two(6), ACT.Copy)
        state = A.take(HEADS, P)
        vnew = vbeta
        hv = lambda x: x.rearrange("p (h t) c -> p h t c", t=TT)
        oview = two(4)
        for n in range(T // CHUNK):
            t, r = n // nch, slice(n % nch * CHUNK, (n % nch + 1) * CHUNK)
            if n:
                with self.block() as block:
                    @block.tensor
                    def _(pe):
                        for h in range(HEADS):
                            nc.tensor.matmul(ps[:, 0, h * P:(h + 1) * P], wT[:, h * TT + t, :], state[:, h, :],
                                             start=True, stop=True)
                with self.block() as block:
                    @block.vector
                    def _(dve):
                        v.tensor_tensor(hv(vnew)[r, :, t, :], hv(u)[r, :, t, :],
                                        ps[r, 0, :].rearrange("p (h c) -> p h c", h=HEADS), ALU.subtract)
            else:
                with self.block() as block:
                    @block.vector
                    def _(dve):
                        v.tensor_copy(hv(vnew)[r, :, t, :], hv(u)[r, :, t, :])
            with self.block() as block:
                @block.tensor
                def _(pe):
                    for h in range(HEADS):
                        p = h * TT + t
                        if n:
                            nc.tensor.matmul(oview[:, p, r], state[:, h, :], qT[:, p, r], start=True, stop=False)
                        nc.tensor.matmul(oview[:, p, r], vnew[r, p, :], qk[r, p, r], start=(n == 0), stop=True)
                    for h in range(HEADS):
                        p = h * TT + t
                        nc.tensor.matmul(ps[:, 6, h * P:(h + 1) * P], kdec[r, p, :], vnew[r, p, :],
                                         start=True, stop=True)
            with self.block() as block:
                @block.vector
                def _(dve):
                    for h in range(HEADS):
                        upd = ps[:, 6, h * P:(h + 1) * P]
                        if n:
                            v.scalar_tensor_tensor(state[:, h, :], state[:, h, :],
                                                   rowexp[:, h * TT + t, r.stop - 1:r.stop], upd, ALU.mult, ALU.add)
                        else:
                            v.tensor_copy(state[:, h, :], upd)
        oa = o[:, 0:HEADS, :]
        with self.block() as block:
            @block.scalar
            def _(act):
                s.activation(pairs(oa), oview, ACT.Copy)
        root = flat(proj)[:, 0:HEADS * T]
        self.scaled_root(flat(oa), HEADS * T, 1.0 / P, root)
        with self.block() as block:
            @block.vector
            def _(dve):
                v.scalar_tensor_tensor(flat(oa), flat(oa), c["o_norm"], root, ALU.mult, ALU.mult).then_inc(self.dve_done.sem, 1)
                dve.wait_ge(self.dve_done.sem, self.dve_done.up())
                v.tensor_tensor(flat(oa), flat(oa), flat(ztile), ALU.mult)
        A.at = base
        self.rope(qkb, c["rot"], c["cos"], c["sin"])

        def scores(h, qt, dst):
            return nc.tensor.matmul(dst, qkb[:, h, qt * P:(qt + 1) * P], qkb[:, HEADS + h, :], start=True, stop=True)
        self.attention(HEADS, T, DKS, scores, lambda h, k: vb_tok[:, k, h * P:(h + 1) * P],
                       lambda h: o[:, HEADS + h, :], True)
        self.output(o, LAT, c["g1"])
        A.at = mark

    def output(self, o, cols, gate):
        nc = self.nc
        n = cols.stop - cols.start

        def tile(k, w, bank, first, last):
            return nc.tensor.matmul(self.ps[:, bank, 0:n], w, o[:, k, :], start=first, stop=last)

        def takes(dve, m, s, i):
            x = self.xT[:, m, cols]
            return nc.vector.scalar_tensor_tensor(x, self.ps[:, s % BANKS, 0:n], gate[:, m:m + 1], x, ALU.mult, ALU.add)
        self.project(KT, o.shape[1], tile, takes, "vector")

    def peer_routes(self, subkeys):
        nc, ps, A = self.nc, self.ps, self.arena
        v = nc.vector
        mark = A.at
        SIDES = 2 * PH
        qT = A.take(SIDES, T)
        keys = A.take(SIDES, KEYS)
        self.load([(keys, subkeys)])
        self.linear_parts(self.split, SIDES, KT, self.latent_part, lambda m: flat(qT)[:, bass.ds(m * T, T)])
        score, work = A.take(SIDES, KEYS), A.take(4, KEYS)
        val, idx = A.take(SIDES, TOPK), A.take(SIDES, TOPK)
        idx_u = A.take(SIDES, TOPK, dt=U32)
        cand, cwork = A.take(PH, TOPK * TOPK), A.take(2, TOPK * TOPK)
        top, gate = A.take(PH, TOPK), A.take(PH, TOPK)
        pos_u, part_u = A.take(PH, TOPK, dt=U32), A.take(PH, TOPK, dt=U32)
        part = A.take(PH, TOPK)
        onehot = A.take(PH * TOPK, TOPK)
        mx, total = A.take(PH), A.take(PH)
        expert = A.take(2, PH * TOPK)
        ps2 = ps[:, 0:4, :].rearrange("p b (c n) -> p (b c) n", n=KEYS)

        def top16(dve, sets):
            lo, hi = slice(0, 8), slice(8, 16)
            for values, scratch, out, out_idx in sets:
                v.max(out[:, lo], values).then_inc(self.dve_done.sem, 1)
            for values, scratch, out, out_idx in sets:
                dve.wait_ge(self.dve_done.sem, self.dve_done.up())
                v.max_index(out_idx[:, lo], out[:, lo], values)
                v.match_replace(out=scratch, in_to_replace=out[:, lo], in_values=values, imm_value=LOWEST
                                ).then_inc(self.dve_done.sem, 1)
            for values, scratch, out, out_idx in sets:
                dve.wait_ge(self.dve_done.sem, self.dve_done.up())
                v.max(out[:, hi], scratch).then_inc(self.dve_done.sem, 1)
            for values, scratch, out, out_idx in sets:
                dve.wait_ge(self.dve_done.sem, self.dve_done.up())
                v.max_index(out_idx[:, hi], out[:, hi], scratch)

        for t in range(TT):
            with self.block() as block:
                @block.tensor
                def _(pe):
                    for j in range(SIDES):
                        nc.tensor.matmul(ps2[:, j, :], qT[:, j, t * P:(t + 1) * P], keys[:, j, :],
                                         start=True, stop=True)
            with self.block() as block:
                @block.scalar
                def _(act):
                    nc.scalar.activation(score, ps2, ACT.Copy)
            with self.block() as block:
                @block.vector
                def _(dve):
                    for j0 in range(0, SIDES, 4):
                        top16(dve, [(score[:, j, :], work[:, j % 4, :], val[:, j, :], idx_u[:, j, :])
                                    for j in range(j0, j0 + 4)])
            sides = val.rearrange("p (h s) k -> p s h k", s=2)
            full = [P, PH, TOPK, TOPK]
            with self.block() as block:
                @block.vector
                def _(dve):
                    v.tensor_copy(idx, idx_u).then_inc(self.dve_done.sem, 1)
                    dve.wait_ge(self.dve_done.sem, self.dve_done.up())
                    v.tensor_tensor(cand.rearrange("p h (a b) -> p h a b", a=TOPK),
                                    sides[:, 0].unsqueeze(3).broadcast_to(full),
                                    sides[:, 1].unsqueeze(2).broadcast_to(full), ALU.add)
            with self.block() as block:
                @block.vector
                def _(dve):
                    for h0 in range(0, PH, 2):
                        top16(dve, [(cand[:, h, :], cwork[:, h % 2, :], top[:, h, :], pos_u[:, h, :])
                                    for h in range(h0, h0 + 2)])
            hw = lambda x: x.unsqueeze(2).broadcast_to([P, PH, TOPK])
            with self.block() as block:
                @block.vector
                def _(dve):
                    v.tensor_copy(mx, top[:, :, 0]).then_inc(self.dve_done.sem, 1)
                    dve.wait_ge(self.dve_done.sem, self.dve_done.up())
                    v.tensor_tensor(gate, top, hw(mx), ALU.subtract)
            with self.block() as block:
                @block.scalar
                def _(act):
                    nc.scalar.activation(gate, gate, ACT.Exp)
            with self.block() as block:
                @block.vector
                def _(dve):
                    v.tensor_reduce(total, gate, AX_X, ALU.add).then_inc(self.dve_done.sem, 1)
                    dve.wait_ge(self.dve_done.sem, self.dve_done.up())
                    v.reciprocal(total, total).then_inc(self.dve_done.sem, 1)
                    dve.wait_ge(self.dve_done.sem, self.dve_done.up())
                    v.tensor_tensor(gate, gate, hw(total), ALU.mult)
            idxs = idx.rearrange("p (h s) k -> p s h k", s=2)
            big = [P, PH * TOPK, TOPK]
            oh4 = onehot.rearrange("p (h k) a -> p h k a", h=PH)
            for side, (op, by) in enumerate(((ALU.logical_shift_right, 4), (ALU.bitwise_and, 15))):
                with self.block() as block:
                    @block.vector
                    def _(dve):
                        v.tensor_scalar(part_u, pos_u, by, None, op).then_inc(self.dve_done.sem, 1)
                        dve.wait_ge(self.dve_done.sem, self.dve_done.up())
                        v.tensor_copy(part, part_u).then_inc(self.dve_done.sem, 1)
                        dve.wait_ge(self.dve_done.sem, self.dve_done.up())
                        v.tensor_tensor(onehot, part.rearrange("p h k -> p (h k)").unsqueeze(2).broadcast_to(big),
                                        self.iota[:, 0:TOPK].unsqueeze(1).broadcast_to(big), ALU.is_equal).then_inc(self.dve_done.sem, 1)
                        dve.wait_ge(self.dve_done.sem, self.dve_done.up())
                        v.tensor_tensor(oh4, oh4, idxs[:, side].unsqueeze(2).broadcast_to(full), ALU.mult).then_inc(self.dve_done.sem, 1)
                        dve.wait_ge(self.dve_done.sem, self.dve_done.up())
                        v.tensor_reduce(expert[:, side, :], onehot, AX_X, ALU.add)
            with self.block() as block:
                @block.tensor
                def _(pe):
                    for j, x in enumerate((expert[:, 0, :], expert[:, 1, :], flat(gate))):
                        nc.tensor.transpose(ps[:, 5, j * P:(j + 1) * P], x, self.ident)
            with self.block() as block:
                @block.vector
                def _(dve):
                    v.tensor_copy(self.selT[:, :, t * P:(t + 1) * P],
                                  ps[:, 5, 0:3 * P].rearrange("p (a b) -> p a b", a=3))
        A.at = mark

    def latent_part(self, part, k):
        return self.hsplit[:, part, k, :]

    def split_h(self):
        self.divide(self.hT[:, :, LAT], self.hsplit[:, 0], self.hsplit[:, 1])

    def divide(self, x, high, low):
        nc = self.nc
        with self.block() as block:
            @block.scalar
            def _(act):
                nc.scalar.activation(high, x, ACT.Copy).then_inc(self.act_done.sem, 1)

            @block.vector
            def _(dve):
                dve.wait_ge(self.act_done.sem, self.act_done.up())
                nc.vector.tensor_tensor(low, x, high.bitcast(F32), ALU.subtract)

    def peer_experts(self, name, gate_col):
        nc, ps = self.nc, self.ps
        v, s = nc.vector, nc.scalar
        work = ExitStack()
        G = work.enter_context(nc.sbuf_tensor(f"routes_{name}", [P, T, KEYS], F32))
        split = work.enter_context(nc.sbuf_tensor(f"split_{name}", [P, SPLITS, 2, UNIT], F32R))
        wsplit = work.enter_context(nc.sbuf_tensor(f"wsplit_{name}", [P, 2, T], F32R))
        gflat = G[:, :, :].rearrange("p a b -> p (a b)")
        B = 4
        spare = self.xT[:, :, 0:TC]
        row1 = lambda i, j: spare[:, 2 * i + j // 2, j % 2 * P:(j % 2 + 1) * P]
        row2 = lambda i, j: spare[:, 4 + 2 * i + j // 2, j % 2 * P:(j % 2 + 1) * P]
        rows2 = lambda i: spare[:, 4 + 2 * i:6 + 2 * i, :].rearrange("p a (b c) -> p a b c", b=2)
        iota4 = self.iota.unsqueeze(1).unsqueeze(1).broadcast_to([P, B // 2, 2, P])
        onehots, placed, taken = self.a, self.b, self.c
        a0 = onehots.n
        sel = self.selT
        with self.block() as block:
            @block.vector
            def _(dve):
                v.memset(row1(0, 0), 0.0).then_inc(placed.sem, 2)
                v.memset(row1(1, 0), 0.0).then_inc(taken.sem, 2)
        b0, c0 = placed.up(2), taken.up(2)
        TURNS = T // B // 2
        with self.block() as block:
            @block.vector
            def _(dve):
                with dve.Fori(0, TURNS) as i:
                    for half in range(2):
                        dve.wait_ge(placed.sem, i * 2 + (b0 + half - 1))
                        for j in range(B):
                            t = i * (2 * B) + (half * B + j)
                            v.tensor_scalar(row1(half, j), self.iota, sel[:, 0, bass.ds(t, 1)],
                                            sel[:, 2, bass.ds(t, 1)], ALU.is_equal, ALU.mult)
                        column_key = sel[:, 1, bass.ds(i * (2 * B) + half * B, B)].rearrange("p (a b) -> p a b", b=2)
                        v.tensor_tensor(rows2(half), iota4, column_key.unsqueeze(3).broadcast_to([P, B // 2, 2, P]),
                                        ALU.is_equal).then_inc(onehots.sem, 1)

            @block.tensor
            def _(pe):
                with pe.Fori(0, TURNS) as i:
                    for half in range(2):
                        pe.wait_ge(onehots.sem, i * 2 + (a0 + half + 1))
                        pe.wait_ge(taken.sem, i * 2 + (c0 + half - 1))
                        for j in range(B):
                            ins = nc.tensor.matmul(ps[:, half, j * P:(j + 1) * P], row1(half, j), row2(half, j),
                                                   start=True, stop=True)
                        ins.then_inc(placed.sem, 1)

            @block.scalar
            def _(act):
                with act.Fori(0, TURNS) as i:
                    for half in range(2):
                        act.wait_ge(placed.sem, i * 2 + (b0 + half + 1))
                        s.activation(gflat[:, bass.ds(i * (2 * B * P) + half * B * P, B * P)], ps[:, half, :],
                                     ACT.Copy).then_inc(taken.sem, 1)
        onehots.up(2 * TURNS), placed.up(2 * TURNS), taken.up(2 * TURNS)

        act_sb = [spare[:, i, :] for i in range(2)]
        raw = spare[:, 2, :]
        hi_done, lo_done, mul_done = self.a, self.b, self.c
        gelu_done, raw_done, high_done, w_done = self.d, self.e, self.f, self.g
        hi0, lo0, mul0, gelu0, raw0, high0, w0 = (x.n for x in (hi_done, lo_done, mul_done, gelu_done, raw_done,
                                                                high_done, w_done))
        unit0 = self.n_used
        PAIRS = 6
        TURNS = (KEYS - 2) // PAIRS
        assert TURNS * PAIRS == KEYS - 2 and 2 * PAIRS % RING == 0 and 2 * PAIRS % SPLITS == 0

        def turns(eng, step):
            with eng.Fori(0, TURNS) as i:
                for q in range(1, PAIRS + 1):
                    step(i * PAIRS + q, q, i)

        with self.block() as block:
            @block.sync
            def _(sp):
                self.stream(sp, 2 * KEYS)

            @block.scalar
            def _(act):
                def high(u, index, turn, reused=True):
                    self.await_unit(act, unit0 + u, turn, 2 * PAIRS)
                    if reused:
                        act.wait_ge(mul_done.sem, index + (mul0 + 1 - SPLITS))
                    s.activation(split[:, u % SPLITS, 0, :], self.slot(unit0 + u), ACT.Copy).then_inc(hi_done.sem, 1)

                def gelu(j, par, after, reused=True):
                    act.wait_ge(mul_done.sem, after + mul0)
                    if reused:
                        act.wait_ge(raw_done.sem, j + (raw0 - 1))
                    s.activation(act_sb[par], ps[:, 4 + par, 0:T], ACT.Gelu).then_inc(gelu_done.sem, 1)

                def step(j, q, i):
                    gelu(j, q % 2, j * 2, not isinstance(j, int))
                    high(2 * q + 2, j * 2 + 2, i)
                    high(2 * q + 3, j * 2 + 3, i)
                high(0, 0, 0, False)
                high(1, 1, 0, False)
                gelu(0, 0, 1, False)
                high(2, 2, 0, False)
                high(3, 3, 0)
                turns(act, step)
                gelu(KEYS - 1, (KEYS - 1) % 2, 2 * KEYS - 2)

            @block.vector
            def _(dve):
                def low(u, index):
                    dve.wait_ge(hi_done.sem, index + (hi0 + 1))
                    v.tensor_tensor(split[:, u % SPLITS, 1, :], self.slot(unit0 + u),
                                    split[:, u % SPLITS, 0, :].bitcast(F32), ALU.subtract).then_inc(self.unit_used.sem, 1)

                def weigh(j, par):
                    dve.wait_ge(gelu_done.sem, j + (gelu0 + 1))
                    dve.wait_ge(w_done.sem, j + w0)
                    v.tensor_tensor(raw, act_sb[par], G[:, :, bass.ds(j, 1)].rearrange("p t o -> p (t o)"),
                                    ALU.mult).then_inc(raw_done.sem, 1)

                def divide(j):
                    dve.wait_ge(raw_done.sem, j + (raw0 + 1))
                    dve.wait_ge(mul_done.sem, j * 2 + (mul0 + 1))
                    v.tensor_copy(wsplit[:, 0, :], raw).then_inc(high_done.sem, 1)
                    dve.wait_ge(high_done.sem, j + (high0 + 1))
                    v.tensor_tensor(wsplit[:, 1, :], raw, wsplit[:, 0, :].bitcast(F32), ALU.subtract
                                    ).then_inc(w_done.sem, 1)

                def step(j, q, i):
                    weigh(j, q % 2)
                    low(2 * q + 2, j * 2 + 2)
                    divide(j)
                    low(2 * q + 3, j * 2 + 3)
                low(0, 0)
                low(1, 1)
                weigh(0, 0)
                low(2, 2)
                divide(0)
                low(3, 3)
                turns(dve, step)
                weigh(KEYS - 1, (KEYS - 1) % 2)
                divide(KEYS - 1)

            @block.tensor
            def _(pe):
                def parts(weights, moving):
                    return ((weights[0], moving[0]), (weights[0], moving[1]), (weights[1], moving[0]))

                def hidden(par, u, index):
                    pe.wait_ge(self.unit_used.sem, index + (unit0 + 1))
                    w = split[:, u % SPLITS]
                    for k in range(KT):
                        c = slice(k * P, (k + 1) * P)
                        for n, (a, b) in enumerate(parts((w[:, 0, c], w[:, 1, c]),
                                                         (self.hsplit[:, 0, k, :], self.hsplit[:, 1, k, :]))):
                            ins = nc.tensor.matmul(ps[:, 4 + par, 0:T], a, b, start=(k == 0 and n == 0),
                                                   stop=(k == KT - 1 and n == 2))
                    ins.then_inc(mul_done.sem, 1)

                def expand(j, u, index, first=False, last=False):
                    pe.wait_ge(self.unit_used.sem, index + (unit0 + 1))
                    pe.wait_ge(w_done.sem, j + (w0 + 1))
                    w = split[:, u % SPLITS]
                    for m in range(KT):
                        c = slice(m * P, (m + 1) * P)
                        for n, (a, b) in enumerate(parts((w[:, 0, c], w[:, 1, c]),
                                                         (wsplit[:, 0, :], wsplit[:, 1, :]))):
                            ins = nc.tensor.matmul(ps[:, m // 2, m % 2 * T:(m % 2 + 1) * T], a, b,
                                                   start=(first and m % 2 == 0 and n == 0), stop=last and n == 2,
                                                   skip_group_check=True)
                    ins.then_inc(mul_done.sem, 1)

                def step(j, q, i):
                    pe.wait_ge(gelu_done.sem, j + gelu0)
                    hidden((q + 1) % 2, 2 * q + 1, j * 2 + 1)
                    expand(j, 2 * q + 2, j * 2 + 2)
                hidden(0, 0, 0)
                hidden(1, 1, 1)
                expand(0, 2, 2, first=True)
                turns(pe, step)
                expand(KEYS - 1, 2 * KEYS - 1, 2 * KEYS - 1, last=True)
        self.n_used += 2 * KEYS
        for x in (hi_done, mul_done):
            x.up(2 * KEYS)
        for x in (gelu_done, raw_done, high_done, w_done):
            x.up(KEYS)
        with self.block() as block:
            @block.vector
            def _(dve):
                for m in range(KT):
                    x = self.xT[:, m, LAT]
                    v.scalar_tensor_tensor(x, ps[:, m // 2, m % 2 * T:(m % 2 + 1) * T], gate_col[:, m:m + 1], x,
                                           ALU.mult, ALU.add)
        work.close()

    def latent_attention(self, c):
        nc, ps, A = self.nc, self.ps, self.arena
        v = nc.vector
        mark = A.at
        low = A.take(7, T)
        q, kn = A.take(12, T), A.take(MLA_H, T)
        vt = A.take(TT, MLA_H * P)
        o = A.take(MLA_H, T)
        sq, root = A.take(4, T), A.take(T)
        self.split_h()
        self.linear_parts(self.split, 7, KT, self.latent_part, lambda m: low[:, m, :])
        for a0, n in ((0, 4), (4, 2)):
            part = low[:, a0:a0 + n, :]
            self.norm_rows(part, slice(0, T), sq[:, 0:n, :], root)
            with self.block() as block:
                @block.vector
                def _(dve):
                    for k in range(n):
                        v.scalar_tensor_tensor(part[:, k, :], part[:, k, :], c["norms"][:, a0 + k:a0 + k + 1], root,
                                               ALU.mult, ALU.mult)
        self.linear(12, 4, low, slice(0, T), lambda m: q[:, m, :])
        self.linear(MLA_H, 2, low[:, 4:6, :], slice(0, T), lambda m: kn[:, m, :])
        self.linear_tokens(MLA_H, 2, low[:, 4:6, :], range(TT), lambda m: vt[:, :, m * P:(m + 1) * P])
        self.rope(q[:, 8:12, :], c["rot"], c["cos"], c["sin"])
        self.rope(low[:, 6:7, :], c["rot"], c["cos"], c["sin"])

        def scores(h, qt, dst):
            r = slice(h % 2 * 64, h % 2 * 64 + 64)
            tok = slice(qt * P, (qt + 1) * P)
            nc.tensor.matmul(dst, q[:, h, tok], kn[:, h, :], start=True, stop=False)
            return nc.tensor.matmul(dst, q[r, 8 + h // 2, tok], low[r, 6, :], start=False, stop=True)
        self.attention(MLA_H, T, float(192) ** -0.5, scores, lambda h, k: vt[:, k, h * P:(h + 1) * P],
                       lambda h: o[:, h, :], True)
        self.output(o, LAT, c["g1"])
        A.at = mark

    def add_normed(self, y, parts, gain):
        nc = self.nc
        v = nc.vector
        mark = self.arena.at
        c0, c1 = parts[0][0].start, parts[-1][0].stop
        sq, root, col = self.arena.take(KT, c1 - c0), self.arena.take(c1 - c0), self.arena.take(len(parts), KT)
        self.norm_rows(y, slice(0, c1 - c0), sq, root)
        with self.block() as block:
            @block.vector
            def _(dve):
                for j, (cols, g) in enumerate(parts):
                    ins = v.tensor_tensor(col[:, j, :], g, gain, ALU.mult)
                ins.then_inc(self.dve_done.sem, 1)
                dve.wait_ge(self.dve_done.sem, self.dve_done.up())
                for j, (cols, g) in enumerate(parts):
                    at = slice(cols.start - c0, cols.stop - c0)
                    for k in range(KT):
                        ins = v.scalar_tensor_tensor(sq[:, k, at], y[:, k, at], col[:, j, k:k + 1], root[:, at],
                                                     ALU.mult, ALU.mult)
                ins.then_inc(self.dve_done.sem, 1)
                dve.wait_ge(self.dve_done.sem, self.dve_done.up())
                x = self.xT[:, :, c0:c1]
                v.tensor_tensor(x, x, sq, ALU.add)
        self.arena.at = mark

    def swiglu(self, name, parts, gain_in, gain_out):
        nc, ps = self.nc, self.ps
        cols = slice(parts[0][0].start, parts[-1][0].stop)
        n = cols.stop - cols.start
        outer = ExitStack()
        hidden = outer.enter_context(nc.sbuf_tensor(f"hidden_{name}", [P, 2, FT, n], F32R))
        slots = 2 if n > T else 4
        split = outer.enter_context(nc.sbuf_tensor(f"split_{name}", [P, slots, 2, UNIT], F32R))
        inner = ExitStack()
        h_parts = inner.enter_context(nc.sbuf_tensor(f"h_parts_{name}", [P, 2, KT, n], F32R))
        scratch = inner.enter_context(nc.sbuf_tensor(f"h_{name}", [P, KT, T], F32))
        lit = inner.enter_context(nc.sbuf_tensor(f"silu_{name}", [P, 2, n], F32))
        raw = inner.enter_context(nc.sbuf_tensor(f"raw_{name}", [P, n], F32))
        for at, shift, scale, _ in parts:
            self.modulated(at, gain_in, scale, shift, scratch[:, :, :], raw[:, 0:T])
            c = slice(at.start - cols.start, at.stop - cols.start)
            self.divide(scratch[:, :, :], h_parts[:, 0, :, c], h_parts[:, 1, :, c])
        silu_done = self.pair_free[0]
        s0, f0 = silu_done.n, self.pair_free[1].n
        high_done, low_done = self.e, self.f
        high0, low0 = high_done.n, low_done.n
        high, low = (hidden[:, part].rearrange("p a b -> p (a b)") for part in range(2))
        place = lambda s, i: (i * 4 if i is not None else 0) + s // 2

        def silu(m, s, i):
            nc.scalar.wait_ge(self.pair_free[1].sem, place(s, i) + (f0 - 1))
            return nc.scalar.activation(lit[:, s // 2 % 2, :], ps[:, s % BANKS, 0:n], ACT.Silu)

        def multiply(m, s, i):
            p = place(s, i)
            nc.vector.wait_ge(silu_done.sem, p + (s0 + 1))
            return nc.vector.tensor_tensor(raw[:, :], ps[:, s % BANKS, 0:n], lit[:, s // 2 % 2, :], ALU.mult)

        def keep(m, s, i):
            p = place(s, i)
            to = bass.ds(p * n, n)
            nc.vector.wait_ge(self.pair_free[1].sem, p + (f0 + 1))
            nc.vector.tensor_copy(high[:, to], raw[:, :]).then_inc(high_done.sem, 1)
            nc.vector.wait_ge(high_done.sem, p + (high0 + 1))
            nc.vector.tensor_tensor(low[:, to], raw[:, :], high[:, to].bitcast(F32), ALU.subtract
                                    ).then_inc(low_done.sem, 1)
            nc.vector.wait_ge(low_done.sem, p + (low0 + 1))
        self.project_parts(split, 2 * FT, KT, lambda part, k: h_parts[:, part, k, :], silu, multiply, keep)
        high_done.up(FT), low_done.up(FT)
        inner.close()
        inner = ExitStack()
        y = inner.enter_context(nc.sbuf_tensor(f"y_{name}", [P, KT, n], F32))
        room = inner.enter_context(nc.sbuf_tensor(f"room_{name}", [P, (KT + 1) * n + 2 * KT], F32))
        self.linear_parts(split, KT, FT, lambda part, k: hidden[:, part, k, :], lambda m: y[:, m, :])
        self.arena = Space(room, (KT + 1) * n + 2 * KT)
        self.add_normed(y[:, :, :], [(c, g) for c, _, _, g in parts], gain_out)
        inner.close()
        outer.close()

    def hgrn_heads(self, q, k, logf, value, resets, masks, out):
        nc, ps, A = self.nc, self.ps, self.arena
        v, s = nc.vector, nc.scalar
        NC = TA // HCHUNK
        NT = TA // P
        items = [(h, d) for h in range(HEADS) for d in range(2)]
        b, att, ktok, state = A.take(TA), A.take(TA), A.take(TA), A.take(NC, P)
        factors = [[A.take(TA) for _ in range(4)] + [A.take(NC)] for _ in range(2)]
        ch = lambda x: x.rearrange("p (c t) -> p c t", t=HCHUNK)
        wide = lambda i: ch(b)[:, :, i:i + 1].broadcast_to([P, NC, HCHUNK])
        tile = lambda j: slice(j * P, (j + 1) * P)
        rows = lambda c: slice(c * HCHUNK % P, c * HCHUNK % P + HCHUNK)
        upd = lambda c: ps[:, 2 + c % 4, c // 4 * P:(c // 4 + 1) * P]
        exponents, exps, products, turned = self.a, self.b, self.c, self.d
        att_done, ktok_done, updates, states = self.e, self.f, self.g, self.dve_done
        for n in range(len(items) + 2):
            front = items[n] if n < len(items) else None
            back = items[n - 1] if 0 < n <= len(items) else None
            ready = items[n - 2] if n >= 2 and items[n - 2][1] == 1 else None
            e_mid, e_inv, e_b, e_last, dec = factors[n % 2]
            p_mid, p_inv, p_b, p_last, p_dec = factors[(n - 1) % 2]
            if front:
                fh, fd = front
                mid, last = (HCHUNK // 2 - 1, HCHUNK - 1) if fd == 0 else (HCHUNK // 2, 0)
                way = (lambda x: x) if fd == 0 else (lambda x: x[:, ::-1])
            if back:
                bh, bd = back
                order = list(range(NC)) if bd == 0 else (list(range(NC // 2 - 1, -1, -1))
                                                         + list(range(NC - 1, NC // 2 - 1, -1)))
                sum_bank = ps[:, 6 + bh % 2, :]
                head = slice(bh * P, (bh + 1) * P)
            states0 = states.n + (1 if front else 0)
            with self.block() as block:
                @block.vector
                def _(dve):
                    if front:
                        v.tensor_tensor_scan(way(b), way(resets[fd]), way(logf(fh, fd)), 0.0, ALU.mult, ALU.add
                                             ).then_inc(self.dve_done.sem, 1)
                        dve.wait_ge(self.dve_done.sem, states0)
                        v.tensor_tensor(ch(e_mid), ch(b), wide(mid), ALU.subtract)
                        v.tensor_tensor(ch(e_last), wide(last), ch(b), ALU.subtract).then_inc(exponents.sem, 1)
                    if back:
                        v.memset(att, 0.0).then_inc(att_done.sem, 1)
                        dve.wait_ge(att_done.sem, att_done.n + 1)
                        dve.wait_ge(products.sem, products.n + 1)
                        for j in range(NT):
                            ins = v.copy_predicated(att[:, tile(j)], masks[bd].bitcast(U32), ps[:, 0, tile(j)])
                        ins.then_inc(att_done.sem, 1)
                        dve.wait_ge(updates.sem, updates.n + 1)
                        v.tensor_copy(state[:, order[0], :], upd(order[0])).then_inc(states.sem, 1)
                        for c in range(1, NC - 1):
                            dve.wait_ge(states.sem, states0 + c)
                            v.scalar_tensor_tensor(state[:, order[c], :], state[:, order[c - 1], :],
                                                   p_dec[:, order[c]:order[c] + 1], upd(order[c]), ALU.mult, ALU.add
                                                   ).then_inc(states.sem, 1)
                    if front:
                        dve.wait_ge(exps.sem, exps.n + 1)
                        v.tensor_tensor(e_mid, e_mid, q(fh), ALU.mult)
                        v.tensor_tensor(e_inv, e_inv, k(fh, fd), ALU.mult)
                        v.tensor_tensor(e_last, e_last, k(fh, fd), ALU.mult)
                        v.tensor_tensor(e_b, e_b, q(fh), ALU.mult)

                @block.scalar
                def _(act):
                    if ready:
                        s.activation(out(ready[0]), ps[:, 6 + ready[0] % 2, :], ACT.Copy)
                    if front:
                        act.wait_ge(exponents.sem, exponents.n + 1)
                        s.activation(e_inv, e_mid, ACT.Exp, scale=-1.0)
                        s.activation(e_b, b, ACT.Exp)
                    if back:
                        act.wait_ge(turned.sem, turned.n + 1)
                        s.activation(ktok, ps[:, 1, :], ACT.Copy).then_inc(ktok_done.sem, 1)
                    if front:
                        s.activation(dec, ch(b)[:, :, last], ACT.Exp)
                        s.activation(e_last, e_last, ACT.Exp).then_inc(self.act_done.sem, 1)
                        act.wait_ge(self.act_done.sem, self.act_done.up())
                        s.activation(e_mid, e_mid, ACT.Exp).then_inc(exps.sem, 1)

                if back:
                    @block.tensor
                    def _(pe):
                        for j in range(NT):
                            ins = nc.tensor.transpose(ps[:, 1, tile(j)], p_last[:, tile(j)], self.ident)
                        ins.then_inc(turned.sem, 1)
                        for j in range(NT):
                            ins = nc.tensor.matmul(ps[:, 0, tile(j)], p_inv[:, tile(j)], p_mid[:, tile(j)],
                                                   start=True, stop=True)
                        ins.then_inc(products.sem, 1)
                        pe.wait_ge(ktok_done.sem, ktok_done.n + 1)
                        for c in order[:-1]:
                            j = c * HCHUNK // P
                            ins = nc.tensor.matmul(upd(c), ktok[rows(c), tile(j)], value[rows(c), j, head],
                                                   start=True, stop=True)
                        ins.then_inc(updates.sem, 1)
                        pe.wait_ge(att_done.sem, att_done.n + 2)
                        for j in range(NT):
                            nc.tensor.matmul(sum_bank[:, tile(j)], value[:, j, head], att[:, tile(j)],
                                             start=(bd == 0 and j == 0), stop=False, skip_group_check=True)
                        for c in range(1, NC):
                            pe.wait_ge(states.sem, states0 + c)
                            t = slice(order[c] * HCHUNK, (order[c] + 1) * HCHUNK)
                            nc.tensor.matmul(sum_bank[:, t], state[:, order[c - 1], :], p_b[:, t], start=False,
                                             stop=(bd == 1 and c == NC - 1), skip_group_check=True)
            if front:
                exponents.up(), exps.up(), self.dve_done.up()
            if back:
                products.up(), turned.up(), att_done.up(2), ktok_done.up(), updates.up(), states.up(NC - 1)

    def mlstm(self, c, qk, v_tok, out):
        nc, ps, A = self.nc, self.ps, self.arena
        v, s = nc.vector, nc.scalar
        mark = A.at
        W = 64
        rows = [A.take(TA)[0:W, :] for _ in range(5)]
        ig, lf, F, m, tmp = rows
        unit = A.take(TA)
        with self.block() as block:
            @block.tensor
            def _(pe):
                for g in range(2):
                    for k in range(KT):
                        nc.tensor.matmul(ps[0:W, g, :], c["gates"][:, k, g * W:(g + 1) * W], self.hT[:, k, :],
                                         start=(k == 0), stop=(k == KT - 1))
        gb = c["gate_b"]
        with self.block() as block:
            @block.vector
            def _(dve):
                v.tensor_scalar(ig, ps[0:W, 0, :], gb[0:W, 0:1], None, ALU.add).then_inc(self.dve_done.sem, 1)
                dve.wait_ge(self.dve_done.sem, self.dve_done.up())
                v.tensor_scalar(lf, ps[0:W, 1, :], gb[0:W, 1:2], None, ALU.add).then_inc(self.dve_done.sem, 1)
                dve.wait_ge(self.dve_done.sem, self.dve_done.up())
                v.tensor_scalar(tmp, lf, -1.0, None, ALU.mult).then_inc(self.dve_done.sem, 1)
                dve.wait_ge(self.dve_done.sem, self.dve_done.up())
                v.tensor_tensor(tmp, tmp, lf, ALU.max).then_inc(self.dve_done.sem, 1)
                dve.wait_ge(self.dve_done.sem, self.dve_done.up())
                v.memset(unit, 1.0)
        with self.block() as block:
            @block.scalar
            def _(act):
                s.activation(tmp, tmp, ACT.Exp, scale=-1.0).then_inc(self.act_done.sem, 1)
                act.wait_ge(self.act_done.sem, self.act_done.up())
                s.activation(tmp, tmp, ACT.Ln, bias=1.0)
        fw, bw = slice(0, 32), slice(32, 64)
        back, back_lat = slice(TC - 1, None, -1), slice(TA - 1, TC - 1, -1)
        done = self.dve_done
        with self.block() as block:
            @block.vector
            def _(dve):
                v.scalar_tensor_tensor(lf, lf, 0.0, tmp, ALU.min, ALU.subtract).then_inc(done.sem, 1)
                dve.wait_ge(done.sem, done.up())
                v.tensor_tensor_scan(F[fw], unit[fw], lf[fw], 0.0, ALU.mult, ALU.add)
                v.tensor_tensor_scan(m[fw], lf[fw], ig[fw], 0.0, ALU.add, ALU.max)
                v.tensor_tensor_scan(F[bw, back], unit[bw, back], lf[bw, back], 0.0, ALU.mult, ALU.add)
                v.tensor_tensor_scan(m[bw, back], lf[bw, back], ig[bw, back], 0.0, ALU.add, ALU.max
                                     ).then_inc(done.sem, 1)
                dve.wait_ge(done.sem, done.up())
                v.tensor_tensor_scan(F[bw, back_lat], unit[bw, back_lat], lf[bw, back_lat], F[bw, 0:1],
                                     ALU.mult, ALU.add)
                v.tensor_tensor_scan(m[bw, back_lat], lf[bw, back_lat], ig[bw, back_lat], m[bw, 0:1],
                                     ALU.add, ALU.max).then_inc(done.sem, 1)
                dve.wait_ge(done.sem, done.up())
                v.tensor_tensor(tmp, F, m, ALU.subtract)
                v.tensor_tensor(ig, ig, F, ALU.subtract).then_inc(done.sem, 1)
                dve.wait_ge(done.sem, done.up())
                v.tensor_scalar(m, m, -1.0, None, ALU.mult)
        key = A.take(TA // P, W)
        pick = A.take(8, P)
        with self.block() as block:
            @block.tensor
            def _(pe):
                for j in range(TA // P):
                    nc.tensor.transpose(ps[:, 2, j * W:(j + 1) * W], ig[:, j * P:(j + 1) * P], self.ident[0:W, 0:W])

            @block.vector
            def _(dve):
                for d in range(2):
                    for h in range(HEADS):
                        r = 32 * d + h
                        v.tensor_copy(pick[0:W, d * HEADS + h, :], self.ident[0:W, r:r + 1].broadcast_to([W, P]))
        with self.block() as block:
            @block.vector
            def _(dve):
                v.tensor_copy(flat(key), ps[:, 2, 0:TA // P * W])
        weights = [A.take(TA // P, TA), self.hT[:, 0:TA // P, :]]
        floors = [A.take(TA), self.hT[:, TA // P, :]]
        den, num = A.take(TA), A.take(TA)
        NT, LT = TA // P, TC // P
        items = [(h, d) for h in range(HEADS) for d in range(2)]

        def seen_by(d):
            if d == 0:
                return [(j, j * P, TA) for j in range(NT)]
            return ([(j, 0, (j + 1) * P) for j in range(LT)] + [(j, TC, TA) for j in range(LT)]
                    + [(j, TC, (j + 1) * P) for j in range(LT, NT)])
        rows_done, scores_done, exponents, exps, sums_done = self.a, self.b, self.c, self.d, self.e
        for n in range(len(items) + 1):
            front = items[n] if n < len(items) else None
            back = items[n - 1] if n > 0 else None
            weight, floor = weights[n % 2], floors[n % 2]
            p_weight, p_floor = weights[(n - 1) % 2], floors[(n - 1) % 2]
            if front:
                h, d = front
                seen = seen_by(d)
                half = slice(h % 2 * 64, h % 2 * 64 + 64)
            if back:
                bh, bd = back
                b_seen = seen_by(bd)
            with self.block() as block:
                @block.tensor
                def _(pe):
                    if front:
                        nc.tensor.matmul(ps[:, 0, :], pick[0:W, d * HEADS + h, :], tmp, start=True, stop=True)
                        nc.tensor.matmul(ps[:, 1, :], pick[0:W, d * HEADS + h, :], m, start=True, stop=True
                                         ).then_inc(rows_done.sem, 1)
                        for j, t0, t1 in seen:
                            ins = nc.tensor.matmul(ps[:, 2 + j, t0:t1], qk[half, 2 + h // 2, j * P:(j + 1) * P],
                                                   qk[half, h // 2, t0:t1], start=True, stop=True)
                        ins.then_inc(scores_done.sem, 1)
                    if back:
                        for bank, lhs in ((6, lambda j: v_tok[:, j, bh * P:(bh + 1) * P]), (7, lambda j: self.ones)):
                            for i, (j, t0, t1) in enumerate(b_seen):
                                ins = nc.tensor.matmul(ps[:, bank, t0:t1], lhs(j), p_weight[:, j, t0:t1],
                                                       start=(i == 0), stop=(i == len(b_seen) - 1),
                                                       skip_group_check=True)
                        ins.then_inc(sums_done.sem, 1)

                @block.scalar
                def _(act):
                    if front:
                        act.wait_ge(rows_done.sem, rows_done.n + 1)
                        s.activation(floor, ps[:, 1, :], ACT.Exp)
                        for i, (j, t0, t1) in enumerate(seen):
                            act.wait_ge(exponents.sem, exponents.n + i + 1)
                            s.activation(weight[:, j, t0:t1], weight[:, j, t0:t1], ACT.Exp).then_inc(exps.sem, 1)

                @block.vector
                def _(dve):
                    if front:
                        dve.wait_ge(rows_done.sem, rows_done.n + 1)
                        for j, t0, t1 in seen:
                            v.tensor_scalar(weight[:, j, t0:t1], ps[:, 0, t0:t1], key[:, j, 32 * d + h:32 * d + h + 1],
                                            0.0, ALU.add, ALU.min).then_inc(exponents.sem, 1)
                        dve.wait_ge(exps.sem, exps.n + len(seen))
                        for j in range(NT):
                            diag = weight[:, j, j * P:(j + 1) * P]
                            ins = v.tensor_tensor(diag, diag, c["tri"][d], ALU.mult)
                        ins.then_inc(done.sem, 1)
                        dve.wait_ge(done.sem, done.up())
                        dve.wait_ge(scores_done.sem, scores_done.n + 1)
                        for j, t0, t1 in seen:
                            v.scalar_tensor_tensor(weight[:, j, t0:t1], ps[:, 2 + j, t0:t1], float(64) ** -0.5,
                                                   weight[:, j, t0:t1], ALU.mult, ALU.mult)
                    if back:
                        dve.wait_ge(sums_done.sem, sums_done.n + 1)
                        v.tensor_scalar(den, ps[:, 7, :], -1.0, None, ALU.mult).then_inc(done.sem, 1)
                        dve.wait_ge(done.sem, done.up())
                        v.tensor_tensor(den, den, ps[:, 7, :], ALU.max).then_inc(done.sem, 1)
                        dve.wait_ge(done.sem, done.up())
                        v.tensor_tensor(den, den, p_floor, ALU.max).then_inc(done.sem, 1)
                        dve.wait_ge(done.sem, done.up())
                        v.reciprocal(den, den).then_inc(done.sem, 1)
                        dve.wait_ge(done.sem, done.up())
                        if bd == 0:
                            v.tensor_tensor(out(bh), ps[:, 6, :], den, ALU.mult)
                        else:
                            v.tensor_tensor(num, ps[:, 6, :], den, ALU.mult).then_inc(done.sem, 1)
                            dve.wait_ge(done.sem, done.up())
                            v.tensor_tensor(out(bh), out(bh), num, ALU.add)
            if front:
                rows_done.up(), scores_done.up(), exponents.up(len(seen)), exps.up(len(seen))
            if back:
                sums_done.up()
        A.at = mark

    def recurrent(self, c, gains, mods):
        nc, ps, A = self.nc, self.ps, self.arena
        v, s = nc.vector, nc.scalar
        mark = A.at
        everything = slice(0, TA)
        o = A.take(2 * HEADS, TA)
        vt = A.take(TA // P, 2 * HEADS * P)
        proj = A.take(24, TA)
        with ExitStack() as parts:
            h_parts = parts.enter_context(nc.sbuf_tensor("h_parts_recurrent", [P, 2, KT, TA], F32R))
            split = parts.enter_context(nc.sbuf_tensor("split_recurrent_in", [P, 2, 2, UNIT], F32R))
            self.divide(self.hT[:, :, :], h_parts[:, 0], h_parts[:, 1])
            self.linear_parts(split, 24, KT, lambda part, k: h_parts[:, part, k, :],
                              lambda m: flat(proj)[:, bass.ds(m * TA, TA)])
        self.linear_tokens(2 * HEADS, KT, self.hT, range(TA // P), lambda m: vt[:, :, m * P:(m + 1) * P])
        q, gate_a, z, gate_b = proj[:, 0:4, :], proj[:, 4:8, :], proj[:, 8:16, :], proj[:, 20:24, :]
        qk = proj[:, 16:20, :]
        outer_arena, rest_room = A, ExitStack()
        room = 17 * TA + 32
        A = self.arena = Space(rest_room.enter_context(nc.sbuf_tensor("arena_recurrent", [P, room], F32)), room)
        inner = A.at
        conv = A.take(4, TA)
        w = c["conv"]
        with self.block() as block:
            @block.vector
            def _(dve):
                for tap in (1, 0, 2):
                    for j in range(4):
                        for c0 in (0, TC):
                            a, b = c0 + (tap == 0), c0 + TC - (tap == 2)
                            src = qk[:, j, a + tap - 1:b + tap - 1]
                            if tap == 1:
                                ins = v.tensor_scalar(conv[:, j, a:b], src, w[:, j, 1:2], None, ALU.mult)
                            else:
                                ins = v.scalar_tensor_tensor(conv[:, j, a:b], src, w[:, j, tap:tap + 1],
                                                             conv[:, j, a:b], ALU.mult, ALU.add)
                    ins.then_inc(self.dve_done.sem, 1)
                    dve.wait_ge(self.dve_done.sem, self.dve_done.up())
        with self.block() as block:
            @block.scalar
            def _(act):
                s.activation(qk, conv, ACT.Silu)
                s.activation(gate_a, gate_a, ACT.Silu)
                s.activation(gate_b, gate_b, ACT.Sigmoid)
        A.at = inner
        self.mlstm(c, qk, vt[:, :, HEADS * P:], lambda h: o[:, HEADS + h, :])
        lb, rest = c["lb_c"], c["rest"]
        raw = c["lb"]
        wide = lambda x: x.unsqueeze(2).broadcast_to([P, 8, 3])
        with self.block() as block:
            @block.vector
            def _(dve):
                v.tensor_reduce(lb, raw, AX_X, ALU.max).then_inc(self.dve_done.sem, 1)
                dve.wait_ge(self.dve_done.sem, self.dve_done.up())
                v.tensor_tensor(raw, raw, wide(lb), ALU.subtract)
        with self.block() as block:
            @block.scalar
            def _(act):
                s.activation(raw, raw, ACT.Exp)
        with self.block() as block:
            @block.vector
            def _(dve):
                v.tensor_reduce(rest, raw, AX_X, ALU.add).then_inc(self.dve_done.sem, 1)
                dve.wait_ge(self.dve_done.sem, self.dve_done.up())
                v.reciprocal(rest, rest).then_inc(self.dve_done.sem, 1)
                dve.wait_ge(self.dve_done.sem, self.dve_done.up())
                v.tensor_tensor(lb, raw[:, :, 0], rest, ALU.mult).then_inc(self.dve_done.sem, 1)
                dve.wait_ge(self.dve_done.sem, self.dve_done.up())
                v.tensor_scalar(rest, lb, -1.0, 1.0, ALU.mult, ALU.add)
        logf = self.hT
        with self.block() as block:
            @block.scalar
            def _(act):
                s.activation(logf, z, ACT.Sigmoid)
                s.activation(conv[:, 0, 0:1], self.ones[:, 0:1], ACT.Copy).then_inc(self.act_done.sem, 1)
                act.wait_ge(self.act_done.sem, self.act_done.up())
                s.activation(z, z, ACT.Sigmoid, scale=-1.0)
        with self.block() as block:
            @block.vector
            def _(dve):
                for j in range(8):
                    v.tensor_scalar(logf[:, j, :], logf[:, j, :], rest[:, j:j + 1], lb[:, j:j + 1], ALU.mult, ALU.add)
                    v.tensor_scalar(z[:, j, :], z[:, j, :], rest[:, j:j + 1], None, ALU.mult)
        with self.block() as block:
            @block.scalar
            def _(act):
                s.activation(logf, logf, ACT.Ln)
        resets = [A.take(TA) for _ in range(2)]
        for d, edge in ((0, 0), (1, HCHUNK - 1)):
            with self.block() as block:
                @block.vector
                def _(dve):
                    v.memset(resets[d], 1.0).then_inc(self.dve_done.sem, 1)
                    dve.wait_ge(self.dve_done.sem, self.dve_done.up())
                    v.memset(resets[d].rearrange("p (c t) -> p c t", t=HCHUNK)[:, :, edge], 0.0)
        self.hgrn_heads(lambda h: q[:, h, :], lambda h, d: z[:, d * HEADS + h, :],
                        lambda h, d: logf[:, d * HEADS + h, :], vt, resets, c["chunk_mask"], lambda h: o[:, h, :])
        A.at = inner
        for j, gate in ((0, gate_a), (HEADS, gate_b)):
            root = A.take(HEADS * TA)
            part = o[:, j:j + HEADS, :]
            self.scaled_root(flat(part), HEADS * TA, 1.0 / P, root)
            rt = root.rearrange("p (h t) -> p h t", h=HEADS)
            with self.block() as block:
                @block.vector
                def _(dve):
                    for h in range(HEADS):
                        ins = v.scalar_tensor_tensor(part[:, h, :], part[:, h, :], c["out_g"][:, j + h:j + h + 1],
                                                     rt[:, h, :], ALU.mult, ALU.mult)
                    ins.then_inc(self.dve_done.sem, 1)
                    dve.wait_ge(self.dve_done.sem, self.dve_done.up())
                    v.tensor_tensor(part, part, gate, ALU.mult)
            A.at = inner
        rest_room.close()
        A = self.arena = outer_arena
        with ExitStack() as parts:
            o_parts = parts.enter_context(nc.sbuf_tensor("o_parts_recurrent", [P, 2, KT, TA], F32R))
            split = parts.enter_context(nc.sbuf_tensor("split_recurrent_out", [P, 2, 2, UNIT], F32R))
            self.divide(o, o_parts[:, 0], o_parts[:, 1])
            self.linear_parts(split, KT, KT, lambda part, k: o_parts[:, part, k, :], lambda m: self.hT[:, m, :])
        A.at = mark
        self.add_normed(self.hT, [(slice(0, TC), mods[2][1]), (LAT, mods[2][0])], gains[1])

    def grouped_attention(self, c, gains, mods):
        nc, ps, A = self.nc, self.ps, self.arena
        v = nc.vector
        mark = A.at
        q, k, vt, o = A.take(GQ_H, T), A.take(GQ_KV, TA), A.take(TA // P, GQ_KV * P), A.take(GQ_H, T)
        self.split_h()
        self.linear_parts(self.split, GQ_H, KT, self.latent_part, lambda m: q[:, m, :])
        self.linear(GQ_KV, KT, self.hT, slice(0, TA), lambda m: k[:, m, :])
        self.linear_tokens(GQ_KV, KT, self.hT, range(TA // P), lambda m: vt[:, :, m * P:(m + 1) * P])
        inner = A.at
        for x, n, j in ((q, GQ_H * T, 0), (k, GQ_KV * TA, 1)):
            root = A.take(n)
            self.scaled_root(flat(x), n, 1.0 / P, root)
            with self.block() as block:
                @block.vector
                def _(dve):
                    v.scalar_tensor_tensor(flat(x), flat(x), c["qk_g"][:, j:j + 1], root,
                                           ALU.mult, ALU.mult)
            A.at = inner
        cos, sin = c["axial"][:, 0, :], c["axial"][:, 1, :]
        self.rope(q, c["rot"], cos, sin)
        self.rope(k[:, :, LAT], c["rot"], cos, sin)

        def scores(h, qt, dst):
            return nc.tensor.matmul(dst, q[:, h, qt * P:(qt + 1) * P], k[:, h * GQ_KV // GQ_H, :],
                                    start=True, stop=True)

        def value(h, kt):
            g = h * GQ_KV // GQ_H
            return vt[:, kt, g * P:(g + 1) * P]
        self.attention(GQ_H, TA, float(P) ** -0.5, scores, value, lambda h: o[:, h, :], False)
        y = A.take(KT, T)
        self.linear(KT, KT, o, slice(0, T), lambda m: y[:, m, :])
        self.add_normed(y, [(LAT, mods[2][0])], gains[1])
        A.at = mark


ORDER = ["mod_0", "hy_in", "hy_out", "peer_q_0", "experts_0",
         "mod_1", "mla_in", "mla_uq", "mla_ukv", "mla_out", "peer_q_1", "experts_1",
         "ada_0", "ab_in", "ab_out", "ffn_in_0", "ffn_out_0",
         "ada_1", "gq_in", "gq_out", "ffn_in_1", "ffn_out_1"]


def program(nc, dram, stop=None):
    with ExitStack() as ctx:
        core = Core(nc, ctx, dram, ORDER)
        s = core.small
        core.constants()
        core.small_cols = s.take(KT)
        core.selT = s.take(3, T)
        xL = core.xT[:, :, LAT]
        cond = s.take(KT, 3)
        mod = s.take(6 * KT, 2)
        bias = s.take(6 * KT)
        gains = s.take(KT, 5)
        norm_g = s.take(KT, 8)
        core.load([(xL, dram["xT"]), (cond, dram["cond"]), (gains, dram["gains"]), (bias, dram["mod_b_0"]),
                   (norm_g, dram["norm_g"])])
        with core.block() as block:
            @block.scalar
            def _(act):
                nc.scalar.activation(cond, cond, ACT.Silu)
        core.split_cond(cond)
        m = [mod[:, i * KT:(i + 1) * KT, 0] for i in range(6)]

        core.modulation("mod_0", mod[:, :, 0:1], 0, 1, bias)
        core.open_work("layer0", 24512, 4)
        s = core.extra
        core.causal_mask()
        c = {"gates": s.take(KT, 8), "conv": s.take(12, 4), "a_log": s.take(HEADS), "dt_bias": s.take(HEADS),
             "decay": s.take(HEADS), "o_norm": s.take(1), "rot": s.take(P), "cos": s.take(T), "sin": s.take(T)}
        pos_i, pos = s.take(T, dt=I32), s.take(T)
        freq = s.take(2)
        core.load([(c["gates"], dram["hy_gates"]), (c["conv"], dram["conv"]), (c["a_log"], dram["a_log"]),
                   (c["dt_bias"], dram["dt_bias"]), (c["o_norm"], dram["o_norm"]), (pos_i, dram["positions"]),
                   (freq, dram["freq"])])
        with core.block() as block:
            @block.vector
            def _(dve):
                nc.vector.tensor_copy(pos, pos_i)
        core.rotation(c["rot"], 64)
        core.rope_tables(pos, freq[:, 0:1], c["cos"], c["sin"])
        core.modulated(LAT, gains[:, :, 0], m[1], m[0])
        c["g1"] = m[2]
        core.hybrid(c)
        if stop == 1:
            return finish(core, dram)
        core.modulated(LAT, gains[:, :, 2], m[4], m[3])
        core.split_h()
        core.peer_routes(dram["subkeys_0"])
        core.close_work()
        core.peer_experts("layer0", m[5])
        if stop == 2:
            return finish(core, dram)

        core.load([(bias, dram["mod_b_1"])])
        core.modulation("mod_1", mod[:, :, 0:1], 0, 1, bias)
        core.open_work("layer1", 16384, 4)
        s = core.extra
        core.causal_mask()
        c = {"norms": s.take(6), "rot": s.take(P), "cos": s.take(T), "sin": s.take(T)}
        pos_i, pos = s.take(T, dt=I32), s.take(T)
        freq = s.take(2)
        core.load([(c["norms"], dram["mla_norms"]), (pos_i, dram["positions"]), (freq, dram["freq"])])
        with core.block() as block:
            @block.vector
            def _(dve):
                nc.vector.tensor_copy(pos, pos_i)
        core.rotation(c["rot"], 32)
        core.rope_tables(pos, freq[:, 1:2], c["cos"], c["sin"])
        core.modulated(LAT, gains[:, :, 1], m[1], m[0])
        c["g1"] = m[2]
        core.latent_attention(c)
        if stop == 3:
            return finish(core, dram)
        core.modulated(LAT, gains[:, :, 3], m[4], m[3])
        core.split_h()
        core.peer_routes(dram["subkeys_1"])
        core.close_work()
        core.peer_experts("layer1", m[5])
        if stop == 4:
            return finish(core, dram)
        core.load([(bias, dram["ada_b_0"])])
        core.modulation("ada_0", mod, 1, 2, bias)
        core.open_work("block2_layer0", 20480, 0)
        s = core.extra
        root = core.arena.take(T)
        core.norm_rows(xL, slice(0, T), core.hT[:, :, LAT], root)
        with core.block() as block:
            @block.vector
            def _(dve):
                for k in range(KT):
                    nc.vector.scalar_tensor_tensor(xL[:, k, :], xL[:, k, :], gains[:, k, 4:5], root,
                                                   ALU.mult, ALU.mult)
        core.arena.at = 0
        if stop == 5:
            return finish(core, dram)

        c = {"gates": s.take(KT, P), "gate_b": s.take(2), "conv": s.take(4, 3), "lb": s.take(8, 3), "lb_c": s.take(8),
             "rest": s.take(8), "out_g": s.take(8)}
        core.load([(core.xT[:, :, 0:TC], dram["ctxT"]), (c["gates"], dram["ab_gates"]),
                   (c["gate_b"][0:64, :], dram["gate_b"]), (c["conv"], dram["ab_conv"]), (c["lb"], dram["lb"]),
                   (c["out_g"], dram["ab_out_g"])])
        mods = [[mod[:, i * KT:(i + 1) * KT, j] for j in range(2)] for i in range(6)]
        CTX = slice(0, TC)
        gain = [norm_g[:, :, i] for i in range(4)]
        for cols, j in ((CTX, 1), (LAT, 0)):
            core.modulated(cols, gain[0], mods[1][j], mods[0][j])
        c["tri"] = [core.selT[:, 0, 0:P], core.selT[:, 0, P:]]
        c["chunk_mask"] = [core.selT[:, 1, 0:P], core.selT[:, 1, P:]]
        orders = [(0, -1, [[1, P]]), (0, 1, [[-1, P]])]
        n = P // HCHUNK
        for d in range(2):
            core.mask(c["tri"][d], [orders[d]])
            core.mask(c["chunk_mask"][d], [(0, 1, [[-HCHUNK, n], [0, HCHUNK]]),
                                           (HCHUNK - 1, -1, [[HCHUNK, n], [0, HCHUNK]]), orders[d]])
        core.recurrent(c, gain, mods)
        if stop == 6:
            return finish(core, dram)
        core.close_work()
        core.swiglu("ffn_0", [(CTX, mods[3][1], mods[4][1], mods[5][1]), (LAT, mods[3][0], mods[4][0], mods[5][0])],
                    gain[2], gain[3])
        if stop == 7:
            return finish(core, dram)

        core.load([(bias, dram["ada_b_1"])])
        core.modulation("ada_1", mod, 1, 2, bias)
        core.open_work("block2_layer1", 16384, 4)
        s = core.extra
        c = {"qk_g": s.take(2), "rot": s.take(P), "axial": s.take(2, T)}
        core.load([(c["qk_g"], dram["qk_g"]), (c["axial"], dram["axial"])])
        core.rotation(c["rot"], 32)
        gain = [norm_g[:, :, 4 + i] for i in range(4)]
        for cols, j in ((CTX, 1), (LAT, 0)):
            core.modulated(cols, gain[0], mods[1][j], mods[0][j])
        core.grouped_attention(c, gain, mods)
        core.close_work()
        core.swiglu("ffn_1", [(LAT, mods[3][0], mods[4][0], mods[5][0])], gain[2], gain[3])
        finish(core, dram)


def finish(core, dram):
    nc = core.nc
    with core.block() as block:
        @block.sync
        def _(sp):
            sp.dma_start(dram["out"], core.xT[:, :, LAT]).then_inc(core.stored.sem, 16)
            sp.wait_ge(core.stored.sem, 16)
    core.close_work()


def tiles(w):
    k, n = w.shape
    w = w.reshape(k // P, P, n // P, P).transpose(2, 0, 1, 3)
    w = w.reshape(-1, TPU, P, P).transpose(0, 2, 1, 3)
    return np.ascontiguousarray(w).reshape(-1, P, UNIT)


def row_tiles(w):
    k, n = w.shape
    return np.ascontiguousarray(w.reshape(k // P, P, n // UNIT, UNIT).transpose(2, 0, 1, 3)).reshape(-1, P, UNIT)


def columns(v):
    v = v.reshape(v.shape[:-1] + (-1, P))
    return np.ascontiguousarray(np.moveaxis(np.moveaxis(v, -1, 0), -1, 1))


def rows(v):
    return np.ascontiguousarray(np.broadcast_to(v, (P,) + v.shape))


def experts(u, v):
    u = u.reshape(KEYS, KEYS, KT, P).transpose(1, 3, 2, 0).reshape(KEYS, P, UNIT)
    v = v.reshape(KEYS, KEYS, UNIT).transpose(1, 0, 2)
    out = np.empty((2 * KEYS, P, UNIT), u.dtype)
    out[0] = u[0]
    out[1:-1:2] = u[1:]
    out[2:-1:2] = v[:-1]
    out[-1] = v[-1]
    return out


def layout(i):
    c = np.concatenate
    a = {}
    a["xT"] = np.ascontiguousarray(i["x"][0].T.reshape(KT, P, T).transpose(1, 0, 2))
    a["cond"] = np.stack([columns(i["c"][0]), columns(i["c_2"][0]), columns(i["c_ctx_2"])], -1)
    a["gains"] = np.stack([columns(v) for v in (i["norm_mix"][0], i["norm_mix"][1], i["norm_ffn"][0],
                                                i["norm_ffn"][1], i["final_norm"])], -1)
    for l in range(2):
        a[f"mod_{l}"], a[f"mod_b_{l}"] = row_tiles(i["mod_w"][l]), columns(i["mod_b"][l])
        a[f"ada_{l}"], a[f"ada_b_{l}"] = row_tiles(i["ada_w_2"][l]), columns(i["ada_b_2"][l])
        a[f"peer_q_{l}"] = tiles(i["peer_w_q"][l])
        a[f"subkeys_{l}"] = np.ascontiguousarray(i["peer_sub_keys"][l].reshape(2 * PH, KEYS, P).transpose(2, 0, 1))
        a[f"experts_{l}"] = experts(i["peer_u"][l], i["peer_v"][l])
        f = i["ffn_w_in_2"][l].reshape(D, 2, FT, P).transpose(0, 2, 1, 3).reshape(D, 2 * FF)
        a[f"ffn_in_{l}"], a[f"ffn_out_{l}"] = tiles(f), tiles(i["ffn_w_out_2"][l])
    w = i["hy_w_in"][0]
    a["hy_in"] = tiles(c([w[:, 0:2048], w[:, 2056:3592]], 1))
    a["hy_gates"] = np.ascontiguousarray(w[:, 2048:2056].reshape(KT, P, 8).transpose(1, 0, 2))
    a["hy_out"] = tiles(i["hy_w_out"][0])
    a["conv"] = np.ascontiguousarray(i["gdn_conv"][0].reshape(4, 12, P).transpose(2, 1, 0))
    a["a_log"], a["dt_bias"] = rows(i["gdn_a_log"][0]), rows(i["gdn_dt_bias"][0])
    a["o_norm"] = np.ascontiguousarray(i["gdn_o_norm"][0].reshape(P, 1))
    a["positions"] = rows(i["positions"][0])
    f = [10000.0 ** (-(np.arange(P) % h) * 2 / (2 * h)) for h in (64, 32)]
    a["freq"] = np.stack(f, -1).astype(np.float32)
    w = i["mla_w_in"][0]
    a["mla_in"] = tiles(c([w, w[:, 768:832]], 1))
    w = i["mla_w_uq"][0].reshape(512, MLA_H, 192)
    a["mla_uq"] = tiles(c([w[:, :, 0:128].reshape(512, -1), w[:, :, 128:].reshape(512, -1)], 1))
    w = i["mla_w_ukv"][0].reshape(256, MLA_H, 256)
    a["mla_ukv"] = tiles(c([w[:, :, 0:128].reshape(256, -1), w[:, :, 128:].reshape(256, -1)], 1))
    a["mla_out"] = tiles(i["mla_w_out"][0])
    a["mla_norms"] = c([columns(i["mla_q_norm"][0]), columns(i["mla_kv_norm"][0])], 1)
    a["ctxT"] = np.ascontiguousarray(i["ctx_2"][0].T.reshape(KT, P, TC).transpose(1, 0, 2))
    a["norm_g"] = columns(i["norm_g_2"]).reshape(P, KT, 8)
    w = i["ab_w_in_2"][0]
    at = np.cumsum([0, 512, 512, 512, 512, 512, 512, 512, 512])
    cut = lambda n: w[:, at[n]:at[n + 1]]
    a["ab_in"] = tiles(c([cut(0), cut(2), cut(3), cut(4), cut(5), cut(7), cut(1), cut(6)], 1))
    g = w[:, 4096:4112].reshape(KT, P, 2, 2, 4).transpose(1, 0, 3, 2, 4)
    a["ab_gates"] = np.zeros((P, KT, 2, 2, 32), np.float32)
    a["ab_gates"][..., 0:4] = g
    a["ab_gates"] = a["ab_gates"].reshape(P, KT, P)
    a["gate_b"] = np.zeros((2, 32, 2), np.float32)
    a["gate_b"][:, 0:4, :] = i["ab_gate_b_2"][0].reshape(2, 2, 4).transpose(0, 2, 1)
    a["gate_b"] = a["gate_b"].reshape(64, 2)
    a["ab_conv"] = np.ascontiguousarray(i["ab_conv_2"][0].reshape(3, 4, P).transpose(2, 1, 0))
    a["lb"] = np.ascontiguousarray(i["hgrn_lb_2"].reshape(2, 3, 4, P).transpose(3, 0, 2, 1)).reshape(P, 8, 3)
    a["ab_out_g"] = columns(i["ab_out_g_2"][0])
    a["ab_out"] = tiles(i["ab_w_out_2"][0])
    a["gq_in"] = tiles(i["attn_w_qkv_2"][0])
    a["qk_g"] = np.ascontiguousarray(i["attn_qk_g_2"][0].T)
    a["gq_out"] = tiles(i["attn_w_out_2"][0])
    inv = np.power(np.float32(10000.0), -np.arange(0, 64, 2, dtype=np.float32) / 64)
    t = np.arange(T)
    ang = np.stack([(t // 64).astype(np.float32)[:, None] * inv, (t % 64).astype(np.float32)[:, None] * inv], 1)
    ang = np.stack([ang, ang], 2).reshape(T, P).T
    a["axial"] = np.ascontiguousarray(np.stack([np.cos(ang), np.sin(ang)], 1).astype(np.float32))
    return a


def kernel(**inputs):
    import concourse.bacc as bacc
    from concourse.bass_utils import run_bass_kernel_spmd

    nc = bacc.Bacc("TRN2", target_bir_lowering=False, num_devices=1)
    arrays = layout({k: np.asarray(v) for k, v in inputs.items()})
    dram = {n: nc.dram_tensor(f"in_{n}", a.shape, mybir.dt.from_np(a.dtype), kind="ExternalInput").ap()
            for n, a in arrays.items()}
    dram["out"] = nc.dram_tensor("out", (P, KT, T), F32, kind="ExternalOutput").ap()
    program(nc, dram)
    r = run_bass_kernel_spmd(nc, [{f"in_{n}": a for n, a in arrays.items()}], core_ids=[0])
    out = r.results[0]["out"]
    return np.ascontiguousarray(out.transpose(2, 1, 0)).reshape(1, T, D)
```
